# Optimizing a Trainium2 kernel written in Bass

```python
import jax, jax.numpy as jnp
from jax import lax
import numpy as np

D_MODEL = 1024
BATCH = 1
SEQ = 128
DEPTH = 2
DEC_BATCH = 1
DEC_SEQ = 512
PAST_LEN = 128

GRID_W = 64
A_HEAD = 64
A_WIDTH = D_MODEL
A_HEADS = A_WIDTH // A_HEAD
A_DECAY_RANK = 64
A_ICLR_RANK = 64
A_GATE_RANK = 128
A_COLS = 3 * A_WIDTH + 2 * A_DECAY_RANK + 2 * A_ICLR_RANK + A_GATE_RANK
POOL_WINDOWS = (2, 4, 8, 16)
B_GROUPS = len(POOL_WINDOWS)
B_WIDTH = D_MODEL // 2
B_GROUP = B_WIDTH // B_GROUPS
C_WIDTH = D_MODEL // 2
C_CONV = 31
IN_COLS = A_COLS + B_WIDTH + 2 * C_WIDTH + 3 * D_MODEL
P_HEADS = 8
P_KEYS = 128
P_EXPERTS = P_KEYS * P_KEYS
P_QDIM = 256
P_HALF = P_QDIM // 2
P_TOPK = 16
P_CHUNK = 128
EPS = 1e-6
GN_EPS = 64e-5
LN_EPS = 1e-5

kernel_name = 'hybrid_rwkv7_pool_conformer_peer_dit'

def rmsnorm(x, g):
    xf = x.astype(jnp.float32)
    y = xf * lax.rsqrt(jnp.mean(xf * xf, axis=-1, keepdims=True) + EPS)
    return (y * g.astype(jnp.float32)).astype(x.dtype)

def layernorm(x, g, b, eps):
    xf = x.astype(jnp.float32)
    mu = jnp.mean(xf, axis=-1, keepdims=True)
    var = jnp.mean(jnp.square(xf - mu), axis=-1, keepdims=True)
    y = (xf - mu) * lax.rsqrt(var + eps) * g.astype(jnp.float32) + b.astype(jnp.float32)
    return y.astype(x.dtype)

def centred_shift(x):
    prev = jnp.pad(x[:, :-1], ((0, 0), (1, 0), (0, 0)))
    nxt = jnp.pad(x[:, 1:], ((0, 0), (0, 1), (0, 0)))
    return 0.5 * (prev + nxt) - x

def rwkv_mix(pa, s0, mu, w0, w2, a0, a2, g2, k_k, k_a, r_k, gn_g, gn_b):
    Bn, T, _ = pa.shape
    dt = pa.dtype
    xa = pa + centred_shift(pa) * mu
    i1 = A_WIDTH
    i2 = 2 * A_WIDTH
    i3 = 3 * A_WIDTH
    i4 = i3 + 2 * A_DECAY_RANK
    i5 = i4 + 2 * A_ICLR_RANK
    r, k, v, w_lo, a_lo, g_lo = jnp.split(xa, [i1, i2, i3, i4, i5], axis=-1)
    w_lo = w_lo.reshape(Bn, T, 2, A_DECAY_RANK)
    a_lo = a_lo.reshape(Bn, T, 2, A_ICLR_RANK)
    w = -jax.nn.softplus(-(w0 + jnp.einsum('btdr,drc->btdc', jnp.tanh(w_lo), w2))) - 0.5
    decay = jnp.exp(-jnp.exp(w.astype(jnp.float32))).astype(dt)
    a = jax.nn.sigmoid(a0 + jnp.einsum('btdr,drc->btdc', a_lo, a2))
    g = jax.nn.sigmoid(g_lo) @ g2
    hs = (A_HEADS, A_HEAD)
    kk = (k * k_k).reshape(Bn, T, *hs).astype(jnp.float32)
    kk = (kk / jnp.maximum(jnp.linalg.norm(kk, axis=-1, keepdims=True), 1e-12)).astype(dt)
    k_dir = (k[:, :, None, :] * (1 + (a - 1) * k_a)).reshape(Bn, T, 2, *hs)
    a_h = a.reshape(Bn, T, 2, *hs)
    decay_h = decay.reshape(Bn, T, 2, *hs)
    r_h = r.reshape(Bn, T, *hs)
    v_h = v.reshape(Bn, T, *hs)

    def both(z):
        return jnp.stack([z, jnp.flip(z, axis=1)], axis=2)

    def orient(z):
        return jnp.stack([z[:, :, 0], jnp.flip(z[:, :, 1], axis=1)], axis=2)

    tm = lambda z: jnp.moveaxis(z, 1, 0)
    seqs = (tm(both(r_h)), tm(orient(decay_h)), tm(orient(k_dir)), tm(both(v_h)), tm(both(kk)), tm(orient(a_h)))

    def step(S, inp):
        r_t, w_t, k_t, v_t, kk_t, a_t = inp
        sa = jnp.einsum('bdhvk,bdhk->bdhv', S, -kk_t)
        S = S * w_t[..., None, :] + sa[..., :, None] * (kk_t * a_t)[..., None, :] + v_t[..., :, None] * k_t[..., None, :]
        y = jnp.einsum('bdhvk,bdhk->bdhv', S, r_t)
        return S, y

    s_fin, ys = lax.scan(step, s0.astype(dt), seqs)
    ys = jnp.moveaxis(ys, 0, 1)
    y = ys[:, :, 0] + jnp.flip(ys[:, :, 1], axis=1)
    y = layernorm(y, gn_g.reshape(hs), gn_b.reshape(hs), GN_EPS)
    bonus = jnp.einsum('bthk,btdhk,hk->bth', r_h, k_dir, r_k)[..., None] * v_h
    return (y + bonus).reshape(Bn, T, A_WIDTH) * g, s_fin

def centred_mean(x, axis, window):
    L = x.shape[axis]
    cs = jnp.cumsum(x.astype(jnp.float32), axis=axis)
    cs = jnp.concatenate([jnp.zeros_like(lax.slice_in_dim(cs, 0, 1, axis=axis)), cs], axis=axis)
    idx = jnp.arange(L)
    lo = jnp.clip(idx - window // 2, 0, L)
    hi = jnp.clip(idx - window // 2 + window, 0, L)
    s = jnp.take(cs, hi, axis=axis) - jnp.take(cs, lo, axis=axis)
    shape = [1] * x.ndim
    shape[axis] = L
    cnt = (hi - lo).astype(jnp.float32).reshape(shape)
    return (s / cnt).astype(x.dtype)

def pool_mix(pb, grid, pool_w, pool_b, pool_scale):
    Bn, T, C = pb.shape
    z = pb.reshape(Bn, T // GRID_W, GRID_W, C) if grid else pb
    groups = jnp.split(z, B_GROUPS, axis=-1)
    d = jnp.stack([centred_mean(zg, 1, w) - zg for zg, w in zip(groups, POOL_WINDOWS)], axis=-2)
    y = jnp.einsum('...gc,gcd->...gd', d, pool_w) + pool_b
    return (y * pool_scale.reshape(B_GROUPS, B_GROUP)).reshape(Bn, T, C)

def conv_mix(pc, grid, conv_w, conv_b, ln_g, ln_b):
    u_a, u_g = jnp.split(pc, 2, axis=-1)
    u = u_a * jax.nn.sigmoid(u_g)
    Bn, T, C = u.shape
    if grid:
        u = u.reshape(Bn * (T // GRID_W), GRID_W, C)
    u = lax.conv_general_dilated(u, conv_w[:, None, :], window_strides=(1,), padding='SAME',
                                 dimension_numbers=('NWC', 'WIO', 'NWC'), feature_group_count=C)
    u = (u + conv_b).reshape(Bn, T, C)
    return jax.nn.silu(layernorm(u, ln_g, ln_b, LN_EPS))

def peer(h, w_q, sub_keys, u_tab, v_tab):
    Bn, T, D = h.shape

    def block(xc):
        q = (xc @ w_q).reshape(-1, P_HEADS, 2, P_HALF)
        s = jnp.einsum('chpq,hpnq->chpn', q, sub_keys)
        s_top, i_top = lax.top_k(s, P_TOPK)
        cand = s_top[:, :, 0, :, None] + s_top[:, :, 1, None, :]
        cand = cand.reshape(cand.shape[0], P_HEADS, P_TOPK * P_TOPK)
        best, j = lax.top_k(cand, P_TOPK)
        e = (jnp.take_along_axis(i_top[:, :, 0], j // P_TOPK, axis=-1) * P_KEYS
             + jnp.take_along_axis(i_top[:, :, 1], j % P_TOPK, axis=-1))
        gate = jax.nn.softmax(best.astype(jnp.float32), axis=-1).astype(xc.dtype)
        u = jnp.take(u_tab, e, axis=0)
        hid = jax.nn.gelu(jnp.einsum('cd,chkd->chk', xc, u), approximate=False)
        vsel = jnp.take(v_tab, e, axis=0)
        return jnp.einsum('chk,chkd->cd', gate * hid, vsel)

    out = lax.map(block, h.reshape(-1, P_CHUNK, D))
    return out.reshape(Bn, T, D)

def setup_inputs(seed: int = 0) -> dict:
    key = jax.random.key(seed)
    ks = iter(jax.random.split(key, 48))
    f32 = jnp.float32
    nrm = lambda shape, s: jax.random.normal(next(ks), shape, f32) * s
    gain = lambda shape: 1.0 + nrm(shape, 0.02)
    L = DEPTH
    return {
        'x_prompt': nrm((BATCH, SEQ, D_MODEL), 1.0),
        'x_sample': nrm((DEC_BATCH, DEC_SEQ, D_MODEL), 1.0),
        'state_rwkv': nrm((DEC_BATCH, DEPTH, 2, A_HEADS, A_HEAD, A_HEAD), 0.5),
        'c': nrm((DEC_BATCH, D_MODEL), 1.0),
        'c_ctx': nrm((D_MODEL,), 1.0),
        'ada_w': nrm((L, D_MODEL, 6 * D_MODEL), 0.5 * D_MODEL ** -0.5),
        'ada_b': nrm((L, 6 * D_MODEL), 0.02),
        'norm1_g': gain((L, D_MODEL)),
        'norm2_g': gain((L, D_MODEL)),
        'w_in': nrm((L, D_MODEL, IN_COLS), D_MODEL ** -0.5),
        'shift_mu': jax.random.uniform(next(ks), (L, A_COLS), f32),
        'decay_w0': jax.random.uniform(next(ks), (L, 2, A_WIDTH), f32, minval=-4.0, maxval=0.0),
        'decay_w2': nrm((L, 2, A_DECAY_RANK, A_WIDTH), 0.5 * A_DECAY_RANK ** -0.5),
        'iclr_a0': nrm((L, 2, A_WIDTH), 0.5),
        'iclr_a2': nrm((L, 2, A_ICLR_RANK, A_WIDTH), 0.5 * A_ICLR_RANK ** -0.5),
        'gate_g2': nrm((L, A_GATE_RANK, A_WIDTH), A_GATE_RANK ** -0.5),
        'k_k': 0.85 + nrm((L, A_WIDTH), 0.05),
        'k_a': 1.0 + nrm((L, A_WIDTH), 0.05),
        'r_k': nrm((L, A_HEADS, A_HEAD), 0.1),
        'gn_g': gain((L, A_WIDTH)),
        'gn_b': nrm((L, A_WIDTH), 0.02),
        'w_a_out': nrm((L, A_WIDTH, D_MODEL), A_WIDTH ** -0.5),
        'pool_w': nrm((L, B_GROUPS, B_GROUP, B_GROUP), B_GROUP ** -0.5),
        'pool_b': nrm((L, B_GROUPS, B_GROUP), 0.02),
        'pool_scale': 1.0 + nrm((L, B_WIDTH), 0.1),
        'w_b_out': nrm((L, B_WIDTH, D_MODEL), B_WIDTH ** -0.5),
        'conv_w': nrm((L, C_CONV, C_WIDTH), C_CONV ** -0.5),
        'conv_b': nrm((L, C_WIDTH), 0.02),
        'cln_g': gain((L, C_WIDTH)),
        'cln_b': nrm((L, C_WIDTH), 0.02),
        'w_c_out': nrm((L, C_WIDTH, D_MODEL), C_WIDTH ** -0.5),
        'w_out': nrm((L, D_MODEL, D_MODEL), D_MODEL ** -0.5),
        'peer_wq': nrm((L, D_MODEL, P_HEADS * P_QDIM), D_MODEL ** -0.5),
        'peer_keys': nrm((L, P_HEADS, 2, P_KEYS, P_HALF), P_HALF ** -0.5),
        'peer_u': nrm((L, P_EXPERTS, D_MODEL), D_MODEL ** -0.5),
        'peer_v': nrm((L, P_EXPERTS, D_MODEL), P_HEADS ** -0.5),
        'final_g': gain((D_MODEL,)),
    }

def reference(x_prompt, x_sample, state_rwkv, c, c_ctx, ada_w, ada_b, norm1_g, norm2_g, w_in, shift_mu,
              decay_w0, decay_w2, iclr_a0, iclr_a2, gate_g2, k_k, k_a, r_k, gn_g, gn_b, w_a_out,
              pool_w, pool_b, pool_scale, w_b_out, conv_w, conv_b, cln_g, cln_b, w_c_out, w_out,
              peer_wq, peer_keys, peer_u, peer_v, final_g):
    def layer(x, cond, grid, s0, l):
        mod = jax.nn.silu(cond) @ ada_w[l] + ada_b[l]
        sh1, sc1, gt1, sh2, sc2, gt2 = jnp.split(mod[:, None, :], 6, axis=-1)
        h = rmsnorm(x, norm1_g[l]) * (1 + sc1) + sh1
        proj = h @ w_in[l]
        pa, pb, pc, pg = jnp.split(proj, [A_COLS, A_COLS + B_WIDTH, A_COLS + B_WIDTH + 2 * C_WIDTH], axis=-1)
        ya, s_fin = rwkv_mix(pa, s0, shift_mu[l], decay_w0[l], decay_w2[l], iclr_a0[l], iclr_a2[l], gate_g2[l],
                             k_k[l], k_a[l], r_k[l], gn_g[l], gn_b[l])
        yb = pool_mix(pb, grid, pool_w[l], pool_b[l], pool_scale[l])
        yc = conv_mix(pc, grid, conv_w[l], conv_b[l], cln_g[l], cln_b[l])
        ga, gb, gc = jnp.split(jax.nn.sigmoid(pg), 3, axis=-1)
        merged = ga * (ya @ w_a_out[l]) + gb * (yb @ w_b_out[l]) + gc * (yc @ w_c_out[l])
        x = x + gt1 * (merged @ w_out[l])
        h2 = rmsnorm(x, norm2_g[l]) * (1 + sc2) + sh2
        x = x + gt2 * peer(h2, peer_wq[l], peer_keys[l], peer_u[l], peer_v[l])
        return x, s_fin

    xp = x_prompt
    s_zero = jnp.zeros((x_prompt.shape[0], 2, A_HEADS, A_HEAD, A_HEAD), x_prompt.dtype)
    ctx_states = []
    for l in range(DEPTH):
        xp, s_ctx = layer(xp, c_ctx[None, :], False, s_zero, l)
        ctx_states.append(s_ctx)
    new_state_rwkv = jnp.stack(ctx_states, axis=1)

    xs = x_sample
    for l in range(DEPTH):
        xs, _ = layer(xs, c, True, state_rwkv[:, l], l)

    return (rmsnorm(xp, final_g), rmsnorm(xs, final_g), new_state_rwkv)


_drawn_inputs = setup_inputs


def setup_inputs(seed=0):
    import zlib

    import numpy as np

    out = dict(_drawn_inputs(seed))
    spreads = {}
    factors = {'state_rwkv': 5.591,
     'norm2_g': 4.713,
     'gn_g': 8.0,
     'gn_b': 8.0,
     'pool_b': 8.0,
     'conv_b': 8.0,
     'cln_g': 8.0,
     'cln_b': 8.0,
     'final_g': 2.684}
    for name, (base, spread) in spreads.items():
        noise = np.random.default_rng([zlib.crc32(name.encode()), seed]).standard_normal(out[name].shape)
        drawn = base * np.exp(spread * noise) if base else spread * noise
        out[name] = __import__('jax').numpy.asarray(drawn.astype(out[name].dtype))
    for name, factor in factors.items():
        out[name] = (out[name] * factor).astype(out[name].dtype)
    return out
```

```python
from contextlib import ExitStack

import concourse.bass as bass
from concourse import mybir

F32 = mybir.dt.float32
U32 = mybir.dt.uint32
ALU = mybir.AluOpType
ACT = mybir.ActivationFunctionType
AX = mybir.AxisListType

P = 128
D = 1024
KB = D // P
LAT, CTX = 512, 128
T = LAT + CTX
TILES = T // P
LAYERS = 2
HD = 64
CH = 64
NCH, NLAT, NCTX = T // CH, LAT // CH, CTX // CH
GRID_W = 64
ROWS = LAT // GRID_W
TAPS = 31
HEADS_Q, KEYS, TOPK, EXPERTS = 8, 128, 16, 16384
SLOTS = HEADS_Q * TOPK
EPS, GN_EPS, LN_EPS = 1e-6, 64e-5, 1e-5
DECAY = 0.6065306597126334
B_R, B_K, B_V, B_LO, B_POOL, B_CONV, B_GATE = 0, 8, 16, 24, 27, 31, 39
R_ADA, R_MU, R_W0, R_A0, R_KK, R_KA = 0, 48, 75, 91, 107, 115
R_N1, R_N2, R_RK, R_GNG, R_GNB, R_PB, R_PS, R_CB, R_LG, R_LB, R_C, R_CC, R_FG = 0, 8, 16, 24, 32, 40, 44, 48, 52, 56, 60, 68, 76
SH1, SC1, GT1, SH2, SC2, GT2 = range(6)
SEGMENTS = ((0, LAT), (LAT, CTX))
WRING = 5
RING = 8
GROUPS = ((0, 4), (4, 4), (8, 2))


class Chain:

    def __init__(self, eng, sem):
        self.eng, self.sem, self.n = eng, sem, 0

    def __call__(self, ins):
        self.n += 1
        ins.then_inc(self.sem, 1)
        self.eng.wait_ge(self.sem, self.n)


class Stage:

    def __init__(self, nc, name):
        self.nc, self.name, self.ctx, self.nums = nc, name, ExitStack(), []

    def sem(self, name):
        s = self.ctx.enter_context(self.nc.semaphore(f"{self.name}_{name}"))
        self.nums.append(s.num)
        return s

    def close(self):
        self.nc.all_engine_barrier()
        nums = sorted(self.nums)
        runs = [n for n in nums if n - 1 not in nums]
        for n in runs:
            end = n
            while end in nums:
                end += 1
            self.nc.gpsimd.sem_clear(range(n, end))
        self.nc.all_engine_barrier()
        self.ctx.close()


class Model:

    def __init__(self, nc, ctx, dram):
        self.nc, self.dram = nc, dram

        def sb(name, shape, dt=F32):
            return ctx.enter_context(nc.sbuf_tensor(name, shape, dt))

        self.x = sb("x", [P, KB, T])
        self.h = sb("h", [P, KB, T])
        self.ya = sb("ya", [P, KB, T])
        self.lo = sb("lo", [P, 3, T])
        self.w = sb("w", [P, WRING, KB, P])
        self.par = sb("par", [P, 3, P])
        self.mod = sb("mod", [P, 6, KB, 2])
        self.scale = sb("scale", [P, 2, KB, 2])
        self.silu_c = sb("silu_c", [P, KB, 2])
        self.ident = sb("ident", [P, P])
        self.ones = sb("ones", [P, P])
        self.block = sb("block", [P, 7, P])
        self.level = sb("level", [P, 6, P])
        self.tri = sb("tri", [P, 2, P])
        self.trid = sb("trid", [P, 2, CH])
        self.reset = sb("reset", [P, NCH, CH])
        self.eps = sb("eps", [P, 4])
        self.row0 = sb("row0", [P, 1])
        self.gate2 = sb("gate2", [P, TILES, KB])
        self.arena = sb("arena", [P, 27264])
        self.used = 0
        self.u_in = [ctx.enter_context(nc.semaphore(f"u_landed{i}")) for i in range(RING)]
        self.v_in = [ctx.enter_context(nc.semaphore(f"v_landed{i}")) for i in range(RING)]
        self.ps = [ctx.enter_context(nc.psum_tensor(f"ps{i}", [P, 1024], F32)) for i in range(4)]
        self.w_in = dram["w_in"].rearrange("l (k p) (b c) -> l b p k c", p=P, c=P)

    def bank(self, n):
        return self.ps[n // 2][:, 512 * (n % 2):512 * (n % 2) + 512]

    def take(self, *shape):
        n = 1
        for s in shape:
            n *= s
        a = self.arena[:, self.used:self.used + n]
        self.used += n
        assert self.used <= self.arena.shape[1], self.used
        if len(shape) == 2:
            a = a.rearrange("p (a b) -> p a b", b=shape[1])
        if len(shape) == 3:
            a = a.rearrange("p (a b c) -> p a b c", b=shape[1], c=shape[2])
        return a


def stage_constants(m):
    nc = m.nc
    st = Stage(nc, "const")
    pool, dve, ready = st.sem("pool"), st.sem("dve"), st.sem("blocks_ready")
    with nc.Block() as block:
        @block.gpsimd
        def _(eng):
            ch = Chain(eng, pool)
            ch(eng.memset(m.ones[:, :], 1.0))
            ch(eng.memset(m.block[:, :, :], 1.0))
            for i in range(7):
                b = 1 << i
                v = m.block[:, i, :].rearrange("p (n b) -> p n b", b=b)
                ch(eng.affine_select(out=v, in_=v, compare_op=ALU.is_ge, fill=0.0, base=0,
                                     pattern=[[-b, P // b], [0, b]], channel_multiplier=1))
                ch(eng.affine_select(out=v, in_=v, compare_op=ALU.is_ge, fill=0.0, base=b - 1,
                                     pattern=[[b, P // b], [0, b]], channel_multiplier=-1))
            ch(eng.tensor_copy(m.ident[:, :], m.block[:, 0, :]))
            for i in range(2):
                ch(eng.tensor_copy(m.tri[:, i, :], m.block[:, 6, :]))
            ch(eng.affine_select(out=m.tri[:, 0, :], in_=m.tri[:, 0, :], compare_op=ALU.is_ge, fill=0.0,
                                 base=-1, pattern=[[1, P]], channel_multiplier=-1))
            ch(eng.affine_select(out=m.tri[:, 1, :], in_=m.tri[:, 1, :], compare_op=ALU.is_ge, fill=0.0,
                                 base=-1, pattern=[[-1, P]], channel_multiplier=1))
            ch(eng.memset(m.reset[:, :, :], 1.0))
            ch(eng.memset(m.reset[:, :, 0:1], 0.0))
            for i, e in enumerate((EPS, GN_EPS, LN_EPS)):
                ch(eng.memset(m.eps[:, i:i + 1], e))
            ch(eng.memset(m.row0[:, :], -float(EXPERTS)))
            eng.sem_inc(ready, 1)

        @block.vector
        def _(eng):
            ch = Chain(eng, dve)
            eng.wait_ge(ready, 1)
            for i in range(6):
                ch(eng.tensor_tensor(m.level[:, i, :], m.block[:, i + 1, :], m.block[:, i, :], ALU.subtract))
            for i in range(2):
                ch(eng.tensor_tensor(m.trid[:, i, :], m.tri[:, i, 0:CH], m.tri[:, i, CH:P], ALU.add))
                ch(eng.tensor_tensor(m.trid[:, i, :], m.trid[:, i, :], m.ident[:, 0:CH], ALU.add))
                ch(eng.tensor_tensor(m.trid[:, i, :], m.trid[:, i, :], m.ident[:, CH:P], ALU.add))
    st.close()


def stage_load_x(m):
    nc, d = m.nc, m.dram
    st = Stage(nc, "load")
    landed, turned, copied = st.sem("landed"), st.sem("turned"), st.sem("copied")
    m.used = 0
    xt = m.take(TILES, D)
    with nc.Block() as block:
        @block.sync
        def _(eng):
            eng.dma_start(xt[:, 0:4, :], d["x_sample"][0].rearrange("(t p) c -> p t c", p=P)).then_inc(landed, 16)
            eng.dma_start(xt[:, 4, :], d["x_prompt"][0]).then_inc(landed, 16)

        @block.tensor
        def _(eng):
            eng.wait_ge(landed, 32)
            for n in range(TILES * KB // 4):
                t, k0 = n // 2, 4 * (n % 2)
                if n >= 8:
                    eng.wait_ge(copied, n - 7)
                for j in range(4):
                    mm = eng.transpose(m.bank(n % 8)[:, P * j:P * j + P], xt[:, t, P * (k0 + j):P * (k0 + j) + P],
                                       m.ident[:, :])
                mm.then_inc(turned, 1)

        @block.vector
        def _(eng):
            for n in range(TILES * KB // 4):
                t, k0 = n // 2, 4 * (n % 2)
                eng.wait_ge(turned, n + 1)
                eng.tensor_copy(m.x[:, k0:k0 + 4, P * t:P * t + P],
                                m.bank(n % 8).rearrange("p (a b) -> p a b", b=P)).then_inc(copied, 1)
    st.close()


def stage_params(m, l):
    nc, d = m.nc, m.dram
    st = Stage(nc, "par")
    landed, turned, copied, sig, dve = (st.sem(n) for n in ("landed", "turned", "copied", "sigmoid", "dve"))
    m.used = 0
    rows = m.take(3, P)
    t1 = m.take(KB, 2)

    def vec(name):
        a = d[name][l]
        if len(a.shape) == 1:
            return a.rearrange("(b c) -> b c", c=P)
        if name == "r_k":
            return a.rearrange("h k -> (h k)").rearrange("(b c) -> b c", c=P)
        return a.rearrange("a (b c) -> (a b) c", c=P)

    loads = [(0, R_ADA, vec("ada_b")), (0, R_MU, vec("shift_mu")), (0, R_W0, vec("decay_w0")),
             (0, R_A0, vec("iclr_a0")), (0, R_KK, vec("k_k")), (0, R_KA, vec("k_a")),
             (1, R_N1, vec("norm1_g")), (1, R_N2, vec("norm2_g")), (1, R_RK, vec("r_k")), (1, R_GNG, vec("gn_g")),
             (1, R_GNB, vec("gn_b")), (1, R_PB, vec("pool_b")), (1, R_PS, vec("pool_scale")),
             (1, R_CB, vec("conv_b")), (1, R_LG, vec("cln_g")), (1, R_LB, vec("cln_b")),
             (1, R_C, d["c"].rearrange("a (b c) -> (a b) c", c=P)),
             (1, R_CC, d["c_ctx"].rearrange("(b c) -> b c", c=P)),
             (1, R_FG, d["final_g"].rearrange("(b c) -> b c", c=P)),
             (2, 0, vec("conv_w"))]
    sizes = (R_KA + KB, R_FG + KB, TAPS * 4)
    with nc.Block() as block:
        @block.sync
        def _(eng):
            for tile, r, src in loads:
                eng.dma_start(rows[r:r + src.shape[0], tile, :], src).then_inc(landed, 16)

        @block.tensor
        def _(eng):
            eng.wait_ge(landed, 16 * len(loads))
            for i, n in enumerate(sizes):
                mm = eng.transpose(m.bank(0)[:, P * i:P * i + n], rows[0:n, i, :], m.ident[0:n, 0:n])
            mm.then_inc(turned, 1)

        @block.scalar
        def _(eng):
            eng.wait_ge(copied, 1)
            for i, r in enumerate((R_C, R_CC)):
                eng.activation(t1[:, :, i], m.par[:, 1, r:r + KB], ACT.Sigmoid).then_inc(sig, 1)

        @block.vector
        def _(eng):
            ch = Chain(eng, dve)
            eng.wait_ge(turned, 1)
            for i, n in enumerate(sizes):
                ch(eng.tensor_copy(m.par[:, i, 0:n], m.bank(0)[:, P * i:P * i + n]))
            eng.sem_inc(copied, 1)
            eng.wait_ge(sig, 2)
            for i, r in enumerate((R_C, R_CC)):
                ch(eng.tensor_tensor(m.silu_c[:, :, i], t1[:, :, i], m.par[:, 1, r:r + KB], ALU.mult))
    st.close()


def stage_modulation(m, l):
    nc = m.nc
    ada = m.dram["ada_w"].rearrange("l (k p) (s b c) -> l s b p k c", p=P, b=KB, c=P)
    with nc.Fori(0, 6) as s:
        st = Stage(nc, "mod")
        landed = [st.sem(f"w{i}") for i in range(WRING)]
        used, done, dve = st.sem("used"), st.sem("done"), st.sem("dve")
        m.used = 0
        bias = m.take(KB)
        with nc.Block() as block:
            @block.sync
            def _(eng):
                for b in range(KB):
                    if b >= WRING:
                        eng.wait_ge(used, b - WRING + 1)
                    eng.dma_start(m.w[:, b % WRING], ada[l, s, b]).then_inc(landed[b % WRING], 16)

            @block.tensor
            def _(eng):
                for b in range(KB):
                    eng.wait_ge(landed[b % WRING], 16 * (b // WRING + 1))
                    for k in range(KB):
                        mm = eng.matmul(m.bank(0)[:, 2 * b:2 * b + 2], m.w[:, b % WRING, k, :], m.silu_c[:, k, :],
                                        start=(k == 0), stop=(k == KB - 1))
                    mm.then_inc(used, 1)

            @block.vector
            def _(eng):
                ch = Chain(eng, dve)
                ch(eng.tensor_copy(bias, m.par[:, 0, 0:48].rearrange("p (s b) -> p s b", b=KB)[:, s, :]))
                eng.wait_ge(used, KB)
                ch(eng.tensor_tensor(m.mod[:, s, :, :], m.bank(0)[:, 0:2 * KB].rearrange("p (b c) -> p b c", c=2),
                                     bias.unsqueeze(2).to_broadcast([P, KB, 2]), ALU.add))
        st.close()
    st = Stage(nc, "scl")
    dve = st.sem("dve")
    with nc.Block() as block:
        @block.vector
        def _(eng):
            ch = Chain(eng, dve)
            for i, (sec, r) in enumerate(((SC1, R_N1), (SC2, R_N2))):
                gain = m.par[:, 1, r:r + KB].unsqueeze(2).to_broadcast([P, KB, 2])
                ch(eng.tensor_scalar(m.scale[:, i], m.mod[:, sec], 1.0, None, ALU.add))
                ch(eng.tensor_tensor(m.scale[:, i], m.scale[:, i], gain, ALU.mult))
            ch(eng.tensor_scalar(m.row0[:, :], m.row0[:, :], float(EXPERTS), None, ALU.add))
            for t in range(TILES):
                ch(eng.tensor_copy(m.gate2[:, t, :], m.mod[:, GT2, :, int(t >= LAT // P)]))
    st.close()


def stage_norm(m, which):
    nc = m.nc
    st = Stage(nc, "norm")
    squared, summed, rooted, scaled = (st.sem(n) for n in ("squared", "summed", "rooted", "scaled"))
    dve = st.sem("dve")
    m.used = 0
    sq, root = m.take(KB, T), m.take(T)
    with nc.Block() as block:
        @block.scalar
        def _(eng):
            for k in range(KB):
                eng.activation(sq[:, k, :], m.x[:, k, :], ACT.Square).then_inc(squared, 1)
            eng.wait_ge(summed, 1)
            eng.activation(root[:, :], m.ps[0][:, 0:T], ACT.Sqrt, scale=1.0 / D, bias=m.eps[:, 0:1])\
               .then_inc(rooted, 1)
            for k in range(KB):
                eng.wait_ge(scaled, k + 1)
                if which == 2:
                    eng.activation(m.h[:, k, :], sq[:, k, :], ACT.Copy, scale=m.par[:, 1, R_FG + k:R_FG + k + 1])
                    continue
                for i, (c0, n) in enumerate(SEGMENTS):
                    eng.activation(m.h[:, k, c0:c0 + n], sq[:, k, c0:c0 + n], ACT.Identity,
                                   scale=m.scale[:, which, k, i:i + 1],
                                   bias=m.mod[:, (SH1, SH2)[which], k, i:i + 1])

        @block.tensor
        def _(eng):
            for k in range(KB):
                eng.wait_ge(squared, k + 1)
                for c0, n in SEGMENTS:
                    mm = eng.matmul(m.ps[0][:, c0:c0 + n], m.ones[:, :], sq[:, k, c0:c0 + n],
                                    start=(k == 0), stop=(k == KB - 1))
            mm.then_inc(summed, 1)

        @block.vector
        def _(eng):
            ch = Chain(eng, dve)
            eng.wait_ge(rooted, 1)
            ch(eng.reciprocal(root[:, :], root[:, :]))
            for k in range(KB):
                eng.tensor_tensor(sq[:, k, :], m.x[:, k, :], root[:, :], ALU.mult).then_inc(scaled, 1)
    st.close()

def shift_mix(m, ch, pad, tmp, mu, dst):
    eng = ch.eng
    n = T + 2
    ch(eng.tensor_tensor(tmp, pad[:, 0:n], pad[:, 2:n + 2], ALU.add))
    ch(eng.scalar_tensor_tensor(out=tmp, in0=tmp, scalar=0.5, in1=pad[:, 1:n + 1],
                                op0=ALU.mult, op1=ALU.subtract))
    for c0, w, off in ((0, LAT, 0), (LAT, CTX, 2)):
        ch(eng.scalar_tensor_tensor(out=dst[:, c0:c0 + w], in0=tmp[:, c0 + off:c0 + off + w], scalar=mu,
                                    in1=pad[:, c0 + off + 1:c0 + off + 1 + w], op0=ALU.mult, op1=ALU.add))


def pad_edges(eng, pad):
    return [eng.memset(pad[:, 0:1], 0.0), eng.memset(pad[:, LAT + 1:LAT + 3], 0.0),
            eng.memset(pad[:, T + 3:T + 4], 0.0)]


def project(eng, m, psum, slot, src):
    for k in range(KB):
        for c0, n in SEGMENTS:
            mm = eng.matmul(psum[:, c0:c0 + n], m.w[:, slot, k, :], src[:, k, c0:c0 + n],
                            start=(k == 0), stop=(k == KB - 1))
    return mm


def stage_lowrank(m, l):
    nc = m.nc
    st = Stage(nc, "lo")
    landed = [st.sem(f"w{i}") for i in range(3)]
    edges, projected, padded, mixed, dve = (st.sem(n) for n in ("edges", "projected", "padded", "mixed", "dve"))
    m.used = 0
    pad, tmp, mix = m.take(3, T + 4), m.take(T + 2), m.take(3, T)
    with nc.Block() as block:
        @block.sync
        def _(eng):
            for i in range(3):
                eng.dma_start(m.w[:, i], m.w_in[l, B_LO + i]).then_inc(landed[i], 16)

        @block.tensor
        def _(eng):
            for i in range(3):
                eng.wait_ge(landed[i], 16)
                project(eng, m, m.ps[i], i, m.h).then_inc(projected, 1)

        @block.scalar
        def _(eng):
            for i in range(3):
                eng.wait_ge(projected, i + 1)
                for c0, n, off in ((0, LAT, 1), (LAT, CTX, 3)):
                    eng.activation(pad[:, i, c0 + off:c0 + off + n], m.ps[i][:, c0:c0 + n], ACT.Copy)\
                       .then_inc(padded, 1)
            for i, f in enumerate((ACT.Tanh, ACT.Copy, ACT.Sigmoid)):
                eng.wait_ge(mixed, i + 1)
                eng.activation(m.lo[:, i, :], mix[:, i, :], f)

        @block.vector
        def _(eng):
            ch = Chain(eng, dve)
            for i in range(3):
                for ins in pad_edges(eng, pad[:, i]):
                    ch(ins)
                eng.wait_ge(padded, 2 * i + 2)
                mu = m.par[:, 0, R_MU + B_LO + i:R_MU + B_LO + i + 1]
                shift_mix(m, ch, pad[:, i], tmp, mu, mix[:, i])
                eng.sem_inc(mixed, 1)
    st.close()


def stage_rwkv(m, l, hp):
    nc, d = m.nc, m.dram
    st = Stage(nc, "rwkv")
    s = st.sem
    w_land = [s(f"w{i}") for i in range(3)]
    small, projected, padded, k_mixed, nrm, ss_done, rooted, act = (
        s(n) for n in ("small", "projected", "padded", "k_mixed", "kk_squared", "kk_summed", "kk_rooted", "act"))
    dve, pool, mixed, par_ready = s("dve"), s("pool"), s("mixed"), s("params_ready")
    g_done, za, sg, qe, exps = s("g_done"), s("za"), s("sigmoids"), s("qe"), s("exps")
    vbd_ready, bd_ready, zeroed, free_za = s("v_ready"), s("operands_ready"), s("zeroed"), s("za_free")
    t_dve, t_act, t_done = s("products_out_dve"), s("products_out_act"), s("products_done")
    d1, lx, lxe, ld_, lde, lte = s("inverse_start"), s("x_done"), s("x_out"), s("dd_done"), s("d_out"), s("dt_out")
    s_in, s_turned, s_set = s("state_in"), s("state_turned"), s("state_set")
    u0_done, u0_out, u_done, u_out, s_done, s_out, y_done, y_out = (
        s(n) for n in ("u0_done", "u0_out", "u_done", "u_out", "s_done", "s_out", "y_done", "y_out"))
    f_turned, f_out, stored = s("final_turned"), s("final_out"), s("final_stored")
    y_ready, gsum, yc_ready, gsq, groot = s("y_ready"), s("y_summed"), s("y_centred"), s("y_squared"), s("gn_rooted")
    q_ready = s("bonus_ready")

    m.used = 0
    par = m.take(14)
    pad, tmp = m.take(T + 4), m.take(T + 2)
    r, k, v, nkk, gate = (m.take(T) for _ in range(5))
    sig, q, e, a = (m.take(T) for _ in range(4))
    x1, x2, x3 = (m.take(T) for _ in range(3))
    kds, ys = m.take(T), m.take(T)
    ws = m.take(3, P)
    a_bd, b_bd, k_bd, v_bd = (m.take(NCH, P) for _ in range(4))
    rt = m.take(NCH, CH)
    b_tok, k_tok, v_tok = (m.take(NCH, P) for _ in range(3))
    akt, dd, dt, abt = (m.take(NCH, P) for _ in range(4))
    xx = b_bd
    rbt, rkt = m.take(NCH, CH), m.take(NCH, CH)
    s_raw = m.take(2, P)
    state = m.take(2, P)
    us, u0s = (tmp[:, 2 * P * i:2 * P * i + 2 * P].rearrange("p (c t) -> p c t", t=P) for i in range(2))
    u = lambda c: slice(CH * c, CH * c + CH)
    chunks = lambda t: t.rearrange("p (c t) -> p c t", t=CH)
    w2 = d["decay_w2"].rearrange("l e r (b c) -> l b (e r) c", c=P)
    a2 = d["iclr_a2"].rearrange("l e r (b c) -> l b (e r) c", c=P)
    g2 = d["gate_g2"].rearrange("l r (b c) -> l b r c", c=P)
    heads = ((0, CH), (CH, P))
    PRODUCTS = [(w, g) for g in range(3) for w in ("abt", "ab", "akt", "rbt", "rkt", "b_tok", "k_tok")]
    BY_DVE = {"abt", "ab", "akt", "rbt", "rkt"}

    def products(e):
        return PRODUCTS + ([("v_tok", g) for g in range(3)] if e == 0 else [])

    def out_count(e, n, by_dve):
        return sum((w in BY_DVE) == by_dve for i in range(e) for w, _ in products(i)) + \
            sum((w in BY_DVE) == by_dve for w, _ in products(e)[:n])

    def done_count(e):
        return sum(len(products(i)) for i in range(e))

    steps = [(i, c) for i in range(NLAT) for c in ((0, 1) if i < NCTX else (0,))]
    NS = len(steps)

    def chunk_of(e, i, c):
        n, base = ((NLAT, 0), (NCTX, NLAT))[c]
        return base + (i if e == 0 else n - 1 - i)

    with nc.Block() as block:
        @block.sync
        def _(eng):
            for i, b in enumerate((B_K, B_R, B_V)):
                eng.dma_start(m.w[:, i], m.w_in[l, hp + b]).then_inc(w_land[i], 16)
            for i, t in enumerate((w2, a2, g2)):
                eng.dma_start(ws[:, i, :], t[l, hp]).then_inc(small, 16)
            eng.wait_ge(zeroed, 1)
            for e_ in range(2):
                if e_ == 1:
                    eng.wait_ge(s_set, 1)
                for i, (p0, p1) in enumerate(heads):
                    src = d["state_rwkv"][0].rearrange("l e (b i) v k -> l e i b v k", i=2)[l, e_, i, hp]
                    eng.dma_start(s_raw[p0:p1, 0, p0:p1], src).then_inc(s_in, 16)
            out = d["new_state"][0].rearrange("l e (b i) v k -> l e i b v k", i=2)
            for e_ in range(2):
                eng.wait_ge(f_out, e_ + 1)
                for i, (p0, p1) in enumerate(heads):
                    eng.dma_start(out[l, e_, i, hp], s_raw[p0:p1, 1, p0:p1]).then_inc(stored, 16)
                eng.wait_ge(stored, 32 * (e_ + 1))

        @block.gpsimd
        def _(eng):
            ch = Chain(eng, pool)
            for t in (a_bd, b_bd, k_bd, v_bd, s_raw):
                ch(eng.memset(t[0:CH, :, CH:P], 0.0))
                ch(eng.memset(t[CH:P, :, 0:CH], 0.0))
            eng.sem_inc(zeroed, 1)

        @block.tensor
        def _(eng):
            for i in range(3):
                eng.wait_ge(w_land[i], 16)
                project(eng, m, m.ps[i], i, m.h).then_inc(projected, 1)
            eng.wait_ge(small, 48)
            for c0, n in SEGMENTS:
                mm = eng.matmul(m.ps[3][:, c0:c0 + n], ws[:, 2, :], m.lo[:, 2, c0:c0 + n], start=True, stop=True)
            mm.then_inc(g_done, 1)
            eng.wait_ge(nrm, 1)
            for c0, n in SEGMENTS:
                mm = eng.matmul(m.ps[0][:, c0:c0 + n], m.block[:, 6, :], tmp[:, c0:c0 + n], start=True, stop=True)
            mm.then_inc(ss_done, 1)
            for e_ in range(2):
                eng.wait_ge(free_za, e_ + 1)
                for i in range(2):
                    for c0, n in SEGMENTS:
                        h0 = CH * e_
                        mm = eng.matmul(m.ps[1 + i][:, c0:c0 + n], ws[h0:h0 + CH, i, :], m.lo[h0:h0 + CH, i, c0:c0 + n],
                                        start=True, stop=True)
                    mm.then_inc(za, 1)
                eng.wait_ge(bd_ready, e_ + 1)
                if e_ == 0:
                    eng.wait_ge(vbd_ready, 1)
                for n, (what, g) in enumerate(products(e_)):
                    if n >= 8:
                        eng.wait_ge(t_dve, out_count(e_, n - 7, True))
                        eng.wait_ge(t_act, out_count(e_, n - 7, False))
                    c0, w = GROUPS[g]
                    for j in range(w):
                        c = c0 + j
                        if what in ("rbt", "rkt"):
                            o = m.bank(n % 8)[:, CH * j:CH * j + CH]
                            mm = eng.matmul(o, (b_bd if what == "rbt" else k_bd)[:, c, :], rt[:, c, :],
                                            start=True, stop=True)
                            continue
                        o = m.bank(n % 8)[:, P * j:P * j + P]
                        if what == "abt":
                            mm = eng.matmul(o, b_bd[:, c, :], a_bd[:, c, :], start=True, stop=True)
                        elif what == "ab":
                            mm = eng.matmul(o, a_bd[:, c, :], b_bd[:, c, :], start=True, stop=True)
                        elif what == "akt":
                            mm = eng.matmul(o, k_bd[:, c, :], a_bd[:, c, :], start=True, stop=True)
                        else:
                            mm = eng.transpose(o, {"b_tok": b_bd, "k_tok": k_bd, "v_tok": v_bd}[what][:, c, :],
                                               m.ident[:, :])
                    mm.then_inc(t_done, 1)
                eng.wait_ge(d1, e_ + 1)
                eng.wait_ge(t_act, out_count(e_ + 1, 0, False))
                for lv in range(5):
                    n0 = 15 * e_ + 3 * lv
                    for g, (c0, w) in enumerate(GROUPS):
                        if lv > 0:
                            eng.wait_ge(lde, n0 - 3 + g + 1)
                            eng.wait_ge(lte, n0 - 3 + g + 1)
                        for j in range(w):
                            mm = eng.matmul(m.bank(g)[:, P * j:P * j + P], abt[:, c0 + j, :], dd[:, c0 + j, :],
                                            start=True, stop=True)
                        mm.then_inc(lx, 1)
                    for g, (c0, w) in enumerate(GROUPS):
                        eng.wait_ge(lxe, n0 + g + 1)
                        for j in range(w):
                            eng.matmul(m.bank(3 + g)[:, P * j:P * j + P], dt[:, c0 + j, :], xx[:, c0 + j, :],
                                       start=True, stop=True)
                        for j in range(w):
                            mm = eng.matmul(m.bank(g)[:, P * j:P * j + P], xx[:, c0 + j, :], dt[:, c0 + j, :],
                                            start=True, stop=True)
                        mm.then_inc(ld_, 1)
                eng.wait_ge(lde, 15 * (e_ + 1))
                eng.wait_ge(lte, 15 * (e_ + 1))
                eng.wait_ge(s_in, 32 * (e_ + 1))
                eng.transpose(m.bank(0)[:, 0:P], s_raw[:, 0, :], m.ident[:, :]).then_inc(s_turned, 1)
                eng.wait_ge(s_set, e_ + 1)
                for n, (i, c) in enumerate(steps):
                    x = chunk_of(e_, i, c)
                    N = NS * e_ + n
                    if n >= 1:
                        eng.wait_ge(s_out, N)
                        eng.wait_ge(y_out, N)
                    bu0, bu, bs, by = (m.bank(4 * c + j) for j in range(4))
                    eng.matmul(bu0[:, 0:P], a_bd[:, x, :], state[:, c, :], start=True, stop=False)
                    eng.matmul(bu0[:, 0:P], akt[:, x, :], v_tok[:, x, :], start=False, stop=True).then_inc(u0_done, 1)
                    eng.matmul(bs[:, 0:P], m.ident[:, :], state[:, c, :], start=True, stop=False)
                    eng.matmul(bs[:, 0:P], k_tok[:, x, :], v_tok[:, x, :], start=False, stop=False)
                    eng.matmul(by[:, 0:CH], state[:, c, :], rt[:, x, :], start=True, stop=False)
                    eng.matmul(by[:, 0:CH], v_tok[:, x, :], rkt[:, x, :], start=False, stop=False)
                    eng.wait_ge(u0_out, N + 1)
                    eng.matmul(bu[:, 0:P], dt[:, x, :], u0s[:, c, :], start=True, stop=True).then_inc(u_done, 1)
                    eng.wait_ge(u_out, N + 1)
                    eng.matmul(bs[:, 0:P], b_tok[:, x, :], us[:, c, :], start=False, stop=True).then_inc(s_done, 1)
                    eng.matmul(by[:, 0:CH], us[:, c, :], rbt[:, x, :], start=False, stop=True).then_inc(y_done, 1)
                eng.wait_ge(s_out, NS * (e_ + 1))
                eng.wait_ge(y_out, NS * (e_ + 1))
                eng.transpose(m.bank(0)[:, 0:P], state[:, 1, :], m.ident[:, :]).then_inc(f_turned, 1)
                eng.wait_ge(f_out, e_ + 1)
            eng.wait_ge(q_ready, 1)
            for c0, n in SEGMENTS:
                mm = eng.matmul(m.ps[2][:, c0:c0 + n], m.block[:, 6, :], x1[:, c0:c0 + n], start=True, stop=True)
            mm.then_inc(gsum, 1)
            eng.wait_ge(y_ready, 1)
            for c0, n in SEGMENTS:
                mm = eng.matmul(m.ps[0][:, c0:c0 + n], m.block[:, 6, :], ys[:, c0:c0 + n], start=True, stop=True)
            mm.then_inc(gsum, 1)
            eng.wait_ge(gsq, 1)
            for c0, n in SEGMENTS:
                mm = eng.matmul(m.ps[1][:, c0:c0 + n], m.block[:, 6, :], x2[:, c0:c0 + n], start=True, stop=True)
            mm.then_inc(gsum, 1)

        @block.scalar
        def _(eng):
            ch = Chain(eng, act)
            eng.wait_ge(par_ready, 1)
            for i in range(3):
                eng.wait_ge(projected, i + 1)
                if i == 0:
                    eng.wait_ge(mixed, 1)
                else:
                    eng.wait_ge(mixed, i + 1)
                for c0, n, off in ((0, LAT, 1), (LAT, CTX, 3)):
                    eng.activation(pad[:, c0 + off:c0 + off + n], m.ps[i][:, c0:c0 + n], ACT.Copy)\
                       .then_inc(padded, 1)
            eng.wait_ge(g_done, 1)
            eng.activation(gate[:, :], m.ps[3][:, 0:T], ACT.Copy)
            eng.wait_ge(ss_done, 1)
            eng.activation(e[:, :], m.ps[0][:, 0:T], ACT.Sqrt).then_inc(rooted, 1)
            for e_ in range(2):
                eng.wait_ge(za, 2 * e_ + 1)
                eng.activation(sig[:, :], m.ps[1][:, 0:T], ACT.Sigmoid, bias=par[:, 3 + e_:4 + e_]).then_inc(sg, 1)
                eng.wait_ge(za, 2 * e_ + 2)
                eng.activation(a[:, :], m.ps[2][:, 0:T], ACT.Sigmoid, bias=par[:, 5 + e_:6 + e_]).then_inc(sg, 1)
                eng.wait_ge(qe, e_ + 1)
                eng.activation(x1[:, :], q[:, :], ACT.Exp, scale=-DECAY).then_inc(exps, 1)
                eng.activation(x2[:, :], e[:, :], ACT.Exp, scale=-DECAY).then_inc(exps, 1)
                eng.activation(x3[:, :], q[:, :], ACT.Exp, scale=DECAY).then_inc(exps, 1)
                for n, (what, g) in enumerate(products(e_)):
                    if what in BY_DVE:
                        continue
                    c0, w = GROUPS[g]
                    eng.wait_ge(t_done, done_count(e_) + n + 1)
                    src = m.bank(n % 8)[:, 0:P * w].rearrange("p (c t) -> p c t", t=P)
                    eng.activation({"b_tok": b_tok, "k_tok": k_tok, "v_tok": v_tok}[what][:, c0:c0 + w, :], src,
                                   ACT.Copy).then_inc(t_act, 1)
                eng.wait_ge(s_turned, e_ + 1)
                ch(eng.activation(state[:, 0, :], m.bank(0)[:, 0:P], ACT.Copy))
                ch(eng.activation(state[:, 1, :], m.ident[:, :], ACT.Copy, scale=0.0))
                eng.sem_inc(s_set, 1)
                for n, (i, c) in enumerate(steps):
                    N = NS * e_ + n
                    eng.wait_ge(u0_done, N + 1)
                    eng.activation(u0s[:, c, :], m.bank(4 * c)[:, 0:P], ACT.Copy).then_inc(u0_out, 1)
                    if e_ == 0:
                        x = chunk_of(e_, i, c)
                        eng.wait_ge(y_done, N + 1)
                        eng.activation(ys[:, u(x)], m.bank(4 * c + 3)[:, 0:CH], ACT.Copy).then_inc(y_out, 1)
                eng.wait_ge(f_turned, e_ + 1)
                if e_ == 1:
                    eng.wait_ge(stored, 32)
                ch(eng.activation(s_raw[:, 1, :], m.bank(0)[:, 0:P], ACT.Copy))
                eng.sem_inc(f_out, 1)
            eng.wait_ge(yc_ready, 1)
            eng.activation(x2[:, :], ys[:, :], ACT.Square).then_inc(gsq, 1)
            eng.wait_ge(gsum, 3)
            eng.activation(x3[:, :], m.ps[1][:, 0:T], ACT.Sqrt, scale=1.0 / HD, bias=m.eps[:, 1:2]).then_inc(groot, 1)

        @block.vector
        def _(eng):
            ch = Chain(eng, dve)
            blk = lambda i, r0: m.par[:, i, r0:r0 + KB]
            for j, (i, r0) in enumerate(((0, R_MU), (0, R_MU + 8), (0, R_MU + 16), (0, R_W0), (0, R_W0 + 8), (0, R_A0),
                                         (0, R_A0 + 8), (0, R_KK), (0, R_KA), (1, R_RK), (1, R_GNG), (1, R_GNB))):
                j = j if j < 9 else j + 1
                ch(eng.tensor_copy(par[:, j:j + 1], m.par[:, i, bass.ds(hp + r0, 1)]))
            ch(eng.tensor_scalar(par[:, 9:10], par[:, 8:9], -1.0, 1.0, ALU.mult, ALU.add))
            for ins in pad_edges(eng, pad):
                ch(ins)
            eng.sem_inc(par_ready, 1)
            eng.sem_inc(mixed, 1)
            eng.wait_ge(padded, 2)
            shift_mix(m, ch, pad, tmp, par[:, 1:2], k)
            ch(eng.tensor_scalar(nkk, k, par[:, 7:8], None, ALU.mult))
            eng.sem_inc(mixed, 1)
            eng.wait_ge(padded, 4)
            shift_mix(m, ch, pad, tmp, par[:, 0:1], r)
            eng.sem_inc(mixed, 1)
            eng.wait_ge(padded, 6)
            shift_mix(m, ch, pad, tmp, par[:, 2:3], v)
            ch(eng.tensor_tensor(tmp[:, 0:T], nkk, nkk, ALU.mult))
            eng.sem_inc(nrm, 1)
            eng.wait_ge(zeroed, 1)
            for p0, p1 in heads:
                ch(eng.tensor_copy(v_bd[p0:p1, :, p0:p1], chunks(v)[p0:p1]))
            eng.sem_inc(vbd_ready, 1)
            eng.wait_ge(rooted, 1)
            eng.sem_inc(free_za, 1)
            ch(eng.tensor_scalar(e, e, 1e-12, None, ALU.max))
            ch(eng.reciprocal(e, e))
            ch(eng.scalar_tensor_tensor(out=nkk, in0=nkk, scalar=-1.0, in1=e, op0=ALU.mult, op1=ALU.mult))
            for e_ in range(2):
                eng.wait_ge(sg, 2 * e_ + 1)
                ch(eng.tensor_tensor_scan(q, m.reset[:, :, :].rearrange("p c t -> p (c t)"), sig, 0.0,
                                          ALU.mult, ALU.add))
                if e_ == 1:
                    ch(eng.tensor_tensor(chunks(e), chunks(q)[:, :, CH - 1:CH].to_broadcast([P, NCH, CH]), chunks(q),
                                         ALU.subtract))
                    ch(eng.tensor_tensor(q, e, sig, ALU.add))
                else:
                    ch(eng.tensor_tensor(e, q, sig, ALU.subtract))
                eng.sem_inc(qe, 1)
                eng.wait_ge(sg, 2 * e_ + 2)
                if e_ == 0:
                    eng.sem_inc(free_za, 1)
                ch(eng.tensor_tensor(sig, nkk, a, ALU.mult))
                ch(eng.tensor_scalar(a, a, par[:, 8:9], par[:, 9:10], ALU.mult, ALU.add))
                ch(eng.tensor_tensor(a, a, k, ALU.mult))
                if e_ == 0:
                    ch(eng.tensor_copy(kds, a))
                else:
                    ch(eng.tensor_tensor(kds, kds, a, ALU.add))
                eng.wait_ge(exps, 3 * (e_ + 1))
                ch(eng.tensor_tensor(rt.rearrange("p c t -> p (c t)"), r, x1, ALU.mult))
                for p0, p1 in heads:
                    ch(eng.tensor_tensor(a_bd[p0:p1, :, p0:p1], chunks(nkk)[p0:p1], chunks(x2)[p0:p1], ALU.mult))
                    ch(eng.scalar_tensor_tensor(out=b_bd[p0:p1, :, p0:p1], in0=chunks(sig)[p0:p1], scalar=-1.0,
                                                in1=chunks(x3)[p0:p1], op0=ALU.mult, op1=ALU.mult))
                    ch(eng.tensor_tensor(k_bd[p0:p1, :, p0:p1], chunks(a)[p0:p1], chunks(x3)[p0:p1], ALU.mult))
                eng.sem_inc(bd_ready, 1)
                for n, (what, g) in enumerate(products(e_)):
                    if what not in BY_DVE:
                        continue
                    c0, w = GROUPS[g]
                    eng.wait_ge(t_done, done_count(e_) + n + 1)
                    if what in ("rbt", "rkt"):
                        src = m.bank(n % 8)[:, 0:CH * w].rearrange("p (c t) -> p c t", t=CH)
                        dst, mask = (rbt if what == "rbt" else rkt)[:, c0:c0 + w, :], m.trid[:, e_]
                        mask = mask.unsqueeze(1).to_broadcast([P, w, CH])
                    else:
                        src = m.bank(n % 8)[:, 0:P * w].rearrange("p (c t) -> p c t", t=P)
                        dst = {"abt": abt, "ab": dd, "akt": akt}[what][:, c0:c0 + w, :]
                        mask = m.tri[:, 1 - e_ if what == "ab" else e_].unsqueeze(1).to_broadcast([P, w, P])
                    eng.tensor_tensor(dst, src, mask, ALU.mult).then_inc(t_dve, 1)
                eng.wait_ge(t_dve, out_count(e_ + 1, 0, True))
                lv0 = m.level[:, 0].unsqueeze(1).to_broadcast([P, NCH, P])
                one = m.ident[:, :].unsqueeze(1).to_broadcast([P, NCH, P])
                ch(eng.tensor_tensor(dd, dd, lv0, ALU.mult))
                ch(eng.tensor_tensor(dd, dd, one, ALU.add))
                ch(eng.tensor_tensor(dt, abt, lv0, ALU.mult))
                ch(eng.tensor_tensor(dt, dt, one, ALU.add))
                eng.sem_inc(d1, 1)
                for lv in range(5):
                    n0 = 15 * e_ + 3 * lv
                    for g, (c0, w) in enumerate(GROUPS):
                        eng.wait_ge(lx, n0 + g + 1)
                        src = m.bank(g)[:, 0:P * w].rearrange("p (c t) -> p c t", t=P)
                        mask = m.level[:, lv + 1].unsqueeze(1).to_broadcast([P, w, P])
                        eng.tensor_tensor(xx[:, c0:c0 + w, :], src, mask, ALU.mult).then_inc(lxe, 1)
                    for g, (c0, w) in enumerate(GROUPS):
                        eng.wait_ge(ld_, n0 + g + 1)
                        for b0, t, sem in ((3, dd, lde), (0, dt, lte)):
                            src = m.bank(b0 + g)[:, 0:P * w].rearrange("p (c t) -> p c t", t=P)
                            eng.tensor_tensor(t[:, c0:c0 + w, :], t[:, c0:c0 + w, :], src, ALU.add).then_inc(sem, 1)
                for n, (i, c) in enumerate(steps):
                    N = NS * e_ + n
                    x = chunk_of(e_, i, c)
                    end = CH * x + (CH - 1 if e_ == 0 else 0)
                    eng.wait_ge(u_done, N + 1)
                    eng.tensor_copy(us[:, c, :], m.bank(4 * c + 1)[:, 0:P]).then_inc(u_out, 1)
                    eng.wait_ge(s_done, N + 1)
                    eng.tensor_scalar(state[:, c, :], m.bank(4 * c + 2)[:, 0:P], x1[:, end:end + 1], None, ALU.mult)\
                       .then_inc(s_out, 1)
                    if e_ == 1:
                        eng.wait_ge(y_done, N + 1)
                        eng.tensor_tensor(ys[:, u(x)], ys[:, u(x)], m.bank(4 * c + 3)[:, 0:CH], ALU.add)\
                           .then_inc(y_out, 1)
            eng.wait_ge(s_out, 2 * NS)
            ch(eng.scalar_tensor_tensor(out=x1, in0=kds, scalar=par[:, 10:11], in1=r, op0=ALU.mult, op1=ALU.mult))
            eng.sem_inc(q_ready, 1)
            eng.wait_ge(y_out, 2 * NS)
            eng.sem_inc(y_ready, 1)
            eng.wait_ge(gsum, 2)
            ch(eng.scalar_tensor_tensor(out=ys, in0=m.ps[0][:, 0:T], scalar=-1.0 / HD, in1=ys,
                                        op0=ALU.mult, op1=ALU.add))
            eng.sem_inc(yc_ready, 1)
            ch(eng.tensor_tensor(v, v, m.ps[2][:, 0:T], ALU.mult))
            eng.wait_ge(groot, 1)
            ch(eng.reciprocal(x3, x3))
            ch(eng.tensor_tensor(ys, ys, x3, ALU.mult))
            ch(eng.tensor_scalar(ys, ys, par[:, 11:12], par[:, 12:13], ALU.mult, ALU.add))
            ch(eng.tensor_tensor(ys, ys, v, ALU.add))
            ch(eng.tensor_tensor(ys, ys, gate, ALU.mult))
            ch(eng.tensor_copy(m.ya[:, hp, :], ys))
    st.close()

def stage_branches(m, l):
    nc, d = m.nc, m.dram
    st = Stage(nc, "br")
    s = st.sem
    landed = [s(f"w{i}") for i in range(WRING)]
    pw_in, used, out_act, zeroed, edges, pooled, mixed = (
        s(n) for n in ("pool_w", "projected", "taken_out", "zeroed", "edges", "pooled", "pool_mixed"))
    dve, pool, act, gated, conv, cen, sums, sq_done, rooted, norm, sgm = (
        s(n) for n in ("dve", "pool", "act", "gated", "convolved", "centred", "sums", "squares", "rooted", "normed",
                       "sigmoids"))
    m.used = 0
    yb, yc = m.take(4, T), m.take(4, T)
    HALO = 8
    NL, NC_ = (ROWS + 2 * HALO) * GRID_W, CTX + 2 * HALO
    za, zb = m.take(4, NL + NC_), m.take(2, NL + NC_)
    cnt = m.take(3, ROWS + 2 * HALO + NC_)
    pw = m.take(4, P)
    HT = TAPS // 2
    RW = GRID_W + 2 * HT
    uc = m.take(ROWS * RW + CTX + 2 * HT)
    ga = m.take(T)
    NPROJ = 12
    cols = [B_POOL + i for i in range(4)]
    for i in range(4):
        cols += [B_CONV + 4 + i, B_CONV + i]

    def lat(t):
        return t[:, 0:NL]

    def ctx(t):
        return t[:, NL:NL + NC_]

    lat_u = uc[:, 0:ROWS * RW].rearrange("p (r w) -> p r w", w=RW)
    ctx_u = uc[:, ROWS * RW:]

    def take_pool(eng, ch, g):
        eng.wait_ge(sums, g + 1)
        ch(eng.tensor_scalar(yb[:, g, :], m.ps[3][:, 0:T], m.par[:, 1, R_PB + g:R_PB + g + 1],
                             m.par[:, 1, R_PS + g:R_PS + g + 1], ALU.add, ALU.mult))
        eng.sem_inc(mixed, 1)

    with nc.Block() as block:
        @block.sync
        def _(eng):
            eng.dma_start(pw, d["pool_w"].rearrange("l g c e -> l c g e")[l]).then_inc(pw_in, 16)
            for n, b in enumerate(cols):
                if n >= WRING:
                    eng.wait_ge(used, n - WRING + 1)
                eng.dma_start(m.w[:, n % WRING], m.w_in[l, b]).then_inc(landed[n % WRING], 16)

        @block.gpsimd
        def _(eng):
            ch = Chain(eng, pool)
            for t in [za[:, i] for i in range(4)]:
                ch(eng.memset(t[:, 0:HALO * GRID_W], 0.0))
                ch(eng.memset(t[:, (HALO + ROWS) * GRID_W:NL + HALO], 0.0))
                ch(eng.memset(t[:, NL + HALO + CTX:NL + NC_], 0.0))
            ch(eng.memset(uc, 0.0))
            ch(eng.memset(cnt, 0.0))
            ch(eng.memset(cnt[:, 0, HALO:HALO + ROWS], 1.0))
            ch(eng.memset(cnt[:, 0, ROWS + 3 * HALO:ROWS + 3 * HALO + CTX], 1.0))
            eng.sem_inc(zeroed, 1)

        @block.tensor
        def _(eng):
            for n in range(NPROJ):
                eng.wait_ge(landed[n % WRING], 16 * (n // WRING + 1))
                if n >= 3:
                    eng.wait_ge(out_act, n - 2)
                project(eng, m, m.ps[n % 3], n % WRING, m.h).then_inc(used, 1)
                if n != 6:
                    continue
                eng.wait_ge(pw_in, 16)
                for g in range(4):
                    eng.wait_ge(pooled, g + 1)
                    if g > 0:
                        eng.wait_ge(mixed, g)
                    for c0, w in SEGMENTS:
                        mm = eng.matmul(m.ps[3][:, c0:c0 + w], pw[:, g, :], za[:, g, c0:c0 + w],
                                        start=True, stop=True)
                    mm.then_inc(sums, 1)
            eng.wait_ge(out_act, NPROJ)
            eng.wait_ge(conv, 4)
            for g in range(4):
                for c0, n in SEGMENTS:
                    mm = eng.matmul(m.ps[0][:, c0:c0 + n], m.ones[:, :], yc[:, g, c0:c0 + n],
                                    start=(g == 0), stop=(g == 3))
            mm.then_inc(sums, 1)
            for g in range(4):
                eng.wait_ge(sq_done, g + 1)
                for c0, n in SEGMENTS:
                    mm = eng.matmul(m.ps[1][:, c0:c0 + n], m.ones[:, :], za[:, g, c0:c0 + n],
                                    start=(g == 0), stop=(g == 3))
            mm.then_inc(sums, 1)

        @block.scalar
        def _(eng):
            ch = Chain(eng, act)
            eng.wait_ge(zeroed, 1)
            for n in range(NPROJ):
                eng.wait_ge(used, n + 1)
                src = m.ps[n % 3]
                if n < 4:
                    ch(eng.activation(lat(za[:, n])[:, HALO * GRID_W:(HALO + ROWS) * GRID_W], src[:, 0:LAT], ACT.Copy))
                    ch(eng.activation(ctx(za[:, n])[:, HALO:HALO + CTX], src[:, LAT:T], ACT.Copy))
                elif n % 2 == 0:
                    if n > 4:
                        eng.wait_ge(gated, (n - 4) // 2)
                    ch(eng.activation(ga, src[:, 0:T], ACT.Sigmoid))
                else:
                    eng.wait_ge(gated, (n - 3) // 2)
                eng.sem_inc(out_act, 1)
            for g in range(4):
                eng.wait_ge(cen, g + 1)
                eng.activation(za[:, g, 0:T], yc[:, g, :], ACT.Square).then_inc(sq_done, 1)
            eng.wait_ge(sums, 6)
            eng.activation(ga, m.ps[1][:, 0:T], ACT.Sqrt, scale=1.0 / 512, bias=m.eps[:, 2:3]).then_inc(rooted, 1)
            for g in range(4):
                eng.wait_ge(norm, g + 1)
                eng.activation(za[:, g, 0:T], yc[:, g, :], ACT.Sigmoid).then_inc(sgm, 1)

        @block.vector
        def _(eng):
            ch = Chain(eng, dve)
            eng.wait_ge(zeroed, 1)
            nr = ROWS + 2 * HALO
            for g in range(4):
                eng.wait_ge(out_act, g + 1)
                srcs, c_src = za[:, g], cnt[:, 0]
                for j in range(g + 1):
                    sh = 1 << j
                    dst, c_dst = zb[:, j % 2], cnt[:, 1 + j % 2]
                    nl, nx = NL - (2 * sh - 1) * GRID_W, NC_ - (2 * sh - 1)
                    ch(eng.tensor_tensor(dst[:, 0:nl], srcs[:, 0:nl], srcs[:, sh * GRID_W:sh * GRID_W + nl], ALU.add))
                    ch(eng.tensor_tensor(ctx(dst)[:, 0:nx], ctx(srcs)[:, 0:nx], ctx(srcs)[:, sh:sh + nx], ALU.add))
                    for a0, w in ((0, nr - (2 * sh - 1)), (nr, nx)):
                        ch(eng.tensor_tensor(c_dst[:, a0:a0 + w], c_src[:, a0:a0 + w], c_src[:, a0 + sh:a0 + sh + w],
                                             ALU.add))
                    srcs, c_src = dst, c_dst
                half = 1 << g
                o, oc = HALO - half, zb[:, (g + 1) % 2]
                cr, cx = c_src[:, o:o + ROWS], c_src[:, nr + o:nr + o + CTX]
                ch(eng.reciprocal(cr, cr))
                ch(eng.reciprocal(cx, cx))
                sl = srcs[:, o * GRID_W:(o + ROWS) * GRID_W].rearrange("p (r w) -> p r w", w=GRID_W)
                ch(eng.tensor_tensor(oc[:, 0:LAT].rearrange("p (r w) -> p r w", w=GRID_W), sl,
                                     cr.unsqueeze(2).to_broadcast([P, ROWS, GRID_W]), ALU.mult))
                ch(eng.tensor_tensor(oc[:, LAT:T], ctx(srcs)[:, o:o + CTX], cx, ALU.mult))
                ch(eng.tensor_tensor(oc[:, 0:LAT], oc[:, 0:LAT], za[:, g, HALO * GRID_W:(HALO + ROWS) * GRID_W],
                                     ALU.subtract))
                ch(eng.tensor_tensor(oc[:, LAT:T], oc[:, LAT:T], ctx(za[:, g])[:, HALO:HALO + CTX], ALU.subtract))
                ch(eng.tensor_copy(za[:, g, 0:T], oc[:, 0:T]))
                eng.sem_inc(pooled, 1)
                if g > 0:
                    take_pool(eng, ch, g - 1)
            take_pool(eng, ch, 3)
            for g in range(4):
                eng.wait_ge(out_act, 5 + 2 * g)
                eng.wait_ge(used, 6 + 2 * g)
                src = m.ps[(5 + 2 * g) % 3]
                ch(eng.tensor_tensor(lat_u[:, :, HT:HT + GRID_W], ga[:, 0:LAT].rearrange("p (r w) -> p r w", w=GRID_W),
                                     src[:, 0:LAT].rearrange("p (r w) -> p r w", w=GRID_W), ALU.mult))
                ch(eng.tensor_tensor(ctx_u[:, HT:HT + CTX], ga[:, LAT:T], src[:, LAT:T], ALU.mult))
                eng.sem_inc(gated, 1)
                dl, dc = yc[:, g, 0:LAT].rearrange("p (r w) -> p r w", w=GRID_W), yc[:, g, LAT:T]
                for t in range(TAPS):
                    wt = m.par[:, 2, 4 * t + g:4 * t + g + 1]
                    il, ic = lat_u[:, :, t:t + GRID_W], ctx_u[:, t:t + CTX]
                    if t == 0:
                        cb = m.par[:, 1, R_CB + g:R_CB + g + 1]
                        ch(eng.tensor_scalar(dl, il, wt, cb, ALU.mult, ALU.add))
                        ch(eng.tensor_scalar(dc, ic, wt, cb, ALU.mult, ALU.add))
                    else:
                        ch(eng.scalar_tensor_tensor(out=dl, in0=il, scalar=wt, in1=dl, op0=ALU.mult, op1=ALU.add))
                        ch(eng.scalar_tensor_tensor(out=dc, in0=ic, scalar=wt, in1=dc, op0=ALU.mult, op1=ALU.add))
                eng.sem_inc(conv, 1)
            eng.wait_ge(sums, 5)
            for g in range(4):
                ch(eng.scalar_tensor_tensor(out=yc[:, g, :], in0=m.ps[0][:, 0:T], scalar=-1.0 / 512, in1=yc[:, g, :],
                                            op0=ALU.mult, op1=ALU.add))
                eng.sem_inc(cen, 1)
            eng.wait_ge(rooted, 1)
            ch(eng.reciprocal(ga, ga))
            for g in range(4):
                ch(eng.tensor_tensor(yc[:, g, :], yc[:, g, :], ga, ALU.mult))
                ch(eng.tensor_scalar(yc[:, g, :], yc[:, g, :], m.par[:, 1, R_LG + g:R_LG + g + 1],
                                     m.par[:, 1, R_LB + g:R_LB + g + 1], ALU.mult, ALU.add))
                eng.sem_inc(norm, 1)
            for g in range(4):
                eng.wait_ge(sgm, g + 1)
                ch(eng.tensor_tensor(yc[:, g, :], yc[:, g, :], za[:, g, 0:T], ALU.mult))

    st.close()


def stage_merge(m, l, db):
    nc, d = m.nc, m.dram
    st = Stage(nc, "mg")
    s = st.sem
    landed = [s(f"w{i}") for i in range(WRING)]
    done, gates, dve = s("done"), s("gates"), s("dve")
    m.used = 0
    yb, yc, merged = m.take(4, T), m.take(4, T), m.take(KB, T)
    g, acc, part = m.take(3, T), m.take(T), m.take(T)
    outs = [d[n].rearrange("l (k p) (b c) -> l b p k c", p=P, c=P) for n in ("w_a_out", "w_b_out", "w_c_out")]
    with nc.Block() as block:
        @block.sync
        def _(eng):
            for i in range(3):
                eng.dma_start(m.w[:, i], m.w_in[l, db + (B_GATE + KB * i)]).then_inc(landed[i], 16)
            eng.dma_start(m.w[:, 3], outs[0][l, db]).then_inc(landed[3], 16)
            eng.dma_start(m.w[:, 4, 0:4], outs[1][l, db]).then_inc(landed[4], 16)
            eng.dma_start(m.w[:, 4, 4:8], outs[2][l, db]).then_inc(landed[4], 16)

        @block.tensor
        def _(eng):
            for i in range(4):
                eng.wait_ge(landed[i], 16)
                project(eng, m, m.ps[i], i, m.h if i < 3 else m.ya).then_inc(done, 1)
            eng.wait_ge(landed[4], 32)
            for i, y in enumerate((yb, yc)):
                eng.wait_ge(gates, i + 1)
                for k in range(4):
                    for c0, n in SEGMENTS:
                        mm = eng.matmul(m.ps[i][:, c0:c0 + n], m.w[:, 4, 4 * i + k, :], y[:, k, c0:c0 + n],
                                        start=(k == 0), stop=(k == 3))
                mm.then_inc(done, 1)

        @block.scalar
        def _(eng):
            for i in range(3):
                eng.wait_ge(done, i + 1)
                eng.activation(g[:, i, :], m.ps[i][:, 0:T], ACT.Sigmoid).then_inc(gates, 1)

        @block.vector
        def _(eng):
            ch = Chain(eng, dve)
            eng.wait_ge(gates, 3)
            eng.wait_ge(done, 4)
            ch(eng.tensor_tensor(acc, g[:, 0, :], m.ps[3][:, 0:T], ALU.mult))
            eng.wait_ge(done, 5)
            ch(eng.tensor_tensor(part, g[:, 1, :], m.ps[0][:, 0:T], ALU.mult))
            ch(eng.tensor_tensor(acc, acc, part, ALU.add))
            eng.wait_ge(done, 6)
            ch(eng.tensor_tensor(part, g[:, 2, :], m.ps[1][:, 0:T], ALU.mult))
            ch(eng.tensor_tensor(merged[:, db, :], acc, part, ALU.add))
    st.close()


def stage_out(m, l, half):
    nc, d = m.nc, m.dram
    st = Stage(nc, "out")
    s = st.sem
    landed = [s(f"w{i}") for i in range(4)]
    done, dve = s("done"), s("dve")
    m.used = 0
    m.take(4, T), m.take(4, T)
    merged = m.take(KB, T)
    gt = m.take(4, 2)
    res = m.take(T)
    w = d["w_out"].rearrange("l (k p) (b c) -> l b p k c", p=P, c=P)
    with nc.Block() as block:
        @block.sync
        def _(eng):
            for i in range(4):
                eng.dma_start(m.w[:, i], w[l, half * 4 + i]).then_inc(landed[i], 16)

        @block.tensor
        def _(eng):
            for i in range(4):
                eng.wait_ge(landed[i], 16)
                project(eng, m, m.ps[i], i, merged).then_inc(done, 1)

        @block.vector
        def _(eng):
            ch = Chain(eng, dve)
            ch(eng.tensor_copy(gt, m.mod[:, GT1, bass.ds(half * 4, 4), :]))
            for i in range(4):
                eng.wait_ge(done, i + 1)
                for j, (c0, n) in enumerate(SEGMENTS):
                    ch(eng.tensor_scalar(res[:, c0:c0 + n], m.ps[i][:, c0:c0 + n], gt[:, i, j:j + 1], None, ALU.mult))
                ch(eng.tensor_tensor(m.x[:, half * 4 + i, :], m.x[:, half * 4 + i, :], res, ALU.add))
    st.close()

def stage_tokens_first(m, store=False):
    nc, d = m.nc, m.dram
    st = Stage(nc, "tok")
    turned, copied, stored = st.sem("turned"), st.sem("copied"), st.sem("stored")
    rows = m.ya[:, :, :].rearrange("p a b -> p (a b)").rearrange("p (t c) -> p t c", c=D)
    NT = TILES * KB // 4
    with nc.Block() as block:
        @block.tensor
        def _(eng):
            for n in range(NT):
                t, k0 = n // 2, 4 * (n % 2)
                if n >= 8:
                    eng.wait_ge(copied, n - 7)
                for j in range(4):
                    mm = eng.transpose(m.bank(n % 8)[:, P * j:P * j + P], m.h[:, k0 + j, P * t:P * t + P], m.ident[:, :])
                mm.then_inc(turned, 1)

        @block.vector
        def _(eng):
            for n in range(NT):
                t, k0 = n // 2, 4 * (n % 2)
                eng.wait_ge(turned, n + 1)
                eng.tensor_copy(rows[:, t, P * k0:P * k0 + 4 * P], m.bank(n % 8)).then_inc(copied, 1)

        if store:
            @block.sync
            def _(eng):
                eng.wait_ge(copied, 8)
                eng.dma_start(d["y_sample"][0].rearrange("(t p) c -> p t c", p=P), rows[:, 0:4, :]).then_inc(stored, 16)
                eng.wait_ge(copied, NT)
                eng.dma_start(d["y_prompt"][0], rows[:, 4, :]).then_inc(stored, 16)
                eng.wait_ge(stored, 32)
    st.close()


def top16(ch, vals, idx, src, spare):
    eng = ch.eng
    ch(eng.max(vals[:, 0:8], src))
    ch(eng.max_index(idx[:, 0:8], vals[:, 0:8], src))
    ch(eng.match_replace(spare, vals[:, 0:8], src, -3.4028235e38))
    ch(eng.max(vals[:, 8:16], spare))
    ch(eng.max_index(idx[:, 8:16], vals[:, 8:16], spare))


def peer_tables(m):
    m.used = 0
    return m.take(TILES, 2 * HEADS_Q, TOPK), m.take(TILES, 2 * HEADS_Q, TOPK)


def stage_scores(m, l, quarter):
    nc, d = m.nc, m.dram
    st = Stage(nc, "sc")
    s = st.sem
    landed = [s(f"w{i}") for i in range(4)]
    keys_in, q_done, k_done, q_out, s_done, s_out, dve, top_done = (
        s(n) for n in ("keys", "q_done", "k_turned", "q_out", "scored", "s_out", "dve", "tops"))
    top_v, top_i = peer_tables(m)
    keys, qt, kt, sc = m.take(4, P), m.take(2, T), m.take(2, P), m.take(2, TILES, P)
    vals, places = m.take(TILES, 4, TOPK), m.take(TILES, 4, TOPK).bitcast(U32)
    spare = m.take(P)
    wq = d["peer_wq"].rearrange("l (k p) (b c) -> l b p k c", p=P, c=P)
    pk = d["peer_keys"].rearrange("l h e n q -> l (h e) n q")

    def take(eng, i):
        eng.wait_ge(s_done, i + 1)
        if i >= 2:
            eng.wait_ge(top_done, i - 1)
        eng.activation(sc[:, i % 2].rearrange("p t n -> p (t n)"), m.ps[2 + i % 2][:, 0:T], ACT.Copy).then_inc(s_out, 1)

    with nc.Block() as block:
        @block.sync
        def _(eng):
            eng.dma_start(keys, pk[l, bass.ds(quarter * 4, 4)].rearrange("b n q -> n b q")).then_inc(keys_in, 16)
            for i in range(4):
                eng.dma_start(m.w[:, i], wq[l, quarter * 4 + i]).then_inc(landed[i], 16)

        @block.tensor
        def _(eng):
            eng.wait_ge(keys_in, 16)

            def score(i):
                eng.wait_ge(q_out, 2 * i + 2)
                if i >= 2:
                    eng.wait_ge(s_out, i - 1)
                for t in range(TILES):
                    mm = eng.matmul(m.ps[2 + i % 2][:, P * t:P * t + P], qt[:, i % 2, P * t:P * t + P],
                                    kt[:, i % 2, :], start=True, stop=True)
                mm.then_inc(s_done, 1)

            for i in range(4):
                eng.wait_ge(landed[i], 16)
                if i >= 2:
                    eng.wait_ge(q_out, 2 * i - 2)
                project(eng, m, m.ps[i % 2], i, m.h).then_inc(q_done, 1)
                eng.transpose(m.ps[i % 2][:, 768:768 + P], keys[:, i, :], m.ident[:, :]).then_inc(k_done, 1)
                if i >= 1:
                    score(i - 1)
            score(3)

        @block.scalar
        def _(eng):
            for i in range(4):
                eng.wait_ge(k_done, i + 1)
                if i >= 2:
                    eng.wait_ge(s_done, i - 1)
                eng.activation(qt[:, i % 2, :], m.ps[i % 2][:, 0:T], ACT.Copy).then_inc(q_out, 1)
                eng.activation(kt[:, i % 2, :], m.ps[i % 2][:, 768:768 + P], ACT.Copy).then_inc(q_out, 1)
                if i >= 1:
                    take(eng, i - 1)
            take(eng, 3)

        @block.vector
        def _(eng):
            ch = Chain(eng, dve)
            for i in range(4):
                eng.wait_ge(s_out, i + 1)
                for t in range(TILES):
                    top16(ch, vals[:, t, i], places[:, t, i], sc[:, i % 2, t], spare)
                eng.sem_inc(top_done, 1)
            ch(eng.tensor_copy(top_v[:, :, bass.ds(quarter * 4, 4), :], vals))
            ch(eng.tensor_copy(top_i[:, :, bass.ds(quarter * 4, 4), :], places))
    st.close()


def stage_select(m, t):
    nc = m.nc
    st = Stage(nc, "sel")
    s = st.sem
    dve, shifted, exped = s("dve"), s("shifted"), s("exponentials")
    top_v, top_i, idx, gate = select_tables(m)
    m.take(D)
    tv, ti = m.take(2 * HEADS_Q, TOPK), m.take(2 * HEADS_Q, TOPK)
    cand, hot = m.take(HEADS_Q, 256), m.take(HEADS_Q, TOPK, TOPK)
    spare, iota = m.take(256), m.take(TOPK)
    best, place = m.take(HEADS_Q, TOPK), m.take(HEADS_Q, TOPK).bitcast(U32)
    part = m.take(HEADS_Q, TOPK).bitcast(U32)
    pf, ex, e2 = m.take(HEADS_Q, TOPK), m.take(HEADS_Q, TOPK), m.take(HEADS_Q, TOPK)
    tot = m.take(HEADS_Q)
    full = [P, HEADS_Q, TOPK, TOPK]
    drawn = s("iota")
    with nc.Block() as block:
        @block.gpsimd
        def _(eng):
            eng.iota(iota.bitcast(mybir.dt.int32), pattern=[[1, TOPK]], base=0, channel_multiplier=0).then_inc(drawn, 1)

        @block.scalar
        def _(eng):
            eng.wait_ge(shifted, 1)
            eng.activation(ex, ex, ACT.Exp).then_inc(exped, 1)

        @block.vector
        def _(eng):
            ch = Chain(eng, dve)
            eng.wait_ge(drawn, 1)
            ch(eng.tensor_copy(spare[:, 0:TOPK], iota.bitcast(mybir.dt.int32)))
            ch(eng.tensor_copy(iota, spare[:, 0:TOPK]))
            ch(eng.tensor_copy(tv, top_v[:, t]))
            ch(eng.tensor_copy(ti, top_i[:, t]))
            for h in range(HEADS_Q):
                c = cand[:, h].rearrange("p (i j) -> p i j", j=TOPK)
                ch(eng.tensor_tensor(c, tv[:, 2 * h].unsqueeze(2).to_broadcast([P, TOPK, TOPK]),
                                     tv[:, 2 * h + 1].unsqueeze(1).to_broadcast([P, TOPK, TOPK]), ALU.add))
                top16(ch, best[:, h], place[:, h], cand[:, h], spare)
            ch(eng.tensor_tensor(ex, best, best[:, :, 0:1].to_broadcast([P, HEADS_Q, TOPK]), ALU.subtract))
            eng.sem_inc(shifted, 1)
            for half, (op, by) in enumerate(((ALU.logical_shift_right, 4), (ALU.bitwise_and, 15))):
                ch(eng.tensor_scalar(part, place, by, None, op))
                ch(eng.tensor_copy(pf, part))
                ch(eng.tensor_tensor(hot, pf.unsqueeze(3).to_broadcast(full),
                                     iota.unsqueeze(1).unsqueeze(1).to_broadcast(full), ALU.is_equal))
                keys = ti.rearrange("p (h e) k -> p h e k", e=2)[:, :, half].unsqueeze(2).to_broadcast(full)
                ch(eng.tensor_tensor(hot, hot, keys, ALU.mult))
                ch(eng.tensor_reduce((pf, e2)[half], hot, AX.X, ALU.add))
                if half == 0:
                    ch(eng.tensor_scalar(cand[:, 0, 0:P], pf.rearrange("p h k -> p (h k)"), float(KEYS), m.row0[:, 0:1],
                                         ALU.mult, ALU.add))
            ch(eng.tensor_tensor(cand[:, 0, 0:P], cand[:, 0, 0:P], e2.rearrange("p h k -> p (h k)"), ALU.add))
            ch(eng.tensor_copy(idx.bitcast(U32), cand[:, 0, 0:P]))
            eng.wait_ge(exped, 1)
            ch(eng.tensor_reduce(tot, ex, AX.X, ALU.add))
            ch(eng.reciprocal(tot, tot))
            ch(eng.tensor_tensor(gate.rearrange("p (h k) -> p h k", k=TOPK), ex,
                                 tot.unsqueeze(2).to_broadcast([P, HEADS_Q, TOPK]), ALU.mult))
    st.close()


def select_tables(m):
    return (*peer_tables(m), m.take(SLOTS), m.take(SLOTS))


def stage_retrieve(m, l, t):
    nc, d = m.nc, m.dram
    st = Stage(nc, "ret")
    s = st.sem
    UNROLL, SUB = 32, 4
    HALF = UNROLL // 2
    u_in, v_in = m.u_in, m.v_in
    before = (l * TILES + t) * (16 * SLOTS // RING)
    u_free, v_free, hid_done, gel_done, w_done, dg_done, staged, g_in = (
        s(n) for n in ("u_free", "v_free", "hid_done", "gelu_done", "weights_done", "diag_done", "staged", "gates_in"))
    dve, summed, sum_out, turned, started = s("dve"), s("summed"), s("sum_out"), s("turned"), s("started")
    prepared, asked = s("prepared"), s("asked")
    _, _, idx, gate = select_tables(m)
    hs = m.take(D)
    ub, vb, dg = m.take(RING, D), m.take(RING, D), m.take(RING, P)
    stage, hid, gel, wgt, g16 = (m.take(UNROLL) for _ in range(5))
    gt, zero = m.take(KB), m.take(P)
    ut = d["peer_u"].rearrange("l e c -> (l e) c")
    vt = d["peer_v"].rearrange("l e c -> (l e) c")
    rows = m.ya[:, :, :].rearrange("p a b -> p (a b)").rearrange("p (t c) -> p t c", c=D)

    def diag(eng, g, q):
        eng.wait_ge(w_done, g * (UNROLL // SUB) + (q + 1))
        for i in range(SUB * q, SUB * q + SUB):
            eng.wait_ge(v_free, g * UNROLL + (i + 1))
            eng.activation(dg[:, i % RING, :], m.ident[:, :], ACT.Copy, scale=wgt[:, i:i + 1]).then_inc(dg_done, 1)

    with nc.Block() as block:
        @block.gpsimd
        def _(eng):
            eng.wait_ge(prepared, 1)
            with eng.Fori(0, SLOTS // UNROLL) as g:
                for i in range(UNROLL):
                    r = i % RING
                    if i % HALF == 0:
                        eng.tensor_copy(stage.bitcast(U32)[:, i:i + HALF],
                                        idx.bitcast(U32)[:, bass.ds(g * UNROLL + i, HALF)]).then_inc(staged, 1)
                        eng.wait_ge(staged, g * 2 + (i // HALF + 1))
                    off = bass.IndirectOffsetOnAxis(ap=stage.bitcast(U32)[:, i:i + 1], axis=0)
                    eng.wait_ge(u_free, g * UNROLL + (i + 1))
                    eng.sem_inc(asked, 1)
                    eng.indirect_dma_start(ub[:, r, :], None, ut, off).then_inc(u_in[r], 16)
                    eng.wait_ge(v_free, g * UNROLL + (i + 1))
                    eng.sem_inc(asked, 1)
                    eng.indirect_dma_start(vb[:, r, :], None, vt, off).then_inc(v_in[r], 16)

        @block.vector
        def _(eng):
            ch = Chain(eng, dve)
            ch(eng.tensor_copy(hs, rows[:, t, :]))
            ch(eng.tensor_copy(gt, m.gate2[:, t, :]))
            ch(eng.memset(zero, 0.0))
            eng.sem_inc(prepared, 1)
            eng.sem_inc(started, 1)
            eng.sem_inc(u_free, RING)

            def weights(g, q):
                a = slice(SUB * q, SUB * q + SUB)
                eng.wait_ge(gel_done, g * (UNROLL // SUB) + (q + 1))
                eng.tensor_tensor(wgt[:, a], gel[:, a], g16[:, a], ALU.mult).then_inc(w_done, 1)

            with eng.Fori(0, SLOTS // UNROLL) as g:
                eng.tensor_copy(g16, gate[:, bass.ds(g * UNROLL, UNROLL)]).then_inc(g_in, 1)
                eng.wait_ge(g_in, g + 1)
                for i in range(UNROLL):
                    r = i % RING
                    eng.wait_ge(u_in[r], before + g * (16 * (UNROLL // RING)) + 16 * (i // RING + 1))
                    ins = eng.tensor_tensor_reduce(ub[:, r, :], ub[:, r, :], hs, 1.0, 0.0, ALU.mult, ALU.add,
                                                   hid[:, i:i + 1])
                    ins.then_inc(u_free, 1)
                    if i % SUB == SUB - 1:
                        q = i // SUB
                        eng.wait_ge(u_free, g * UNROLL + (RING + i + 1))
                        eng.sem_inc(hid_done, 1)
                        if q > 0:
                            weights(g, q - 1)
                weights(g, UNROLL // SUB - 1)
                eng.wait_ge(w_done, g * (UNROLL // SUB) + UNROLL // SUB)
            eng.wait_ge(summed, 1)
            for i in range(2):
                ch(eng.tensor_copy(hs[:, 512 * i:512 * i + 512], m.bank(i)))
            eng.sem_inc(sum_out, 1)
            eng.wait_ge(turned, 1)
            sums = ub[:, 0, :].rearrange("p (k c) -> p k c", c=P)
            ch(eng.tensor_tensor(sums, m.ps[1][:, :].rearrange("p (k c) -> p k c", c=P),
                                 gt.unsqueeze(2).to_broadcast([P, KB, P]), ALU.mult))
            xs = m.x[:, :, bass.ds(t * P, P)]
            ch(eng.tensor_tensor(xs, xs, sums, ALU.add))

        @block.scalar
        def _(eng):
            with eng.Fori(0, SLOTS // UNROLL) as g:
                for q in range(UNROLL // SUB):
                    a = slice(SUB * q, SUB * q + SUB)
                    eng.wait_ge(hid_done, g * (UNROLL // SUB) + (q + 1))
                    eng.activation(gel[:, a], hid[:, a], ACT.Gelu).then_inc(gel_done, 1)
                    if q > 0:
                        diag(eng, g, q - 1)
                diag(eng, g, UNROLL // SUB - 1)

        @block.tensor
        def _(eng):
            eng.wait_ge(started, 1)
            for i in range(2):
                mm = eng.matmul(m.bank(i), zero, hs[:, 512 * i:512 * i + 512], start=True, stop=False)
            mm.then_inc(v_free, RING)
            with eng.Fori(0, SLOTS // UNROLL) as g:
                for i in range(UNROLL):
                    r = i % RING
                    eng.wait_ge(v_in[r], before + g * (16 * (UNROLL // RING)) + 16 * (i // RING + 1))
                    eng.wait_ge(dg_done, g * UNROLL + (i + 1))
                    for j in range(2):
                        mm = eng.matmul(m.bank(j), dg[:, r, :], vb[:, r, 512 * j:512 * j + 512], start=False, stop=False)
                    mm.then_inc(v_free, 1)
            for i in range(2):
                mm = eng.matmul(m.bank(i), zero, hs[:, 512 * i:512 * i + 512], start=False, stop=True)
            mm.then_inc(summed, 1)
            eng.wait_ge(sum_out, 1)
            for k in range(KB):
                mm = eng.transpose(m.ps[1][:, P * k:P * k + P], hs[:, P * k:P * k + P], m.ident[:, :])
            mm.then_inc(turned, 1)
    st.close()

def program(nc, dram):
    with ExitStack() as ctx:
        m = Model(nc, ctx, dram)
        stage_constants(m)
        stage_load_x(m)
        with nc.Fori(0, LAYERS) as l:
            stage_params(m, l)
            stage_modulation(m, l)
            stage_norm(m, 0)
            stage_lowrank(m, l)
            with nc.Fori(0, KB) as hp:
                stage_rwkv(m, l, hp)
            stage_branches(m, l)
            with nc.Fori(0, KB) as db:
                stage_merge(m, l, db)
            with nc.Fori(0, 2) as half:
                stage_out(m, l, half)
            stage_norm(m, 1)
            stage_tokens_first(m)
            with nc.Fori(0, 4) as quarter:
                stage_scores(m, l, quarter)
            with nc.Fori(0, TILES) as t:
                stage_select(m, t)
                stage_retrieve(m, l, t)
        stage_norm(m, 2)
        stage_tokens_first(m, store=True)


_OUTS = [("y_prompt", (1, CTX, D)), ("y_sample", (1, LAT, D)), ("new_state", (1, LAYERS, 2, 16, HD, HD))]


def kernel(**inputs):
    import numpy as np
    import concourse.bacc as bacc
    from concourse.bass_utils import run_bass_kernel_spmd

    nc = bacc.Bacc("TRN2", target_bir_lowering=False, num_devices=1)
    arrays, dram = {}, {}
    for name, value in inputs.items():
        a = np.ascontiguousarray(value)
        arrays[name] = a
        dram[name] = nc.dram_tensor(name, a.shape, mybir.dt.from_np(a.dtype), kind="ExternalInput").ap()
    for name, shape in _OUTS:
        dram[name] = nc.dram_tensor(name, shape, F32, kind="ExternalOutput").ap()
    program(nc, dram)
    r = run_bass_kernel_spmd(nc, [arrays], core_ids=[0])
    return tuple(r.results[0][name] for name, _ in _OUTS)
```

```python
from contextlib import ExitStack

import concourse.bass as bass
from concourse import mybir

F32 = mybir.dt.float32
U32 = mybir.dt.uint32
ALU = mybir.AluOpType
ACT = mybir.ActivationFunctionType
AX = mybir.AxisListType

P = 128
D = 1024
KB = D // P
LAT, CTX = 512, 128
T = LAT + CTX
TILES = T // P
LAYERS = 2
HD = 64
CH = 64
NCH, NLAT, NCTX = T // CH, LAT // CH, CTX // CH
GRID_W = 64
ROWS = LAT // GRID_W
TAPS = 31
HEADS_Q, KEYS, TOPK, EXPERTS = 8, 128, 16, 16384
SLOTS = HEADS_Q * TOPK
EPS, GN_EPS, LN_EPS = 1e-6, 64e-5, 1e-5
DECAY = 0.6065306597126334
B_R, B_K, B_V, B_LO, B_POOL, B_CONV, B_GATE = 0, 8, 16, 24, 27, 31, 39
R_ADA, R_MU, R_W0, R_A0, R_KK, R_KA = 0, 48, 75, 91, 107, 115
R_N1, R_N2, R_RK, R_GNG, R_GNB, R_PB, R_PS, R_CB, R_LG, R_LB, R_C, R_CC, R_FG = 0, 8, 16, 24, 32, 40, 44, 48, 52, 56, 60, 68, 76
SH1, SC1, GT1, SH2, SC2, GT2 = range(6)
SEGMENTS = ((0, LAT), (LAT, CTX))
WRING = 5
RING = 8
GROUPS = ((0, 4), (4, 4), (8, 2))


class Chain:

    def __init__(self, eng, sem):
        self.eng, self.sem, self.n = eng, sem, 0

    def __call__(self, ins):
        self.n += 1
        ins.then_inc(self.sem, 1)
        self.eng.wait_ge(self.sem, self.n)


class Stage:

    def __init__(self, nc, name):
        self.nc, self.name, self.ctx, self.nums = nc, name, ExitStack(), []

    def sem(self, name):
        s = self.ctx.enter_context(self.nc.semaphore(f"{self.name}_{name}"))
        self.nums.append(s.num)
        return s

    def close(self):
        self.nc.all_engine_barrier()
        nums = sorted(self.nums)
        runs = [n for n in nums if n - 1 not in nums]
        for n in runs:
            end = n
            while end in nums:
                end += 1
            self.nc.gpsimd.sem_clear(range(n, end))
        self.nc.all_engine_barrier()
        self.ctx.close()


class Model:

    def __init__(self, nc, ctx, dram):
        self.nc, self.dram = nc, dram

        def sb(name, shape, dt=F32):
            return ctx.enter_context(nc.sbuf_tensor(name, shape, dt))

        self.x = sb("x", [P, KB, T])
        self.h = sb("h", [P, KB, T])
        self.ya = sb("ya", [P, KB, T])
        self.lo = sb("lo", [P, 3, T])
        self.w = sb("w", [P, WRING, KB, P])
        self.par = sb("par", [P, 3, P])
        self.mod = sb("mod", [P, 6, KB, 2])
        self.scale = sb("scale", [P, 2, KB, 2])
        self.silu_c = sb("silu_c", [P, KB, 2])
        self.ident = sb("ident", [P, P])
        self.ones = sb("ones", [P, P])
        self.block = sb("block", [P, 7, P])
        self.level = sb("level", [P, 6, P])
        self.tri = sb("tri", [P, 2, P])
        self.tri1 = sb("tri1", [P, 2, P])
        self.trid = sb("trid", [P, 2, CH])
        self.reset = sb("reset", [P, NCH, CH])
        self.eps = sb("eps", [P, 4])
        self.row0 = sb("row0", [P, 1])
        self.gate2 = sb("gate2", [P, TILES, KB])
        self.arena = sb("arena", [P, 27008])
        self.used = 0
        self.u_in = [ctx.enter_context(nc.semaphore(f"u_landed{i}")) for i in range(RING)]
        self.v_in = [ctx.enter_context(nc.semaphore(f"v_landed{i}")) for i in range(RING)]
        self.ps = [ctx.enter_context(nc.psum_tensor(f"ps{i}", [P, 1024], F32)) for i in range(4)]
        self.w_in = dram["w_in"].rearrange("l (k p) (b c) -> l b p k c", p=P, c=P)

    def bank(self, n):
        return self.ps[n // 2][:, 512 * (n % 2):512 * (n % 2) + 512]

    def take(self, *shape):
        n = 1
        for s in shape:
            n *= s
        a = self.arena[:, self.used:self.used + n]
        self.used += n
        assert self.used <= self.arena.shape[1], self.used
        if len(shape) == 2:
            a = a.rearrange("p (a b) -> p a b", b=shape[1])
        if len(shape) == 3:
            a = a.rearrange("p (a b c) -> p a b c", b=shape[1], c=shape[2])
        return a


def stage_constants(m):
    nc = m.nc
    st = Stage(nc, "const")
    pool, dve, ready = st.sem("pool"), st.sem("dve"), st.sem("blocks_ready")
    with nc.Block() as block:
        @block.gpsimd
        def _(eng):
            ch = Chain(eng, pool)
            ch(eng.memset(m.ones[:, :], 1.0))
            ch(eng.memset(m.block[:, :, :], 1.0))
            for i in range(7):
                b = 1 << i
                v = m.block[:, i, :].rearrange("p (n b) -> p n b", b=b)
                ch(eng.affine_select(out=v, in_=v, compare_op=ALU.is_ge, fill=0.0, base=0,
                                     pattern=[[-b, P // b], [0, b]], channel_multiplier=1))
                ch(eng.affine_select(out=v, in_=v, compare_op=ALU.is_ge, fill=0.0, base=b - 1,
                                     pattern=[[b, P // b], [0, b]], channel_multiplier=-1))
            ch(eng.tensor_copy(m.ident[:, :], m.block[:, 0, :]))
            for i in range(2):
                ch(eng.tensor_copy(m.tri[:, i, :], m.block[:, 6, :]))
            ch(eng.affine_select(out=m.tri[:, 0, :], in_=m.tri[:, 0, :], compare_op=ALU.is_ge, fill=0.0,
                                 base=-1, pattern=[[1, P]], channel_multiplier=-1))
            ch(eng.affine_select(out=m.tri[:, 1, :], in_=m.tri[:, 1, :], compare_op=ALU.is_ge, fill=0.0,
                                 base=-1, pattern=[[-1, P]], channel_multiplier=1))
            ch(eng.memset(m.reset[:, :, :], 1.0))
            ch(eng.memset(m.reset[:, :, 0:1], 0.0))
            for i, e in enumerate((EPS, GN_EPS, LN_EPS)):
                ch(eng.memset(m.eps[:, i:i + 1], e))
            ch(eng.memset(m.row0[:, :], -float(EXPERTS)))
            eng.sem_inc(ready, 1)

        @block.vector
        def _(eng):
            ch = Chain(eng, dve)
            eng.wait_ge(ready, 1)
            for i in range(6):
                ch(eng.tensor_tensor(m.level[:, i, :], m.block[:, i + 1, :], m.block[:, i, :], ALU.subtract))
            for i in range(2):
                ch(eng.tensor_tensor(m.tri1[:, i, :], m.tri[:, 1 - i, :], m.level[:, 0, :], ALU.mult))
                ch(eng.tensor_tensor(m.trid[:, i, :], m.tri[:, i, 0:CH], m.tri[:, i, CH:P], ALU.add))
                ch(eng.tensor_tensor(m.trid[:, i, :], m.trid[:, i, :], m.ident[:, 0:CH], ALU.add))
                ch(eng.tensor_tensor(m.trid[:, i, :], m.trid[:, i, :], m.ident[:, CH:P], ALU.add))
    st.close()


def stage_load_x(m):
    nc, d = m.nc, m.dram
    st = Stage(nc, "load")
    landed, turned, copied = st.sem("landed"), st.sem("turned"), st.sem("copied")
    m.used = 0
    xt = m.take(TILES, D)
    with nc.Block() as block:
        @block.sync
        def _(eng):
            eng.dma_start(xt[:, 0:4, :], d["x_sample"][0].rearrange("(t p) c -> p t c", p=P)).then_inc(landed, 16)
            eng.dma_start(xt[:, 4, :], d["x_prompt"][0]).then_inc(landed, 16)

        @block.tensor
        def _(eng):
            eng.wait_ge(landed, 32)
            for n in range(TILES * KB // 4):
                t, k0 = n // 2, 4 * (n % 2)
                if n >= 8:
                    eng.wait_ge(copied, n - 7)
                for j in range(4):
                    mm = eng.transpose(m.bank(n % 8)[:, P * j:P * j + P], xt[:, t, P * (k0 + j):P * (k0 + j) + P],
                                       m.ident[:, :])
                mm.then_inc(turned, 1)

        @block.vector
        def _(eng):
            for n in range(TILES * KB // 4):
                t, k0 = n // 2, 4 * (n % 2)
                eng.wait_ge(turned, n + 1)
                eng.tensor_copy(m.x[:, k0:k0 + 4, P * t:P * t + P],
                                m.bank(n % 8).rearrange("p (a b) -> p a b", b=P)).then_inc(copied, 1)
    st.close()


def stage_params(m, l):
    nc, d = m.nc, m.dram
    st = Stage(nc, "par")
    landed, turned, copied, sig, dve = (st.sem(n) for n in ("landed", "turned", "copied", "sigmoid", "dve"))
    m.used = 0
    rows = m.take(3, P)
    t1 = m.take(KB, 2)

    def vec(name):
        a = d[name][l]
        if len(a.shape) == 1:
            return a.rearrange("(b c) -> b c", c=P)
        if name == "r_k":
            return a.rearrange("h k -> (h k)").rearrange("(b c) -> b c", c=P)
        return a.rearrange("a (b c) -> (a b) c", c=P)

    loads = [(0, R_ADA, vec("ada_b")), (0, R_MU, vec("shift_mu")), (0, R_W0, vec("decay_w0")),
             (0, R_A0, vec("iclr_a0")), (0, R_KK, vec("k_k")), (0, R_KA, vec("k_a")),
             (1, R_N1, vec("norm1_g")), (1, R_N2, vec("norm2_g")), (1, R_RK, vec("r_k")), (1, R_GNG, vec("gn_g")),
             (1, R_GNB, vec("gn_b")), (1, R_PB, vec("pool_b")), (1, R_PS, vec("pool_scale")),
             (1, R_CB, vec("conv_b")), (1, R_LG, vec("cln_g")), (1, R_LB, vec("cln_b")),
             (1, R_C, d["c"].rearrange("a (b c) -> (a b) c", c=P)),
             (1, R_CC, d["c_ctx"].rearrange("(b c) -> b c", c=P)),
             (1, R_FG, d["final_g"].rearrange("(b c) -> b c", c=P)),
             (2, 0, vec("conv_w"))]
    sizes = (R_KA + KB, R_FG + KB, TAPS * 4)
    with nc.Block() as block:
        @block.sync
        def _(eng):
            for tile, r, src in loads:
                eng.dma_start(rows[r:r + src.shape[0], tile, :], src).then_inc(landed, 16)

        @block.tensor
        def _(eng):
            eng.wait_ge(landed, 16 * len(loads))
            for i, n in enumerate(sizes):
                mm = eng.transpose(m.bank(0)[:, P * i:P * i + n], rows[0:n, i, :], m.ident[0:n, 0:n])
            mm.then_inc(turned, 1)

        @block.scalar
        def _(eng):
            eng.wait_ge(copied, 1)
            for i, r in enumerate((R_C, R_CC)):
                eng.activation(t1[:, :, i], m.par[:, 1, r:r + KB], ACT.Sigmoid).then_inc(sig, 1)

        @block.vector
        def _(eng):
            ch = Chain(eng, dve)
            eng.wait_ge(turned, 1)
            for i, n in enumerate(sizes):
                ch(eng.tensor_copy(m.par[:, i, 0:n], m.bank(0)[:, P * i:P * i + n]))
            eng.sem_inc(copied, 1)
            eng.wait_ge(sig, 2)
            for i, r in enumerate((R_C, R_CC)):
                ch(eng.tensor_tensor(m.silu_c[:, :, i], t1[:, :, i], m.par[:, 1, r:r + KB], ALU.mult))
    st.close()


def stage_modulation(m, l):
    nc = m.nc
    ada = m.dram["ada_w"].rearrange("l (k p) (s b c) -> l s b p k c", p=P, b=KB, c=P)
    with nc.Fori(0, 6) as s:
        st = Stage(nc, "mod")
        landed = [st.sem(f"w{i}") for i in range(WRING)]
        used, done, dve = st.sem("used"), st.sem("done"), st.sem("dve")
        m.used = 0
        bias = m.take(KB)
        with nc.Block() as block:
            @block.sync
            def _(eng):
                for b in range(KB):
                    if b >= WRING:
                        eng.wait_ge(used, b - WRING + 1)
                    eng.dma_start(m.w[:, b % WRING], ada[l, s, b]).then_inc(landed[b % WRING], 16)

            @block.tensor
            def _(eng):
                for b in range(KB):
                    eng.wait_ge(landed[b % WRING], 16 * (b // WRING + 1))
                    for k in range(KB):
                        mm = eng.matmul(m.bank(0)[:, 2 * b:2 * b + 2], m.w[:, b % WRING, k, :], m.silu_c[:, k, :],
                                        start=(k == 0), stop=(k == KB - 1))
                    mm.then_inc(used, 1)

            @block.vector
            def _(eng):
                ch = Chain(eng, dve)
                ch(eng.tensor_copy(bias, m.par[:, 0, 0:48].rearrange("p (s b) -> p s b", b=KB)[:, s, :]))
                eng.wait_ge(used, KB)
                ch(eng.tensor_tensor(m.mod[:, s, :, :], m.bank(0)[:, 0:2 * KB].rearrange("p (b c) -> p b c", c=2),
                                     bias.unsqueeze(2).to_broadcast([P, KB, 2]), ALU.add))
        st.close()
    st = Stage(nc, "scl")
    dve = st.sem("dve")
    with nc.Block() as block:
        @block.vector
        def _(eng):
            ch = Chain(eng, dve)
            for i, (sec, r) in enumerate(((SC1, R_N1), (SC2, R_N2))):
                gain = m.par[:, 1, r:r + KB].unsqueeze(2).to_broadcast([P, KB, 2])
                ch(eng.tensor_scalar(m.scale[:, i], m.mod[:, sec], 1.0, None, ALU.add))
                ch(eng.tensor_tensor(m.scale[:, i], m.scale[:, i], gain, ALU.mult))
            ch(eng.tensor_scalar(m.row0[:, :], m.row0[:, :], float(EXPERTS), None, ALU.add))
            for t in range(TILES):
                ch(eng.tensor_copy(m.gate2[:, t, :], m.mod[:, GT2, :, int(t >= LAT // P)]))
    st.close()


def stage_norm(m, which):
    nc = m.nc
    st = Stage(nc, "norm")
    squared, summed, rooted, scaled = (st.sem(n) for n in ("squared", "summed", "rooted", "scaled"))
    dve = st.sem("dve")
    m.used = 0
    sq, root = m.take(KB, T), m.take(T)
    with nc.Block() as block:
        @block.scalar
        def _(eng):
            for k in range(KB):
                eng.activation(sq[:, k, :], m.x[:, k, :], ACT.Square).then_inc(squared, 1)
            eng.wait_ge(summed, 1)
            eng.activation(root[:, :], m.ps[0][:, 0:T], ACT.Sqrt, scale=1.0 / D, bias=m.eps[:, 0:1])\
               .then_inc(rooted, 1)
            for k in range(KB):
                eng.wait_ge(scaled, k + 1)
                if which == 2:
                    eng.activation(m.h[:, k, :], sq[:, k, :], ACT.Copy, scale=m.par[:, 1, R_FG + k:R_FG + k + 1])
                    continue
                for i, (c0, n) in enumerate(SEGMENTS):
                    eng.activation(m.h[:, k, c0:c0 + n], sq[:, k, c0:c0 + n], ACT.Identity,
                                   scale=m.scale[:, which, k, i:i + 1],
                                   bias=m.mod[:, (SH1, SH2)[which], k, i:i + 1])

        @block.tensor
        def _(eng):
            for k in range(KB):
                eng.wait_ge(squared, k + 1)
                for c0, n in SEGMENTS:
                    mm = eng.matmul(m.ps[0][:, c0:c0 + n], m.ones[:, :], sq[:, k, c0:c0 + n],
                                    start=(k == 0), stop=(k == KB - 1))
            mm.then_inc(summed, 1)

        @block.vector
        def _(eng):
            ch = Chain(eng, dve)
            eng.wait_ge(rooted, 1)
            ch(eng.reciprocal(root[:, :], root[:, :]))
            for k in range(KB):
                eng.tensor_tensor(sq[:, k, :], m.x[:, k, :], root[:, :], ALU.mult).then_inc(scaled, 1)
    st.close()

def shift_mix(m, ch, pad, tmp, mu, dst):
    eng = ch.eng
    n = T + 2
    ch(eng.tensor_tensor(tmp, pad[:, 0:n], pad[:, 2:n + 2], ALU.add))
    ch(eng.scalar_tensor_tensor(out=tmp, in0=tmp, scalar=0.5, in1=pad[:, 1:n + 1],
                                op0=ALU.mult, op1=ALU.subtract))
    for c0, w, off in ((0, LAT, 0), (LAT, CTX, 2)):
        ch(eng.scalar_tensor_tensor(out=dst[:, c0:c0 + w], in0=tmp[:, c0 + off:c0 + off + w], scalar=mu,
                                    in1=pad[:, c0 + off + 1:c0 + off + 1 + w], op0=ALU.mult, op1=ALU.add))


def pad_edges(eng, pad):
    return [eng.memset(pad[:, 0:1], 0.0), eng.memset(pad[:, LAT + 1:LAT + 3], 0.0),
            eng.memset(pad[:, T + 3:T + 4], 0.0)]


def project(eng, m, psum, slot, src):
    for k in range(KB):
        for c0, n in SEGMENTS:
            mm = eng.matmul(psum[:, c0:c0 + n], m.w[:, slot, k, :], src[:, k, c0:c0 + n],
                            start=(k == 0), stop=(k == KB - 1))
    return mm


def stage_lowrank(m, l):
    nc = m.nc
    st = Stage(nc, "lo")
    landed = [st.sem(f"w{i}") for i in range(3)]
    edges, projected, padded, mixed, dve = (st.sem(n) for n in ("edges", "projected", "padded", "mixed", "dve"))
    m.used = 0
    pad, tmp, mix = m.take(3, T + 4), m.take(T + 2), m.take(3, T)
    with nc.Block() as block:
        @block.sync
        def _(eng):
            for i in range(3):
                eng.dma_start(m.w[:, i], m.w_in[l, B_LO + i]).then_inc(landed[i], 16)

        @block.tensor
        def _(eng):
            for i in range(3):
                eng.wait_ge(landed[i], 16)
                project(eng, m, m.ps[i], i, m.h).then_inc(projected, 1)

        @block.scalar
        def _(eng):
            for i in range(3):
                eng.wait_ge(projected, i + 1)
                for c0, n, off in ((0, LAT, 1), (LAT, CTX, 3)):
                    eng.activation(pad[:, i, c0 + off:c0 + off + n], m.ps[i][:, c0:c0 + n], ACT.Copy)\
                       .then_inc(padded, 1)
            for i, f in enumerate((ACT.Tanh, ACT.Copy, ACT.Sigmoid)):
                eng.wait_ge(mixed, i + 1)
                eng.activation(m.lo[:, i, :], mix[:, i, :], f)

        @block.vector
        def _(eng):
            ch = Chain(eng, dve)
            for i in range(3):
                for ins in pad_edges(eng, pad[:, i]):
                    ch(ins)
                eng.wait_ge(padded, 2 * i + 2)
                mu = m.par[:, 0, R_MU + B_LO + i:R_MU + B_LO + i + 1]
                shift_mix(m, ch, pad[:, i], tmp, mu, mix[:, i])
                eng.sem_inc(mixed, 1)
    st.close()


def stage_rwkv(m, l, hp):
    nc, d = m.nc, m.dram
    st = Stage(nc, "rwkv")
    s = st.sem
    w_land = [s(f"w{i}") for i in range(3)]
    small, projected, padded, nrm, ss_done, rooted, act = (
        s(n) for n in ("small", "projected", "padded", "kk_squared", "kk_summed", "kk_rooted", "act"))
    dve, pool, mixed, zeroed = s("dve"), s("pool"), s("mixed"), s("zeroed")
    g_done, za, sg, qe, exps = s("g_done"), s("za"), s("sigmoids"), s("qe"), s("exps")
    vbd_ready, bd_ready = s("v_ready"), s("operands_ready")
    t_dve, t_act, t_done = s("products_out_dve"), s("products_out_act"), s("products_done")
    d1, lx, lxe, ld_, lde, lte = s("inverse_start"), s("x_done"), s("x_out"), s("dd_done"), s("d_out"), s("dt_out")
    p_done, p_act, p_dve = s("post_done"), s("post_out_act"), s("post_out_dve")
    s_in, s_turned, s_set = s("state_in"), s("state_turned"), s("state_set")
    s_done, s_out, y_done, y_out = s("s_done"), s("s_out"), s("y_done"), s("y_out")
    f_turned, f_out, stored = s("final_turned"), s("final_out"), s("final_stored")
    gsum, yc_ready, gsq, groot = s("y_summed"), s("y_centred"), s("y_squared"), s("gn_rooted")
    q_ready = s("bonus_ready")

    m.used = 0
    par = m.take(13)
    wc = m.take(2, NCH)
    pad, tmp = m.take(T + 4), m.take(T + 2)
    r, k, v, nkk = (m.take(T) for _ in range(4))
    sig, q, e, a = (m.take(T) for _ in range(4))
    x1, x2, x3 = (m.take(T) for _ in range(3))
    free_w = m.w[:, 3:5].rearrange("p s k c -> p (s k c)")
    kds, ys, gate = (free_w[:, T * i:T * i + T] for i in range(3))
    ws = m.take(3, P)
    a_bd, b_bd, k_bd, v_bd = (m.take(NCH, P) for _ in range(4))
    rt = m.take(NCH, CH)
    a_tok, b_tok, k_tok, v_tok = (m.take(NCH, P) for _ in range(4))
    akt, dd, dt, abt = (m.take(NCH, P) for _ in range(4))
    rbt, rkt = m.take(NCH, CH), m.take(NCH, CH)
    s_raw = m.take(3, P)
    xx = v_bd
    yy, cc, gg, states = dd, akt, xx, abt
    chunks = lambda t: t.rearrange("p (c t) -> p c t", t=CH)
    w2 = d["decay_w2"].rearrange("l e r (b c) -> l b (e r) c", c=P)
    a2 = d["iclr_a2"].rearrange("l e r (b c) -> l b (e r) c", c=P)
    g2 = d["gate_g2"].rearrange("l r (b c) -> l b r c", c=P)
    heads = ((0, CH), (CH, P))
    BY_DVE = {"abt", "ab", "akt", "rbt", "rkt"}
    TURNED = {"a_tok": (a_bd, a_tok), "b_tok": (b_bd, b_tok), "k_tok": (k_bd, k_tok), "v_tok": (v_bd, v_tok)}

    def products(e_):
        names = ("abt", "ab", "akt") + (("v_tok",) if e_ == 0 else ()) + ("a_tok", "b_tok", "k_tok", "rbt", "rkt", "akv")
        return [(w, g) for w in names for g in range(3)]

    def out_count(e_, n, by_dve):
        return sum((w in BY_DVE) == by_dve for i in range(e_) for w, _ in products(i)) + \
            sum((w in BY_DVE) == by_dve for w, _ in products(e_)[:n])

    def done_count(e_):
        return sum(len(products(i)) for i in range(e_))

    steps = [(i, c) for i in range(NLAT) for c in ((0, 1) if i < NCTX else (0,))]
    updates = [x for x in steps if x != (NLAT - 1, 0)]
    NS = len(updates)

    def chunk_of(e_, i, c):
        n, base = ((NLAT, 0), (NCTX, NLAT))[c]
        return base + (i if e_ == 0 else n - 1 - i)

    def state_after(e_, i, c):
        return s_raw[:, 2, :] if (i, c) == (NCTX - 1, 1) else states[:, chunk_of(e_, i + 1, c), :]

    def cols(bank, w, n=P):
        return bank[:, 0:n * w].rearrange("p (c t) -> p c t", t=n)

    def over(mask, w, n=P):
        return mask.unsqueeze(1).to_broadcast([P, w, n])

    def pre_a(eng, ch, e_):
        eng.wait_ge(sg, 2 * e_ + 1)
        ch(eng.tensor_tensor_scan(q, m.reset[:, :, :].rearrange("p c t -> p (c t)"), sig, 0.0, ALU.mult, ALU.add))
        if e_ == 1:
            ch(eng.tensor_tensor(chunks(e), chunks(q)[:, :, CH - 1:CH].to_broadcast([P, NCH, CH]), chunks(q),
                                 ALU.subtract))
            ch(eng.tensor_tensor(q, e, sig, ALU.add))
        else:
            ch(eng.tensor_tensor(e, q, sig, ALU.subtract))
        eng.sem_inc(qe, 1)

    def pre_b(eng, ch, e_):
        eng.wait_ge(sg, 2 * e_ + 2)
        ch(eng.tensor_tensor(sig, nkk, a, ALU.mult))
        ch(eng.tensor_scalar(a, a, par[:, 8:9], par[:, 9:10], ALU.mult, ALU.add))
        ch(eng.tensor_tensor(a, a, k, ALU.mult))
        if e_ == 0:
            ch(eng.tensor_copy(kds, a))
        else:
            ch(eng.tensor_tensor(kds, kds, a, ALU.add))

    def pre_c(eng, ch, e_):
        eng.wait_ge(exps, 3 * (e_ + 1))
        end = CH - 1 if e_ == 0 else 0
        ch(eng.tensor_copy(wc[:, e_].unsqueeze(2), chunks(x1)[:, :, end:end + 1]))
        for p0, p1 in heads:
            ch(eng.tensor_tensor(a_bd[p0:p1, :, p0:p1], chunks(nkk)[p0:p1], chunks(x2)[p0:p1], ALU.mult))

    def pre_d(eng, ch, e_):
        for p0, p1 in heads:
            ch(eng.scalar_tensor_tensor(out=b_bd[p0:p1, :, p0:p1], in0=chunks(sig)[p0:p1], scalar=-1.0,
                                        in1=chunks(x3)[p0:p1], op0=ALU.mult, op1=ALU.mult))
            ch(eng.tensor_tensor(k_bd[p0:p1, :, p0:p1], chunks(a)[p0:p1], chunks(x3)[p0:p1], ALU.mult))

    def pre_e(eng, ch, e_):
        ch(eng.tensor_tensor(rt.rearrange("p c t -> p (c t)"), r, x1, ALU.mult))
        eng.sem_inc(bd_ready, 1)

    def za_product(eng, e_, i):
        h0 = CH * e_
        for c0, n in SEGMENTS:
            mm = eng.matmul(m.ps[3][:, c0:c0 + n], ws[h0:h0 + CH, i, :], m.lo[h0:h0 + CH, i, c0:c0 + n],
                            start=True, stop=True)
        mm.then_inc(za, 1)

    def act_sigmoid(eng, e_, i):
        eng.wait_ge(za, 2 * e_ + i + 1)
        eng.activation((sig, a)[i], m.ps[3][:, 0:T], ACT.Sigmoid, bias=par[:, 3 + 2 * i + e_:4 + 2 * i + e_])\
           .then_inc(sg, 1)

    def act_exps(eng, e_):
        eng.wait_ge(qe, e_ + 1)
        eng.activation(x2, e, ACT.Exp, scale=-DECAY).then_inc(exps, 1)
        eng.activation(x3, q, ACT.Exp, scale=DECAY).then_inc(exps, 1)
        eng.activation(x1, q, ACT.Exp, scale=-DECAY).then_inc(exps, 1)

    with nc.Block() as block:
        @block.sync
        def _(eng):
            for i, b in enumerate((B_K, B_R, B_V)):
                eng.dma_start(m.w[:, i], m.w_in[l, hp + b]).then_inc(w_land[i], 16)
            for i, t in enumerate((w2, a2, g2)):
                eng.dma_start(ws[:, i, :], t[l, hp]).then_inc(small, 16)
            eng.wait_ge(zeroed, 1)
            for e_ in range(2):
                if e_ == 1:
                    eng.wait_ge(s_set, 1)
                for i, (p0, p1) in enumerate(heads):
                    src = d["state_rwkv"][0].rearrange("l e (b i) v k -> l e i b v k", i=2)[l, e_, i, hp]
                    eng.dma_start(s_raw[p0:p1, 0, p0:p1], src).then_inc(s_in, 16)
            out = d["new_state"][0].rearrange("l e (b i) v k -> l e i b v k", i=2)
            for e_ in range(2):
                eng.wait_ge(f_out, e_ + 1)
                for i, (p0, p1) in enumerate(heads):
                    eng.dma_start(out[l, e_, i, hp], s_raw[p0:p1, 1, p0:p1]).then_inc(stored, 16)
                eng.wait_ge(stored, 32 * (e_ + 1))

        @block.gpsimd
        def _(eng):
            ch = Chain(eng, pool)
            for t in (a_bd, b_bd, k_bd, v_bd, s_raw):
                ch(eng.memset(t[0:CH, :, CH:P], 0.0))
                ch(eng.memset(t[CH:P, :, 0:CH], 0.0))
            eng.sem_inc(zeroed, 1)

        @block.tensor
        def _(eng):
            for i in range(2):
                eng.wait_ge(w_land[i], 16)
                project(eng, m, m.ps[i], i, m.h).then_inc(projected, 1)
            eng.wait_ge(small, 48)
            za_product(eng, 0, 0)
            eng.wait_ge(w_land[2], 16)
            project(eng, m, m.ps[2], 2, m.h).then_inc(projected, 1)
            eng.wait_ge(sg, 1)
            za_product(eng, 0, 1)
            eng.wait_ge(nrm, 1)
            for c0, n in SEGMENTS:
                mm = eng.matmul(m.ps[0][:, c0:c0 + n], m.block[:, 6, :], x1[:, c0:c0 + n], start=True, stop=True)
            mm.then_inc(ss_done, 1)
            eng.wait_ge(sg, 2)
            for c0, n in SEGMENTS:
                mm = eng.matmul(m.ps[3][:, c0:c0 + n], ws[:, 2, :], m.lo[:, 2, c0:c0 + n], start=True, stop=True)
            mm.then_inc(g_done, 1)
            eng.wait_ge(padded, 6)
            for e_ in range(2):
                eng.wait_ge(bd_ready, e_ + 1)
                if e_ == 0:
                    eng.wait_ge(vbd_ready, 1)
                    eng.wait_ge(rooted, 2)
                else:
                    eng.wait_ge(f_out, 1)
                    eng.wait_ge(y_out, 1)
                for n, (what, g) in enumerate(products(e_)):
                    if n >= 8:
                        eng.wait_ge(t_dve, out_count(e_, n - 7, True))
                        eng.wait_ge(t_act, out_count(e_, n - 7, False))
                    c0, w = GROUPS[g]
                    for j in range(w):
                        c = c0 + j
                        if what in ("rbt", "rkt"):
                            mm = eng.matmul(m.bank(n % 8)[:, CH * j:CH * j + CH], (b_bd if what == "rbt" else k_bd)[:, c, :],
                                            rt[:, c, :], start=True, stop=True)
                            continue
                        o = m.bank(n % 8)[:, P * j:P * j + P]
                        if what == "abt":
                            mm = eng.matmul(o, b_bd[:, c, :], a_bd[:, c, :], start=True, stop=True)
                        elif what == "ab":
                            mm = eng.matmul(o, a_bd[:, c, :], b_bd[:, c, :], start=True, stop=True)
                        elif what == "akt":
                            mm = eng.matmul(o, k_bd[:, c, :], a_bd[:, c, :], start=True, stop=True)
                        elif what == "akv":
                            mm = eng.matmul(o, akt[:, c, :], v_tok[:, c, :], start=True, stop=True)
                        else:
                            mm = eng.transpose(o, TURNED[what][0][:, c, :], m.ident[:, :])
                    mm.then_inc(t_done, 1)
                eng.wait_ge(d1, e_ + 1)
                eng.wait_ge(t_dve, out_count(e_ + 1, 0, True))
                eng.wait_ge(t_act, out_count(e_ + 1, 0, False))
                for lv in range(5):
                    n0 = 15 * e_ + 3 * lv
                    for g, (c0, w) in enumerate(GROUPS):
                        if lv > 0:
                            eng.wait_ge(lde, 12 * e_ + 3 * (lv - 1) + g + 1)
                            eng.wait_ge(lte, n0 - 3 + g + 1)
                        for j in range(w):
                            mm = eng.matmul(m.bank(g)[:, P * j:P * j + P], abt[:, c0 + j, :], dd[:, c0 + j, :],
                                            start=True, stop=True)
                        mm.then_inc(lx, 1)
                    for g, (c0, w) in enumerate(GROUPS):
                        eng.wait_ge(lxe, n0 + g + 1)
                        for j in range(w):
                            if lv < 4:
                                eng.matmul(m.bank(3 + g)[:, P * j:P * j + P], dt[:, c0 + j, :], xx[:, c0 + j, :],
                                           start=True, stop=True)
                        for j in range(w):
                            mm = eng.matmul(m.bank(g)[:, P * j:P * j + P], xx[:, c0 + j, :], dt[:, c0 + j, :],
                                            start=True, stop=True)
                        mm.then_inc(ld_, 1)
                    if e_ == 0 and lv < 2:
                        if lv == 1:
                            eng.wait_ge(sg, 3)
                        za_product(eng, 1, lv)
                for n, (what, g) in enumerate([(x, g) for x in ("yy", "cc", "gg", "rr") for g in range(3)]):
                    c0, w = GROUPS[g]
                    if what == "yy":
                        eng.wait_ge(lte, 15 * e_ + 12 + g + 1)
                    if what == "gg":
                        eng.wait_ge(p_act, 6 * e_ + g + 1)
                    if what == "rr":
                        eng.wait_ge(p_act, 6 * e_ + 3 + g + 1)
                    for j in range(w):
                        c, o = c0 + j, m.bank(n % 6)[:, P * j:P * j + P]
                        if what == "yy":
                            mm = eng.matmul(o, dt[:, c, :], a_tok[:, c, :], start=True, stop=True)
                        elif what == "cc":
                            mm = eng.matmul(o, dt[:, c, :], akt[:, c, :], start=True, stop=True)
                        elif what == "gg":
                            mm = eng.matmul(o, yy[:, c, :], b_tok[:, c, :], start=True, stop=True)
                        else:
                            mm = eng.matmul(m.bank(n % 6)[:, CH * j:CH * j + CH], yy[:, c, :], rbt[:, c, :],
                                            start=True, stop=True)
                    mm.then_inc(p_done, 1)
                eng.wait_ge(s_in, 32 * (e_ + 1))
                if e_ == 0:
                    eng.wait_ge(sg, 4)
                eng.transpose(m.ps[3][:, 0:P], s_raw[:, 0, :], m.ident[:, :]).then_inc(s_turned, 1)

                def h_part(n):
                    x = chunk_of(e_, *updates[n])
                    if n < 6:
                        eng.wait_ge(p_dve, 6 * e_ + 6)
                    else:
                        eng.wait_ge(s_out, NS * e_ + n - 5)
                    eng.matmul(m.bank(n % 6)[:, 0:P], b_tok[:, x, :], cc[:, x, :], start=True, stop=False)
                    eng.matmul(m.bank(n % 6)[:, 0:P], k_tok[:, x, :], v_tok[:, x, :], start=False, stop=False)

                h_part(0)
                h_part(1)
                eng.wait_ge(s_set, e_ + 1)
                for i, c in steps:
                    x = chunk_of(e_, i, c)
                    if i > 0:
                        eng.wait_ge(s_out, NS * e_ + updates.index((i - 1, c)) + 1)
                    if (i, c) in updates:
                        n = updates.index((i, c))
                        eng.matmul(m.bank(n % 6)[:, 0:P], gg[:, x, :], states[:, x, :], start=False, stop=True)\
                           .then_inc(s_done, 1)
                    by = m.ps[3][:, CH * x:CH * x + CH]
                    eng.matmul(by, states[:, x, :], rt[:, x, :], start=True, stop=False)
                    eng.matmul(by, cc[:, x, :], rbt[:, x, :], start=False, stop=False)
                    mm = eng.matmul(by, v_tok[:, x, :], rkt[:, x, :], start=False, stop=True)
                    if (i, c) in updates and n + 2 < NS:
                        h_part(n + 2)
                mm.then_inc(y_done, 1)
                eng.wait_ge(s_out, NS * (e_ + 1))
                eng.transpose(m.bank(0)[:, 0:P], s_raw[:, 2, :], m.ident[:, :]).then_inc(f_turned, 1)
            eng.wait_ge(q_ready, 1)
            eng.wait_ge(f_out, 2)
            for c0, n in SEGMENTS:
                mm = eng.matmul(m.ps[2][:, c0:c0 + n], m.block[:, 6, :], x1[:, c0:c0 + n], start=True, stop=True)
            mm.then_inc(gsum, 1)
            eng.wait_ge(y_out, 2)
            for c0, n in SEGMENTS:
                mm = eng.matmul(m.ps[0][:, c0:c0 + n], m.block[:, 6, :], ys[:, c0:c0 + n], start=True, stop=True)
            mm.then_inc(gsum, 1)
            eng.wait_ge(gsq, 1)
            for c0, n in SEGMENTS:
                mm = eng.matmul(m.ps[1][:, c0:c0 + n], m.block[:, 6, :], x2[:, c0:c0 + n], start=True, stop=True)
            mm.then_inc(gsum, 1)

        @block.scalar
        def _(eng):
            ch = Chain(eng, act)

            def pad_in(i):
                eng.wait_ge(projected, i + 1)
                eng.wait_ge(mixed, i + 1)
                for c0, n, off in ((0, LAT, 1), (LAT, CTX, 3)):
                    eng.activation(pad[:, c0 + off:c0 + off + n], m.ps[i][:, c0:c0 + n], ACT.Copy).then_inc(padded, 1)

            pad_in(0)
            pad_in(1)
            act_sigmoid(eng, 0, 0)
            pad_in(2)
            act_sigmoid(eng, 0, 1)
            eng.wait_ge(ss_done, 1)
            eng.wait_ge(vbd_ready, 1)
            eng.activation(tmp[:, 0:T], m.ps[0][:, 0:T], ACT.Sqrt).then_inc(rooted, 1)
            act_exps(eng, 0)
            eng.wait_ge(g_done, 1)
            eng.activation(gate, m.ps[3][:, 0:T], ACT.Copy).then_inc(rooted, 1)
            for e_ in range(2):
                for n, (what, g) in enumerate(products(e_)):
                    if what in BY_DVE:
                        continue
                    c0, w = GROUPS[g]
                    eng.wait_ge(t_done, done_count(e_) + n + 1)
                    dst = akt if what == "akv" else TURNED[what][1]
                    eng.activation(dst[:, c0:c0 + w, :], cols(m.bank(n % 8), w), ACT.Copy).then_inc(t_act, 1)
                if e_ == 0:
                    act_sigmoid(eng, 1, 0)
                    act_sigmoid(eng, 1, 1)
                    act_exps(eng, 1)
                for n in range(6):
                    c0, w = GROUPS[n % 3]
                    eng.wait_ge(p_done, 12 * e_ + n + 1)
                    eng.activation((yy, cc)[n // 3][:, c0:c0 + w, :], cols(m.bank(n), w), ACT.Copy).then_inc(p_act, 1)
                eng.wait_ge(s_turned, e_ + 1)
                ch(eng.activation(states[:, chunk_of(e_, 0, 0), :], m.ps[3][:, 0:P], ACT.Copy))
                ch(eng.activation(states[:, chunk_of(e_, 0, 1), :], m.ident[:, :], ACT.Copy, scale=0.0))
                eng.sem_inc(s_set, 1)
                if e_ == 0:
                    eng.wait_ge(y_done, 1)
                    eng.activation(ys, m.ps[3][:, 0:T], ACT.Copy).then_inc(y_out, 1)
                eng.wait_ge(f_turned, e_ + 1)
                if e_ == 1:
                    eng.wait_ge(stored, 32)
                ch(eng.activation(s_raw[:, 1, :], m.bank(0)[:, 0:P], ACT.Copy))
                eng.sem_inc(f_out, 1)
            eng.wait_ge(yc_ready, 1)
            eng.activation(x2, ys, ACT.Square).then_inc(gsq, 1)
            eng.wait_ge(gsum, 3)
            eng.activation(x3, m.ps[1][:, 0:T], ACT.Sqrt, scale=1.0 / HD, bias=m.eps[:, 1:2]).then_inc(groot, 1)

        @block.vector
        def _(eng):
            ch = Chain(eng, dve)
            for j, (i, r0) in enumerate(((0, R_MU), (0, R_MU + 8), (0, R_MU + 16), (0, R_W0), (0, R_W0 + 8), (0, R_A0),
                                         (0, R_A0 + 8), (0, R_KK), (0, R_KA), (1, R_RK), (1, R_GNG), (1, R_GNB))):
                j = j if j < 9 else j + 1
                ch(eng.tensor_copy(par[:, j:j + 1], m.par[:, i, bass.ds(hp + r0, 1)]))
            ch(eng.tensor_scalar(par[:, 9:10], par[:, 8:9], -1.0, 1.0, ALU.mult, ALU.add))
            for ins in pad_edges(eng, pad):
                ch(ins)
            eng.sem_inc(mixed, 1)
            eng.wait_ge(padded, 2)
            shift_mix(m, ch, pad, tmp, par[:, 1:2], k)
            eng.sem_inc(mixed, 1)
            ch(eng.tensor_scalar(nkk, k, par[:, 7:8], None, ALU.mult))
            ch(eng.tensor_tensor(x1, nkk, nkk, ALU.mult))
            eng.sem_inc(nrm, 1)
            eng.wait_ge(padded, 4)
            shift_mix(m, ch, pad, tmp, par[:, 0:1], r)
            eng.sem_inc(mixed, 1)
            pre_a(eng, ch, 0)
            eng.wait_ge(padded, 6)
            shift_mix(m, ch, pad, tmp, par[:, 2:3], v)
            eng.wait_ge(zeroed, 1)
            for p0, p1 in heads:
                ch(eng.tensor_copy(v_bd[p0:p1, :, p0:p1], chunks(v)[p0:p1]))
            eng.sem_inc(vbd_ready, 1)
            eng.wait_ge(rooted, 1)
            ch(eng.tensor_scalar(tmp[:, 0:T], tmp[:, 0:T], 1e-12, None, ALU.max))
            ch(eng.reciprocal(tmp[:, 0:T], tmp[:, 0:T]))
            ch(eng.scalar_tensor_tensor(out=nkk, in0=nkk, scalar=-1.0, in1=tmp[:, 0:T], op0=ALU.mult, op1=ALU.mult))
            for f in (pre_b, pre_c, pre_d, pre_e):
                f(eng, ch, 0)
            for e_ in range(2):
                for n, (what, g) in enumerate(products(e_)):
                    if what not in BY_DVE:
                        continue
                    c0, w = GROUPS[g]
                    eng.wait_ge(t_done, done_count(e_) + n + 1)
                    if what in ("rbt", "rkt"):
                        src, mask = cols(m.bank(n % 8), w, CH), over(m.trid[:, e_], w, CH)
                        dst = (rbt if what == "rbt" else rkt)[:, c0:c0 + w, :]
                    else:
                        src = cols(m.bank(n % 8), w)
                        dst = {"abt": abt, "ab": dd, "akt": akt}[what][:, c0:c0 + w, :]
                        mask = over(m.tri1[:, e_] if what == "ab" else m.tri[:, e_], w)
                    eng.tensor_tensor(dst, src, mask, ALU.mult).then_inc(t_dve, 1)
                    if (what, g) == ("ab", 2):
                        eng.wait_ge(t_dve, out_count(e_, n + 1, True))
                        ch(eng.tensor_tensor(dd, dd, over(m.ident[:, :], NCH), ALU.add))
                        ch(eng.tensor_tensor(dt, abt, over(m.level[:, 0], NCH), ALU.mult))
                        ch(eng.tensor_tensor(dt, dt, over(m.ident[:, :], NCH), ALU.add))
                        eng.sem_inc(d1, 1)
                for lv in range(5):
                    n0 = 15 * e_ + 3 * lv
                    for g, (c0, w) in enumerate(GROUPS):
                        eng.wait_ge(lx, n0 + g + 1)
                        eng.tensor_tensor(xx[:, c0:c0 + w, :], cols(m.bank(g), w), over(m.level[:, lv + 1], w), ALU.mult)\
                           .then_inc(lxe, 1)
                    for g, (c0, w) in enumerate(GROUPS):
                        eng.wait_ge(ld_, n0 + g + 1)
                        for b0, t, sem in ((3, dd, lde), (0, dt, lte)):
                            if (b0, lv) != (3, 4):
                                eng.tensor_tensor(t[:, c0:c0 + w, :], t[:, c0:c0 + w, :], cols(m.bank(b0 + g), w), ALU.add)\
                                   .then_inc(sem, 1)
                    if e_ == 0 and lv < 4:
                        (pre_a, pre_b, pre_c, pre_d)[lv](eng, ch, 1)
                for n in range(6, 12):
                    c0, w = GROUPS[n % 3]
                    eng.wait_ge(p_done, 12 * e_ + n + 1)
                    if n < 9:
                        eng.tensor_tensor(gg[:, c0:c0 + w, :], cols(m.bank(n % 6), w), over(m.ident[:, :], w), ALU.add)\
                           .then_inc(p_dve, 1)
                    else:
                        eng.tensor_tensor(rt[:, c0:c0 + w, :], rt[:, c0:c0 + w, :], cols(m.bank(n % 6), w, CH), ALU.add)\
                           .then_inc(p_dve, 1)
                for n, (i, c) in enumerate(updates):
                    x = chunk_of(e_, i, c)
                    eng.wait_ge(s_done, NS * e_ + n + 1)
                    eng.tensor_scalar(state_after(e_, i, c), m.bank(n % 6)[:, 0:P], wc[:, e_, x:x + 1], None, ALU.mult)\
                       .then_inc(s_out, 1)
                eng.wait_ge(y_done, e_ + 1)
                if e_ == 0:
                    pre_e(eng, ch, 1)
                else:
                    eng.tensor_tensor(ys, ys, m.ps[3][:, 0:T], ALU.add).then_inc(y_out, 1)
            ch(eng.scalar_tensor_tensor(out=x1, in0=kds, scalar=par[:, 10:11], in1=r, op0=ALU.mult, op1=ALU.mult))
            eng.sem_inc(q_ready, 1)
            eng.wait_ge(gsum, 2)
            ch(eng.scalar_tensor_tensor(out=ys, in0=m.ps[0][:, 0:T], scalar=-1.0 / HD, in1=ys,
                                        op0=ALU.mult, op1=ALU.add))
            eng.sem_inc(yc_ready, 1)
            ch(eng.tensor_tensor(v, v, m.ps[2][:, 0:T], ALU.mult))
            eng.wait_ge(groot, 1)
            ch(eng.reciprocal(x3, x3))
            ch(eng.tensor_tensor(ys, ys, x3, ALU.mult))
            ch(eng.tensor_scalar(ys, ys, par[:, 11:12], par[:, 12:13], ALU.mult, ALU.add))
            ch(eng.tensor_tensor(ys, ys, v, ALU.add))
            ch(eng.tensor_tensor(ys, ys, gate, ALU.mult))
            ch(eng.tensor_copy(m.ya[:, hp, :], ys))
    st.close()

def stage_branches(m, l):
    nc, d = m.nc, m.dram
    st = Stage(nc, "br")
    s = st.sem
    landed = [s(f"w{i}") for i in range(WRING)]
    pw_in, used, out_act, zeroed, edges, pooled, mixed = (
        s(n) for n in ("pool_w", "projected", "taken_out", "zeroed", "edges", "pooled", "pool_mixed"))
    dve, pool, act, gated, conv, cen, sums, sq_done, rooted, norm, sgm = (
        s(n) for n in ("dve", "pool", "act", "gated", "convolved", "centred", "sums", "squares", "rooted", "normed",
                       "sigmoids"))
    m.used = 0
    yb, yc = m.take(4, T), m.take(4, T)
    HALO = 8
    NL, NC_ = (ROWS + 2 * HALO) * GRID_W, CTX + 2 * HALO
    za, zb = m.take(4, NL + NC_), m.take(2, NL + NC_)
    cnt = m.take(3, ROWS + 2 * HALO + NC_)
    pw = m.take(4, P)
    HT = TAPS // 2
    RW = GRID_W + 2 * HT
    uc = m.take(ROWS * RW + CTX + 2 * HT)
    ga = m.take(T)
    NPROJ = 12
    cols = [B_POOL + i for i in range(4)]
    for i in range(4):
        cols += [B_CONV + 4 + i, B_CONV + i]

    def lat(t):
        return t[:, 0:NL]

    def ctx(t):
        return t[:, NL:NL + NC_]

    lat_u = uc[:, 0:ROWS * RW].rearrange("p (r w) -> p r w", w=RW)
    ctx_u = uc[:, ROWS * RW:]

    def take_pool(eng, ch, g):
        eng.wait_ge(sums, g + 1)
        ch(eng.tensor_scalar(yb[:, g, :], m.ps[3][:, 0:T], m.par[:, 1, R_PB + g:R_PB + g + 1],
                             m.par[:, 1, R_PS + g:R_PS + g + 1], ALU.add, ALU.mult))
        eng.sem_inc(mixed, 1)

    with nc.Block() as block:
        @block.sync
        def _(eng):
            eng.dma_start(pw, d["pool_w"].rearrange("l g c e -> l c g e")[l]).then_inc(pw_in, 16)
            for n, b in enumerate(cols):
                if n >= WRING:
                    eng.wait_ge(used, n - WRING + 1)
                eng.dma_start(m.w[:, n % WRING], m.w_in[l, b]).then_inc(landed[n % WRING], 16)

        @block.gpsimd
        def _(eng):
            ch = Chain(eng, pool)
            for t in [za[:, i] for i in range(4)]:
                ch(eng.memset(t[:, 0:HALO * GRID_W], 0.0))
                ch(eng.memset(t[:, (HALO + ROWS) * GRID_W:NL + HALO], 0.0))
                ch(eng.memset(t[:, NL + HALO + CTX:NL + NC_], 0.0))
            ch(eng.memset(uc, 0.0))
            ch(eng.memset(cnt, 0.0))
            ch(eng.memset(cnt[:, 0, HALO:HALO + ROWS], 1.0))
            ch(eng.memset(cnt[:, 0, ROWS + 3 * HALO:ROWS + 3 * HALO + CTX], 1.0))
            eng.sem_inc(zeroed, 1)

        @block.tensor
        def _(eng):
            for n in range(NPROJ):
                eng.wait_ge(landed[n % WRING], 16 * (n // WRING + 1))
                if n >= 3:
                    eng.wait_ge(out_act, n - 2)
                project(eng, m, m.ps[n % 3], n % WRING, m.h).then_inc(used, 1)
                if n != 6:
                    continue
                eng.wait_ge(pw_in, 16)
                for g in range(4):
                    eng.wait_ge(pooled, g + 1)
                    if g > 0:
                        eng.wait_ge(mixed, g)
                    for c0, w in SEGMENTS:
                        mm = eng.matmul(m.ps[3][:, c0:c0 + w], pw[:, g, :], za[:, g, c0:c0 + w],
                                        start=True, stop=True)
                    mm.then_inc(sums, 1)
            eng.wait_ge(out_act, NPROJ)
            eng.wait_ge(conv, 4)
            for g in range(4):
                for c0, n in SEGMENTS:
                    mm = eng.matmul(m.ps[0][:, c0:c0 + n], m.ones[:, :], yc[:, g, c0:c0 + n],
                                    start=(g == 0), stop=(g == 3))
            mm.then_inc(sums, 1)
            for g in range(4):
                eng.wait_ge(sq_done, g + 1)
                for c0, n in SEGMENTS:
                    mm = eng.matmul(m.ps[1][:, c0:c0 + n], m.ones[:, :], za[:, g, c0:c0 + n],
                                    start=(g == 0), stop=(g == 3))
            mm.then_inc(sums, 1)

        @block.scalar
        def _(eng):
            ch = Chain(eng, act)
            eng.wait_ge(zeroed, 1)
            for n in range(NPROJ):
                eng.wait_ge(used, n + 1)
                src = m.ps[n % 3]
                if n < 4:
                    ch(eng.activation(lat(za[:, n])[:, HALO * GRID_W:(HALO + ROWS) * GRID_W], src[:, 0:LAT], ACT.Copy))
                    ch(eng.activation(ctx(za[:, n])[:, HALO:HALO + CTX], src[:, LAT:T], ACT.Copy))
                elif n % 2 == 0:
                    if n > 4:
                        eng.wait_ge(gated, (n - 4) // 2)
                    ch(eng.activation(ga, src[:, 0:T], ACT.Sigmoid))
                else:
                    eng.wait_ge(gated, (n - 3) // 2)
                eng.sem_inc(out_act, 1)
            for g in range(4):
                eng.wait_ge(cen, g + 1)
                eng.activation(za[:, g, 0:T], yc[:, g, :], ACT.Square).then_inc(sq_done, 1)
            eng.wait_ge(sums, 6)
            eng.activation(ga, m.ps[1][:, 0:T], ACT.Sqrt, scale=1.0 / 512, bias=m.eps[:, 2:3]).then_inc(rooted, 1)
            for g in range(4):
                eng.wait_ge(norm, g + 1)
                eng.activation(za[:, g, 0:T], yc[:, g, :], ACT.Sigmoid).then_inc(sgm, 1)

        @block.vector
        def _(eng):
            ch = Chain(eng, dve)
            eng.wait_ge(zeroed, 1)
            nr = ROWS + 2 * HALO
            for g in range(4):
                eng.wait_ge(out_act, g + 1)
                srcs, c_src = za[:, g], cnt[:, 0]
                for j in range(g + 1):
                    sh = 1 << j
                    dst, c_dst = zb[:, j % 2], cnt[:, 1 + j % 2]
                    nl, nx = NL - (2 * sh - 1) * GRID_W, NC_ - (2 * sh - 1)
                    ch(eng.tensor_tensor(dst[:, 0:nl], srcs[:, 0:nl], srcs[:, sh * GRID_W:sh * GRID_W + nl], ALU.add))
                    ch(eng.tensor_tensor(ctx(dst)[:, 0:nx], ctx(srcs)[:, 0:nx], ctx(srcs)[:, sh:sh + nx], ALU.add))
                    for a0, w in ((0, nr - (2 * sh - 1)), (nr, nx)):
                        ch(eng.tensor_tensor(c_dst[:, a0:a0 + w], c_src[:, a0:a0 + w], c_src[:, a0 + sh:a0 + sh + w],
                                             ALU.add))
                    srcs, c_src = dst, c_dst
                half = 1 << g
                o, oc = HALO - half, zb[:, (g + 1) % 2]
                cr, cx = c_src[:, o:o + ROWS], c_src[:, nr + o:nr + o + CTX]
                ch(eng.reciprocal(cr, cr))
                ch(eng.reciprocal(cx, cx))
                sl = srcs[:, o * GRID_W:(o + ROWS) * GRID_W].rearrange("p (r w) -> p r w", w=GRID_W)
                ch(eng.tensor_tensor(oc[:, 0:LAT].rearrange("p (r w) -> p r w", w=GRID_W), sl,
                                     cr.unsqueeze(2).to_broadcast([P, ROWS, GRID_W]), ALU.mult))
                ch(eng.tensor_tensor(oc[:, LAT:T], ctx(srcs)[:, o:o + CTX], cx, ALU.mult))
                ch(eng.tensor_tensor(oc[:, 0:LAT], oc[:, 0:LAT], za[:, g, HALO * GRID_W:(HALO + ROWS) * GRID_W],
                                     ALU.subtract))
                ch(eng.tensor_tensor(oc[:, LAT:T], oc[:, LAT:T], ctx(za[:, g])[:, HALO:HALO + CTX], ALU.subtract))
                ch(eng.tensor_copy(za[:, g, 0:T], oc[:, 0:T]))
                eng.sem_inc(pooled, 1)
                if g > 0:
                    take_pool(eng, ch, g - 1)
            take_pool(eng, ch, 3)
            for g in range(4):
                eng.wait_ge(out_act, 5 + 2 * g)
                eng.wait_ge(used, 6 + 2 * g)
                src = m.ps[(5 + 2 * g) % 3]
                ch(eng.tensor_tensor(lat_u[:, :, HT:HT + GRID_W], ga[:, 0:LAT].rearrange("p (r w) -> p r w", w=GRID_W),
                                     src[:, 0:LAT].rearrange("p (r w) -> p r w", w=GRID_W), ALU.mult))
                ch(eng.tensor_tensor(ctx_u[:, HT:HT + CTX], ga[:, LAT:T], src[:, LAT:T], ALU.mult))
                eng.sem_inc(gated, 1)
                dl, dc = yc[:, g, 0:LAT].rearrange("p (r w) -> p r w", w=GRID_W), yc[:, g, LAT:T]
                for t in range(TAPS):
                    wt = m.par[:, 2, 4 * t + g:4 * t + g + 1]
                    il, ic = lat_u[:, :, t:t + GRID_W], ctx_u[:, t:t + CTX]
                    if t == 0:
                        cb = m.par[:, 1, R_CB + g:R_CB + g + 1]
                        ch(eng.tensor_scalar(dl, il, wt, cb, ALU.mult, ALU.add))
                        ch(eng.tensor_scalar(dc, ic, wt, cb, ALU.mult, ALU.add))
                    else:
                        ch(eng.scalar_tensor_tensor(out=dl, in0=il, scalar=wt, in1=dl, op0=ALU.mult, op1=ALU.add))
                        ch(eng.scalar_tensor_tensor(out=dc, in0=ic, scalar=wt, in1=dc, op0=ALU.mult, op1=ALU.add))
                eng.sem_inc(conv, 1)
            eng.wait_ge(sums, 5)
            for g in range(4):
                ch(eng.scalar_tensor_tensor(out=yc[:, g, :], in0=m.ps[0][:, 0:T], scalar=-1.0 / 512, in1=yc[:, g, :],
                                            op0=ALU.mult, op1=ALU.add))
                eng.sem_inc(cen, 1)
            eng.wait_ge(rooted, 1)
            ch(eng.reciprocal(ga, ga))
            for g in range(4):
                ch(eng.tensor_tensor(yc[:, g, :], yc[:, g, :], ga, ALU.mult))
                ch(eng.tensor_scalar(yc[:, g, :], yc[:, g, :], m.par[:, 1, R_LG + g:R_LG + g + 1],
                                     m.par[:, 1, R_LB + g:R_LB + g + 1], ALU.mult, ALU.add))
                eng.sem_inc(norm, 1)
            for g in range(4):
                eng.wait_ge(sgm, g + 1)
                ch(eng.tensor_tensor(yc[:, g, :], yc[:, g, :], za[:, g, 0:T], ALU.mult))

    st.close()


def stage_merge(m, l, db):
    nc, d = m.nc, m.dram
    st = Stage(nc, "mg")
    s = st.sem
    landed = [s(f"w{i}") for i in range(WRING)]
    done, gates, dve = s("done"), s("gates"), s("dve")
    m.used = 0
    yb, yc, merged = m.take(4, T), m.take(4, T), m.take(KB, T)
    g, acc, part = m.take(3, T), m.take(T), m.take(T)
    outs = [d[n].rearrange("l (k p) (b c) -> l b p k c", p=P, c=P) for n in ("w_a_out", "w_b_out", "w_c_out")]
    with nc.Block() as block:
        @block.sync
        def _(eng):
            for i in range(3):
                eng.dma_start(m.w[:, i], m.w_in[l, db + (B_GATE + KB * i)]).then_inc(landed[i], 16)
            eng.dma_start(m.w[:, 3], outs[0][l, db]).then_inc(landed[3], 16)
            eng.dma_start(m.w[:, 4, 0:4], outs[1][l, db]).then_inc(landed[4], 16)
            eng.dma_start(m.w[:, 4, 4:8], outs[2][l, db]).then_inc(landed[4], 16)

        @block.tensor
        def _(eng):
            for i in range(4):
                eng.wait_ge(landed[i], 16)
                project(eng, m, m.ps[i], i, m.h if i < 3 else m.ya).then_inc(done, 1)
            eng.wait_ge(landed[4], 32)
            for i, y in enumerate((yb, yc)):
                eng.wait_ge(gates, i + 1)
                for k in range(4):
                    for c0, n in SEGMENTS:
                        mm = eng.matmul(m.ps[i][:, c0:c0 + n], m.w[:, 4, 4 * i + k, :], y[:, k, c0:c0 + n],
                                        start=(k == 0), stop=(k == 3))
                mm.then_inc(done, 1)

        @block.scalar
        def _(eng):
            for i in range(3):
                eng.wait_ge(done, i + 1)
                eng.activation(g[:, i, :], m.ps[i][:, 0:T], ACT.Sigmoid).then_inc(gates, 1)

        @block.vector
        def _(eng):
            ch = Chain(eng, dve)
            eng.wait_ge(gates, 3)
            eng.wait_ge(done, 4)
            ch(eng.tensor_tensor(acc, g[:, 0, :], m.ps[3][:, 0:T], ALU.mult))
            eng.wait_ge(done, 5)
            ch(eng.tensor_tensor(part, g[:, 1, :], m.ps[0][:, 0:T], ALU.mult))
            ch(eng.tensor_tensor(acc, acc, part, ALU.add))
            eng.wait_ge(done, 6)
            ch(eng.tensor_tensor(part, g[:, 2, :], m.ps[1][:, 0:T], ALU.mult))
            ch(eng.tensor_tensor(merged[:, db, :], acc, part, ALU.add))
    st.close()


def stage_out(m, l, half):
    nc, d = m.nc, m.dram
    st = Stage(nc, "out")
    s = st.sem
    landed = [s(f"w{i}") for i in range(4)]
    done, dve = s("done"), s("dve")
    m.used = 0
    m.take(4, T), m.take(4, T)
    merged = m.take(KB, T)
    gt = m.take(4, 2)
    res = m.take(T)
    w = d["w_out"].rearrange("l (k p) (b c) -> l b p k c", p=P, c=P)
    with nc.Block() as block:
        @block.sync
        def _(eng):
            for i in range(4):
                eng.dma_start(m.w[:, i], w[l, half * 4 + i]).then_inc(landed[i], 16)

        @block.tensor
        def _(eng):
            for i in range(4):
                eng.wait_ge(landed[i], 16)
                project(eng, m, m.ps[i], i, merged).then_inc(done, 1)

        @block.vector
        def _(eng):
            ch = Chain(eng, dve)
            ch(eng.tensor_copy(gt, m.mod[:, GT1, bass.ds(half * 4, 4), :]))
            for i in range(4):
                eng.wait_ge(done, i + 1)
                for j, (c0, n) in enumerate(SEGMENTS):
                    ch(eng.tensor_scalar(res[:, c0:c0 + n], m.ps[i][:, c0:c0 + n], gt[:, i, j:j + 1], None, ALU.mult))
                ch(eng.tensor_tensor(m.x[:, half * 4 + i, :], m.x[:, half * 4 + i, :], res, ALU.add))
    st.close()

def stage_tokens_first(m, store=False):
    nc, d = m.nc, m.dram
    st = Stage(nc, "tok")
    turned, copied, stored = st.sem("turned"), st.sem("copied"), st.sem("stored")
    rows = m.ya[:, :, :].rearrange("p a b -> p (a b)").rearrange("p (t c) -> p t c", c=D)
    NT = TILES * KB // 4
    with nc.Block() as block:
        @block.tensor
        def _(eng):
            for n in range(NT):
                t, k0 = n // 2, 4 * (n % 2)
                if n >= 8:
                    eng.wait_ge(copied, n - 7)
                for j in range(4):
                    mm = eng.transpose(m.bank(n % 8)[:, P * j:P * j + P], m.h[:, k0 + j, P * t:P * t + P], m.ident[:, :])
                mm.then_inc(turned, 1)

        @block.vector
        def _(eng):
            for n in range(NT):
                t, k0 = n // 2, 4 * (n % 2)
                eng.wait_ge(turned, n + 1)
                eng.tensor_copy(rows[:, t, P * k0:P * k0 + 4 * P], m.bank(n % 8)).then_inc(copied, 1)

        if store:
            @block.sync
            def _(eng):
                eng.wait_ge(copied, 8)
                eng.dma_start(d["y_sample"][0].rearrange("(t p) c -> p t c", p=P), rows[:, 0:4, :]).then_inc(stored, 16)
                eng.wait_ge(copied, NT)
                eng.dma_start(d["y_prompt"][0], rows[:, 4, :]).then_inc(stored, 16)
                eng.wait_ge(stored, 32)
    st.close()


def top16(ch, vals, idx, src, spare):
    eng = ch.eng
    ch(eng.max(vals[:, 0:8], src))
    ch(eng.max_index(idx[:, 0:8], vals[:, 0:8], src))
    ch(eng.match_replace(spare, vals[:, 0:8], src, -3.4028235e38))
    ch(eng.max(vals[:, 8:16], spare))
    ch(eng.max_index(idx[:, 8:16], vals[:, 8:16], spare))


def peer_tables(m):
    m.used = 0
    return m.take(TILES + 1, 2 * HEADS_Q, TOPK), m.take(TILES + 1, 2 * HEADS_Q, TOPK)


def stage_scores(m, l, quarter):
    nc, d = m.nc, m.dram
    st = Stage(nc, "sc")
    s = st.sem
    landed = [s(f"w{i}") for i in range(4)]
    keys_in, q_done, k_done, q_out, s_done, s_out, dve, top_done = (
        s(n) for n in ("keys", "q_done", "k_turned", "q_out", "scored", "s_out", "dve", "tops"))
    top_v, top_i = peer_tables(m)
    keys, qt, kt, sc = m.take(4, P), m.take(2, T), m.take(2, P), m.take(2, TILES, P)
    vals, places = m.take(TILES, 4, TOPK), m.take(TILES, 4, TOPK).bitcast(U32)
    spare = m.take(P)
    wq = d["peer_wq"].rearrange("l (k p) (b c) -> l b p k c", p=P, c=P)
    pk = d["peer_keys"].rearrange("l h e n q -> l (h e) n q")

    def take(eng, i):
        eng.wait_ge(s_done, i + 1)
        if i >= 2:
            eng.wait_ge(top_done, i - 1)
        eng.activation(sc[:, i % 2].rearrange("p t n -> p (t n)"), m.ps[2 + i % 2][:, 0:T], ACT.Copy).then_inc(s_out, 1)

    with nc.Block() as block:
        @block.sync
        def _(eng):
            eng.dma_start(keys, pk[l, bass.ds(quarter * 4, 4)].rearrange("b n q -> n b q")).then_inc(keys_in, 16)
            for i in range(4):
                eng.dma_start(m.w[:, i], wq[l, quarter * 4 + i]).then_inc(landed[i], 16)

        @block.tensor
        def _(eng):
            eng.wait_ge(keys_in, 16)

            def score(i):
                eng.wait_ge(q_out, 2 * i + 2)
                if i >= 2:
                    eng.wait_ge(s_out, i - 1)
                for t in range(TILES):
                    mm = eng.matmul(m.ps[2 + i % 2][:, P * t:P * t + P], qt[:, i % 2, P * t:P * t + P],
                                    kt[:, i % 2, :], start=True, stop=True)
                mm.then_inc(s_done, 1)

            for i in range(4):
                eng.wait_ge(landed[i], 16)
                if i >= 2:
                    eng.wait_ge(q_out, 2 * i - 2)
                project(eng, m, m.ps[i % 2], i, m.h).then_inc(q_done, 1)
                eng.transpose(m.ps[i % 2][:, 768:768 + P], keys[:, i, :], m.ident[:, :]).then_inc(k_done, 1)
                if i >= 1:
                    score(i - 1)
            score(3)

        @block.scalar
        def _(eng):
            for i in range(4):
                eng.wait_ge(k_done, i + 1)
                if i >= 2:
                    eng.wait_ge(s_done, i - 1)
                eng.activation(qt[:, i % 2, :], m.ps[i % 2][:, 0:T], ACT.Copy).then_inc(q_out, 1)
                eng.activation(kt[:, i % 2, :], m.ps[i % 2][:, 768:768 + P], ACT.Copy).then_inc(q_out, 1)
                if i >= 1:
                    take(eng, i - 1)
            take(eng, 3)

        @block.vector
        def _(eng):
            ch = Chain(eng, dve)
            for i in range(4):
                eng.wait_ge(s_out, i + 1)
                for t in range(TILES):
                    top16(ch, vals[:, t, i], places[:, t, i], sc[:, i % 2, t], spare)
                eng.sem_inc(top_done, 1)
            ch(eng.tensor_copy(top_v[:, 0:TILES, bass.ds(quarter * 4, 4), :], vals))
            ch(eng.tensor_copy(top_i[:, 0:TILES, bass.ds(quarter * 4, 4), :], places))
    st.close()


GROUP = 32
PAIR = GROUP // TOPK
GROUPS_T = SLOTS // GROUP


class Selection:
    pass


def select_tables(m):
    w = Selection()
    w.top_v, w.top_i = peer_tables(m)
    w.idx, w.gate = m.take((TILES + 1) * SLOTS), m.take((TILES + 1) * SLOTS)
    w.iota, w.tv, w.ti = m.take(TOPK), m.take(2 * PAIR, TOPK), m.take(2 * PAIR, TOPK)
    w.cand, w.hot, w.spare = m.take(PAIR, TOPK * TOPK), m.take(PAIR, TOPK, TOPK), m.take(TOPK * TOPK)
    w.best, w.place, w.part = m.take(PAIR, TOPK), m.take(PAIR, TOPK).bitcast(U32), m.take(PAIR, TOPK).bitcast(U32)
    w.e, w.ex, w.rows, w.tot = m.take(PAIR, PAIR * TOPK), m.take(PAIR, TOPK), m.take(GROUP), m.take(PAIR)
    return w


def select_part(ch, w, g, part, shifted, exped, softmaxed):
    eng = ch.eng
    full = [P, PAIR, TOPK, TOPK]
    flat = "p h k -> p (h k)"
    if part == 0:
        for local, table in ((w.tv, w.top_v), (w.ti, w.top_i)):
            ch(eng.tensor_copy(local.rearrange(flat),
                               table.rearrange("p t b k -> p (t b k)")[:, bass.ds(g * (2 * GROUP), 2 * GROUP)]))
        tv = w.tv.rearrange("p (h e) k -> p h e k", e=2)
        ch(eng.tensor_tensor(w.cand.rearrange("p h (i j) -> p h i j", j=TOPK), tv[:, :, 0].unsqueeze(3).to_broadcast(full),
                             tv[:, :, 1].unsqueeze(2).to_broadcast(full), ALU.add))
        top16(ch, w.best[:, 0], w.place[:, 0], w.cand[:, 0], w.spare)
    elif part == 1:
        top16(ch, w.best[:, 1], w.place[:, 1], w.cand[:, 1], w.spare)
        ch(eng.tensor_tensor(w.ex, w.best, w.best[:, :, 0:1].to_broadcast([P, PAIR, TOPK]), ALU.subtract))
        eng.sem_inc(shifted, 1)
    else:
        half = part - 2
        op, by = ((ALU.logical_shift_right, 4), (ALU.bitwise_and, 15))[half]
        e = w.e[:, half].rearrange("p (h k) -> p h k", k=TOPK)
        ch(eng.tensor_scalar(w.part, w.place, by, None, op))
        ch(eng.tensor_copy(e, w.part))
        ch(eng.tensor_tensor(w.hot, e.unsqueeze(3).to_broadcast(full),
                             w.iota.unsqueeze(1).unsqueeze(1).to_broadcast(full), ALU.is_equal))
        keys = w.ti.rearrange("p (h e) k -> p h e k", e=2)[:, :, half].unsqueeze(2).to_broadcast(full)
        ch(eng.tensor_tensor(w.hot, w.hot, keys, ALU.mult))
        ch(eng.tensor_reduce(e, w.hot, AX.X, ALU.add))
    if part == 3:
        ch(eng.tensor_scalar(w.rows, w.e[:, 0], float(KEYS), w.row0, ALU.mult, ALU.add))
        ch(eng.tensor_tensor(w.rows, w.rows, w.e[:, 1], ALU.add))
        ch(eng.tensor_copy(w.idx.bitcast(U32)[:, bass.ds(g * GROUP, GROUP)], w.rows))
        eng.wait_ge(exped, softmaxed)
        ch(eng.tensor_reduce(w.tot, w.ex, AX.X, ALU.add))
        ch(eng.reciprocal(w.tot, w.tot))
        ch(eng.tensor_tensor(w.ex, w.ex, w.tot.unsqueeze(2).to_broadcast([P, PAIR, TOPK]), ALU.mult))
        ch(eng.tensor_copy(w.gate[:, bass.ds(g * GROUP, GROUP)], w.ex.rearrange(flat)))


def stage_select_first(m):
    nc = m.nc
    st = Stage(nc, "sel")
    dve, pair, shifted, exped, drawn = (st.sem(n) for n in ("dve", "pair", "shifted", "exponentials", "iota"))
    w = select_tables(m)
    w.row0 = m.row0[:, 0:1]
    ints = w.spare[:, 0:TOPK].bitcast(mybir.dt.int32)
    with nc.Block() as block:
        @block.gpsimd
        def _(eng):
            eng.iota(ints, pattern=[[1, TOPK]], base=0, channel_multiplier=0).then_inc(drawn, 1)

        @block.scalar
        def _(eng):
            with eng.Fori(0, GROUPS_T) as g:
                eng.wait_ge(shifted, g + 1)
                eng.activation(w.ex, w.ex, ACT.Exp).then_inc(exped, 1)

        @block.vector
        def _(eng):
            ch = Chain(eng, dve)
            for table in (w.top_v, w.top_i):
                ch(eng.memset(table[:, TILES], 0.0))
            eng.wait_ge(drawn, 1)
            ch(eng.tensor_copy(w.iota, ints))
            with eng.Fori(0, GROUPS_T) as g:
                eng.sem_clear(pair)
                ch = Chain(eng, pair)
                for part in range(4):
                    select_part(ch, w, g, part, shifted, exped, g + 1)
    st.close()


def stage_retrieve(m, l):
    nc, d = m.nc, m.dram
    st = Stage(nc, "ret")
    s = st.sem
    SUB = 4
    QS = GROUP // SUB
    LEAD = 4
    HALF = GROUP // 2
    u_in, v_in = m.u_in, m.v_in
    before = l * (16 * TILES * SLOTS // RING)
    u_free, v_free, hid_done, gel_done, w_done, dg_done, staged, g_in = (
        s(n) for n in ("u_free", "v_free", "hid_done", "gelu_done", "weights_done", "diag_done", "staged", "gates_in"))
    dve, pair, shifted, exped, selected = (s(n) for n in ("dve", "pair", "shifted", "exponentials", "selected"))
    summed, sum_out, turned, asked, h_in, x_out, zeroed, begun = (
        s(n) for n in ("summed", "sum_out", "turned", "asked", "h_in", "x_out", "zeroed", "begun"))
    w = select_tables(m)
    w.row0 = m.row0[:, 0:1]
    hs, sm = m.take(D), m.take(D)
    ub, vb, dg = m.take(RING, D), m.take(RING, D), m.take(RING, P)
    stage, hid, gel, wgt, g16 = (m.take(GROUP) for _ in range(5))
    gt, zero = m.take(KB), m.take(512)
    ut = d["peer_u"].rearrange("l e c -> (l e) c")
    vt = d["peer_v"].rearrange("l e c -> (l e) c")
    rows = m.ya[:, :, :].rearrange("p a b -> p (a b)").rearrange("p (t c) -> p t c", c=D)

    def stage_rows(eng, g, half):
        a = HALF * half
        eng.wait_ge(selected, g + 1)
        eng.tensor_copy(stage.bitcast(U32)[:, a:a + HALF],
                        w.idx.bitcast(U32)[:, bass.ds(g * GROUP + a, HALF)]).then_inc(staged, 1)
        eng.wait_ge(staged, g * 2 + (half + 1))

    def gather(eng, g, i, free, table, buf, landed):
        off = bass.IndirectOffsetOnAxis(ap=stage.bitcast(U32)[:, i % GROUP:i % GROUP + 1], axis=0)
        eng.wait_ge(free, g * GROUP + (i + 1))
        eng.sem_inc(asked, 1)
        eng.indirect_dma_start(buf[:, i % RING, :], None, table, off).then_inc(landed[i % RING], 16)

    def gather_u(eng, g, i):
        gather(eng, g, i, u_free, ut, ub, u_in)

    def gather_v(eng, g, i):
        gather(eng, g, i, v_free, vt, vb, v_in)

    def weights(eng, g, q):
        a = slice(SUB * q, SUB * q + SUB)
        eng.wait_ge(gel_done, g * QS + (q + 1))
        eng.tensor_tensor(wgt[:, a], gel[:, a], g16[:, a], ALU.mult).then_inc(w_done, 1)

    def diag(eng, g, q):
        eng.wait_ge(w_done, g * QS + (q + 1))
        for i in range(SUB * q, SUB * q + SUB):
            eng.wait_ge(v_free, g * GROUP + (i + 1))
            eng.activation(dg[:, i % RING, :], m.ident[:, :], ACT.Copy, scale=wgt[:, i:i + 1]).then_inc(dg_done, 1)

    with nc.Block() as block:
        @block.gpsimd
        def _(eng):
            stage_rows(eng, 0, 0)
            for i in range(LEAD):
                gather_u(eng, 0, i)
            with eng.Fori(0, TILES * GROUPS_T - 1) as g:
                for i in range(GROUP):
                    if i == HALF - LEAD:
                        stage_rows(eng, g, 1)
                    if i == GROUP - LEAD:
                        stage_rows(eng, g + 1, 0)
                    gather_u(eng, g, i + LEAD)
                    gather_v(eng, g, i)
            g = TILES * GROUPS_T - 1
            for i in range(GROUP):
                if i == HALF - LEAD:
                    stage_rows(eng, g, 1)
                if i < GROUP - LEAD:
                    gather_u(eng, g, i + LEAD)
                gather_v(eng, g, i)

        @block.vector
        def _(eng):
            eng.sem_inc(selected, GROUPS_T)
            eng.sem_inc(u_free, RING)
            eng.sem_inc(x_out, 1)
            eng.memset(zero, 0.0).then_inc(zeroed, 1)
            with eng.Fori(0, TILES) as t:
                eng.tensor_copy(hs, rows[:, t, :]).then_inc(h_in, 1)
                eng.tensor_copy(gt, m.gate2[:, t, :]).then_inc(h_in, 1)
                eng.wait_ge(h_in, t * 2 + 2)
                eng.sem_inc(begun, 1)
                with eng.Fori(0, GROUPS_T) as tg:
                    g = t * GROUPS_T + tg
                    eng.tensor_copy(g16, w.gate[:, bass.ds(g * GROUP, GROUP)]).then_inc(g_in, 1)
                    eng.wait_ge(g_in, g + 1)
                    eng.sem_inc(begun, 1)
                    eng.sem_clear(pair)
                    ch = Chain(eng, pair)
                    for i in range(GROUP):
                        r = i % RING
                        eng.wait_ge(u_in[r], before + g * (16 * (GROUP // RING)) + 16 * (i // RING + 1))
                        eng.tensor_tensor_reduce(ub[:, r, :], ub[:, r, :], hs, 1.0, 0.0, ALU.mult, ALU.add,
                                                 hid[:, i:i + 1]).then_inc(u_free, 1)
                        if i % SUB == SUB - 1:
                            q = i // SUB
                            eng.wait_ge(u_free, g * GROUP + (RING + i + 1))
                            eng.sem_inc(hid_done, 1)
                            if q > 0:
                                weights(eng, g, q - 1)
                            if q % 2 == 0:
                                select_part(ch, w, g + GROUPS_T, q // 2, shifted, exped, g + 1)
                    weights(eng, g, QS - 1)
                    eng.wait_ge(w_done, g * QS + QS)
                    eng.sem_inc(selected, 1)
                eng.wait_ge(turned, t + 1)
                turned_sums = m.ps[1][:, :].rearrange("p (k c) -> p k c", c=P)
                sums = sm.rearrange("p (k c) -> p k c", c=P)
                eng.tensor_tensor(sums, turned_sums, gt.unsqueeze(2).to_broadcast([P, KB, P]), ALU.mult).then_inc(dve, 1)
                eng.wait_ge(dve, t * 2 + 1)
                xs = m.x[:, :, bass.ds(t * P, P)]
                eng.tensor_tensor(xs, xs, sums, ALU.add).then_inc(dve, 1)
                eng.wait_ge(dve, t * 2 + 2)
                eng.sem_inc(x_out, 1)

        @block.scalar
        def _(eng):
            with eng.Fori(0, TILES) as t:
                with eng.Fori(0, GROUPS_T) as tg:
                    g = t * GROUPS_T + tg
                    for q in range(QS):
                        a = slice(SUB * q, SUB * q + SUB)
                        eng.wait_ge(hid_done, g * QS + (q + 1))
                        eng.activation(gel[:, a], hid[:, a], ACT.Gelu).then_inc(gel_done, 1)
                        if q > 0:
                            diag(eng, g, q - 1)
                        if q == 4:
                            eng.wait_ge(shifted, g + 1)
                            eng.activation(w.ex, w.ex, ACT.Exp).then_inc(exped, 1)
                    diag(eng, g, QS - 1)
                eng.wait_ge(summed, t + 1)
                eng.wait_ge(x_out, t + 1)
                for i in range(2):
                    eng.activation(sm[:, 512 * i:512 * i + 512], m.bank(i), ACT.Copy).then_inc(sum_out, 1)

        @block.tensor
        def _(eng):
            eng.wait_ge(zeroed, 1)
            eng.sem_inc(v_free, RING)
            with eng.Fori(0, TILES) as t:
                for i in range(2):
                    eng.matmul(m.bank(i), zero[:, 0:P], zero, start=True, stop=False)
                with eng.Fori(0, GROUPS_T) as tg:
                    g = t * GROUPS_T + tg
                    for i in range(GROUP):
                        r = i % RING
                        eng.wait_ge(v_in[r], before + g * (16 * (GROUP // RING)) + 16 * (i // RING + 1))
                        eng.wait_ge(dg_done, g * GROUP + (i + 1))
                        for j in range(2):
                            mm = eng.matmul(m.bank(j), dg[:, r, :], vb[:, r, 512 * j:512 * j + 512], start=False, stop=False)
                        mm.then_inc(v_free, 1)
                for i in range(2):
                    mm = eng.matmul(m.bank(i), zero[:, 0:P], zero, start=False, stop=True)
                mm.then_inc(summed, 1)
                eng.wait_ge(sum_out, t * 2 + 2)
                for k in range(KB):
                    mm = eng.transpose(m.ps[1][:, P * k:P * k + P], sm[:, P * k:P * k + P], m.ident[:, :])
                mm.then_inc(turned, 1)
    st.close()

def program(nc, dram):
    with ExitStack() as ctx:
        m = Model(nc, ctx, dram)
        stage_constants(m)
        stage_load_x(m)
        with nc.Fori(0, LAYERS) as l:
            stage_params(m, l)
            stage_modulation(m, l)
            stage_norm(m, 0)
            stage_lowrank(m, l)
            with nc.Fori(0, KB) as hp:
                stage_rwkv(m, l, hp)
            stage_branches(m, l)
            with nc.Fori(0, KB) as db:
                stage_merge(m, l, db)
            with nc.Fori(0, 2) as half:
                stage_out(m, l, half)
            stage_norm(m, 1)
            stage_tokens_first(m)
            with nc.Fori(0, 4) as quarter:
                stage_scores(m, l, quarter)
            stage_select_first(m)
            stage_retrieve(m, l)
        stage_norm(m, 2)
        stage_tokens_first(m, store=True)


_OUTS = [("y_prompt", (1, CTX, D)), ("y_sample", (1, LAT, D)), ("new_state", (1, LAYERS, 2, 16, HD, HD))]


def kernel(**inputs):
    import numpy as np
    import concourse.bacc as bacc
    from concourse.bass_utils import run_bass_kernel_spmd

    nc = bacc.Bacc("TRN2", target_bir_lowering=False, num_devices=1)
    arrays, dram = {}, {}
    for name, value in inputs.items():
        a = np.ascontiguousarray(value)
        arrays[name] = a
        dram[name] = nc.dram_tensor(name, a.shape, mybir.dt.from_np(a.dtype), kind="ExternalInput").ap()
    for name, shape in _OUTS:
        dram[name] = nc.dram_tensor(name, shape, F32, kind="ExternalOutput").ap()
    program(nc, dram)
    r = run_bass_kernel_spmd(nc, [arrays], core_ids=[0])
    return tuple(r.results[0][name] for name, _ in _OUTS)
```

```python
from contextlib import ExitStack

import concourse.bass as bass
from concourse import mybir

F32 = mybir.dt.float32
U32 = mybir.dt.uint32
ALU = mybir.AluOpType
ACT = mybir.ActivationFunctionType
AX = mybir.AxisListType

P = 128
D = 1024
KB = D // P
LAT, CTX = 512, 128
T = LAT + CTX
TILES = T // P
LAYERS = 2
HD = 64
CH = 64
NCH, NLAT, NCTX = T // CH, LAT // CH, CTX // CH
GRID_W = 64
ROWS = LAT // GRID_W
TAPS = 31
HEADS_Q, KEYS, TOPK, EXPERTS = 8, 128, 16, 16384
SLOTS = HEADS_Q * TOPK
EPS, GN_EPS, LN_EPS = 1e-6, 64e-5, 1e-5
DECAY = 0.6065306597126334
B_R, B_K, B_V, B_LO, B_POOL, B_CONV, B_GATE = 0, 8, 16, 24, 27, 31, 39
R_ADA, R_MU, R_W0, R_A0, R_KK, R_KA = 0, 48, 75, 91, 107, 115
R_N1, R_N2, R_RK, R_GNG, R_GNB, R_PB, R_PS, R_CB, R_LG, R_LB, R_C, R_CC, R_FG = 0, 8, 16, 24, 32, 40, 44, 48, 52, 56, 60, 68, 76
SH1, SC1, GT1, SH2, SC2, GT2 = range(6)
SEGMENTS = ((0, LAT), (LAT, CTX))
WRING = 5
RING = 8
GROUPS = ((0, 4), (4, 4), (8, 2))
PAIRS = tuple((c, 2) for c in range(0, NCH, 2))


class Chain:

    def __init__(self, eng, sem):
        self.eng, self.sem, self.n = eng, sem, 0

    def __call__(self, ins):
        self.n += 1
        ins.then_inc(self.sem, 1)
        self.eng.wait_ge(self.sem, self.n)


class Stage:

    def __init__(self, nc, name):
        self.nc, self.name, self.ctx, self.nums = nc, name, ExitStack(), []

    def sem(self, name):
        s = self.ctx.enter_context(self.nc.semaphore(f"{self.name}_{name}"))
        self.nums.append(s.num)
        return s

    def close(self):
        self.nc.all_engine_barrier()
        nums = sorted(self.nums)
        runs = [n for n in nums if n - 1 not in nums]
        for n in runs:
            end = n
            while end in nums:
                end += 1
            self.nc.gpsimd.sem_clear(range(n, end))
        self.nc.all_engine_barrier()
        self.ctx.close()


class Model:

    def __init__(self, nc, ctx, dram):
        self.nc, self.dram = nc, dram

        def sb(name, shape, dt=F32):
            return ctx.enter_context(nc.sbuf_tensor(name, shape, dt))

        self.x = sb("x", [P, KB, T])
        self.h = sb("h", [P, KB, T])
        self.ya = sb("ya", [P, KB, T])
        self.lo = sb("lo", [P, 3, T])
        self.w = sb("w", [P, WRING, KB, P])
        self.par = sb("par", [P, 3, P])
        self.mod = sb("mod", [P, 6, KB, 2])
        self.scale = sb("scale", [P, 2, KB, 2])
        self.silu_c = sb("silu_c", [P, KB, 2])
        self.ident = sb("ident", [P, P])
        self.ones = sb("ones", [P, P])
        self.block = sb("block", [P, 7, P])
        self.level = sb("level", [P, 6, P])
        self.tri = sb("tri", [P, 2, P])
        self.trid = sb("trid", [P, 2, CH])
        self.reset = sb("reset", [P, NCH, CH])
        self.eps = sb("eps", [P, 4])
        self.row0 = sb("row0", [P, 1])
        self.gate2 = sb("gate2", [P, TILES, KB])
        self.arena = sb("arena", [P, 27008])
        self.used = 0
        self.u_in = [ctx.enter_context(nc.semaphore(f"u_landed{i}")) for i in range(RING)]
        self.v_in = [ctx.enter_context(nc.semaphore(f"v_landed{i}")) for i in range(RING)]
        self.qkv_in = [ctx.enter_context(nc.semaphore(f"rwkv_weights{i}")) for i in range(3)]
        self.ps = [ctx.enter_context(nc.psum_tensor(f"ps{i}", [P, 1024], F32)) for i in range(4)]
        self.w_in = dram["w_in"].rearrange("l (k p) (b c) -> l b p k c", p=P, c=P)

    def load_rwkv_weights(self, eng, l, hp, i):
        eng.dma_start(self.w[:, i], self.w_in[l, hp + (B_K, B_R, B_V)[i]]).then_inc(self.qkv_in[i], 16)

    def wait_rwkv_weights(self, eng, l, hp, i):
        eng.wait_ge(self.qkv_in[i], l * (16 * (KB + 1)) + (hp * 16 + 16))

    def bank(self, n):
        return self.ps[n // 2][:, 512 * (n % 2):512 * (n % 2) + 512]

    def take(self, *shape):
        n = 1
        for s in shape:
            n *= s
        a = self.arena[:, self.used:self.used + n]
        self.used += n
        assert self.used <= self.arena.shape[1], self.used
        if len(shape) == 2:
            a = a.rearrange("p (a b) -> p a b", b=shape[1])
        if len(shape) == 3:
            a = a.rearrange("p (a b c) -> p a b c", b=shape[1], c=shape[2])
        return a


def stage_constants(m):
    nc = m.nc
    st = Stage(nc, "const")
    pool, dve, ready = st.sem("pool"), st.sem("dve"), st.sem("blocks_ready")
    with nc.Block() as block:
        @block.gpsimd
        def _(eng):
            ch = Chain(eng, pool)
            ch(eng.memset(m.ones[:, :], 1.0))
            ch(eng.memset(m.block[:, :, :], 1.0))
            for i in range(7):
                b = 1 << i
                v = m.block[:, i, :].rearrange("p (n b) -> p n b", b=b)
                ch(eng.affine_select(out=v, in_=v, compare_op=ALU.is_ge, fill=0.0, base=0,
                                     pattern=[[-b, P // b], [0, b]], channel_multiplier=1))
                ch(eng.affine_select(out=v, in_=v, compare_op=ALU.is_ge, fill=0.0, base=b - 1,
                                     pattern=[[b, P // b], [0, b]], channel_multiplier=-1))
            ch(eng.tensor_copy(m.ident[:, :], m.block[:, 0, :]))
            for i in range(2):
                ch(eng.tensor_copy(m.tri[:, i, :], m.block[:, 6, :]))
            ch(eng.affine_select(out=m.tri[:, 0, :], in_=m.tri[:, 0, :], compare_op=ALU.is_ge, fill=0.0,
                                 base=-1, pattern=[[1, P]], channel_multiplier=-1))
            ch(eng.affine_select(out=m.tri[:, 1, :], in_=m.tri[:, 1, :], compare_op=ALU.is_ge, fill=0.0,
                                 base=-1, pattern=[[-1, P]], channel_multiplier=1))
            ch(eng.memset(m.reset[:, :, :], 1.0))
            ch(eng.memset(m.reset[:, :, 0:1], 0.0))
            for i, e in enumerate((EPS, GN_EPS, LN_EPS)):
                ch(eng.memset(m.eps[:, i:i + 1], e))
            ch(eng.memset(m.row0[:, :], -float(EXPERTS)))
            eng.sem_inc(ready, 1)

        @block.vector
        def _(eng):
            ch = Chain(eng, dve)
            eng.wait_ge(ready, 1)
            for i in range(6):
                ch(eng.tensor_tensor(m.level[:, i, :], m.block[:, i + 1, :], m.block[:, i, :], ALU.subtract))
            for i in range(2):
                ch(eng.tensor_tensor(m.trid[:, i, :], m.tri[:, i, 0:CH], m.tri[:, i, CH:P], ALU.add))
                ch(eng.tensor_tensor(m.trid[:, i, :], m.trid[:, i, :], m.ident[:, 0:CH], ALU.add))
                ch(eng.tensor_tensor(m.trid[:, i, :], m.trid[:, i, :], m.ident[:, CH:P], ALU.add))
    st.close()


def stage_load_x(m):
    nc, d = m.nc, m.dram
    st = Stage(nc, "load")
    landed, turned, copied = st.sem("landed"), st.sem("turned"), st.sem("copied")
    m.used = 0
    xt = m.take(TILES, D)
    with nc.Block() as block:
        @block.sync
        def _(eng):
            eng.dma_start(xt[:, 0:4, :], d["x_sample"][0].rearrange("(t p) c -> p t c", p=P)).then_inc(landed, 16)
            eng.dma_start(xt[:, 4, :], d["x_prompt"][0]).then_inc(landed, 16)

        @block.tensor
        def _(eng):
            eng.wait_ge(landed, 32)
            for n in range(TILES * KB // 4):
                t, k0 = n // 2, 4 * (n % 2)
                if n >= 8:
                    eng.wait_ge(copied, n - 7)
                for j in range(4):
                    mm = eng.transpose(m.bank(n % 8)[:, P * j:P * j + P], xt[:, t, P * (k0 + j):P * (k0 + j) + P],
                                       m.ident[:, :])
                mm.then_inc(turned, 1)

        @block.vector
        def _(eng):
            for n in range(TILES * KB // 4):
                t, k0 = n // 2, 4 * (n % 2)
                eng.wait_ge(turned, n + 1)
                eng.tensor_copy(m.x[:, k0:k0 + 4, P * t:P * t + P],
                                m.bank(n % 8).rearrange("p (a b) -> p a b", b=P)).then_inc(copied, 1)
    st.close()


def stage_params(m, l):
    nc, d = m.nc, m.dram
    st = Stage(nc, "par")
    landed, turned, copied, sig, dve = (st.sem(n) for n in ("landed", "turned", "copied", "sigmoid", "dve"))
    m.used = 0
    rows = m.take(3, P)
    t1 = m.take(KB, 2)

    def vec(name):
        a = d[name][l]
        if len(a.shape) == 1:
            return a.rearrange("(b c) -> b c", c=P)
        if name == "r_k":
            return a.rearrange("h k -> (h k)").rearrange("(b c) -> b c", c=P)
        return a.rearrange("a (b c) -> (a b) c", c=P)

    loads = [(0, R_ADA, vec("ada_b")), (0, R_MU, vec("shift_mu")), (0, R_W0, vec("decay_w0")),
             (0, R_A0, vec("iclr_a0")), (0, R_KK, vec("k_k")), (0, R_KA, vec("k_a")),
             (1, R_N1, vec("norm1_g")), (1, R_N2, vec("norm2_g")), (1, R_RK, vec("r_k")), (1, R_GNG, vec("gn_g")),
             (1, R_GNB, vec("gn_b")), (1, R_PB, vec("pool_b")), (1, R_PS, vec("pool_scale")),
             (1, R_CB, vec("conv_b")), (1, R_LG, vec("cln_g")), (1, R_LB, vec("cln_b")),
             (1, R_C, d["c"].rearrange("a (b c) -> (a b) c", c=P)),
             (1, R_CC, d["c_ctx"].rearrange("(b c) -> b c", c=P)),
             (1, R_FG, d["final_g"].rearrange("(b c) -> b c", c=P)),
             (2, 0, vec("conv_w"))]
    sizes = (R_KA + KB, R_FG + KB, TAPS * 4)
    with nc.Block() as block:
        def load(eng, part):
            for tile, r, src in part:
                eng.dma_start(rows[r:r + src.shape[0], tile, :], src).then_inc(landed, 16)

        @block.sync
        def _(eng):
            load(eng, loads[0::2])

        @block.tensor
        def _(eng):
            eng.wait_ge(landed, 16 * len(loads))
            for i, n in enumerate(sizes):
                mm = eng.transpose(m.bank(0)[:, P * i:P * i + n], rows[0:n, i, :], m.ident[0:n, 0:n])
            mm.then_inc(turned, 1)

        @block.scalar
        def _(eng):
            load(eng, loads[1::2])
            eng.wait_ge(copied, 1)
            for i, r in enumerate((R_C, R_CC)):
                eng.activation(t1[:, :, i], m.par[:, 1, r:r + KB], ACT.Sigmoid).then_inc(sig, 1)

        @block.vector
        def _(eng):
            ch = Chain(eng, dve)
            eng.wait_ge(turned, 1)
            for i, n in enumerate(sizes):
                ch(eng.tensor_copy(m.par[:, i, 0:n], m.bank(0)[:, P * i:P * i + n]))
            eng.sem_inc(copied, 1)
            eng.wait_ge(sig, 2)
            for i, r in enumerate((R_C, R_CC)):
                ch(eng.tensor_tensor(m.silu_c[:, :, i], t1[:, :, i], m.par[:, 1, r:r + KB], ALU.mult))
    st.close()


def stage_modulation(m, l):
    nc = m.nc
    ada = m.dram["ada_w"].rearrange("l (k p) (s c) -> l s p k c", p=P, c=D)
    st = Stage(nc, "mod")
    landed = [st.sem(f"w{i}") for i in range(2)]
    done, copied, turned, dve = (st.sem(n) for n in ("done", "copied", "turned", "dve"))
    m.used = 0
    w = [m.take(KB, D) for i in range(2)]
    rows = m.take(6, D)
    with nc.Block() as block:
        @block.sync
        def _(eng):
            with eng.Fori(0, 3) as s:
                for i in range(2):
                    eng.wait_ge(done, s * 2 + (i + 1))
                    for k in (0, KB // 2):
                        eng.dma_start(w[i][:, k:k + KB // 2, :], ada[l, s * 2 + i][:, k:k + KB // 2, :])\
                           .then_inc(landed[i], 16)

        @block.tensor
        def _(eng):
            eng.sem_inc(done, 2)
            with eng.Fori(0, 3) as s:
                for i in range(2):
                    eng.wait_ge(landed[i], s * 32 + 32)
                    eng.wait_ge(copied, s * 2 + (i + 1))
                    for c0 in (0, 512):
                        for k in range(KB):
                            mm = eng.matmul(m.ps[i][0:2, c0:c0 + 512], m.silu_c[:, k, :], w[i][:, k, c0:c0 + 512],
                                            start=(k == 0), stop=(k == KB - 1))
                    mm.then_inc(done, 1)
            eng.wait_ge(copied, 8)
            for n in range(6 * KB):
                mm = eng.transpose(m.bank(4)[:, 2 * n:2 * n + 2], rows[0:2, n // KB, P * (n % KB):P * (n % KB) + P],
                                   m.ident[0:2, 0:2])
            mm.then_inc(turned, 1)

        @block.vector
        def _(eng):
            ch = Chain(eng, dve)
            eng.sem_inc(copied, 2)
            with eng.Fori(0, 3) as s:
                for i in range(2):
                    eng.wait_ge(done, s * 2 + (i + 3))
                    eng.tensor_copy(rows[0:2, s * 2 + i, :], m.ps[i][0:2, :]).then_inc(copied, 1)
            eng.wait_ge(turned, 1)
            mod = m.mod[:, :, :, :].rearrange("p s b c -> p (s b) c")
            turned_rows = m.bank(4)[:, 0:12 * KB].rearrange("p (b c) -> p b c", c=2)
            bias = m.par[:, 0, R_ADA:R_ADA + 6 * KB].unsqueeze(2).to_broadcast([P, 6 * KB, 2])
            ch(eng.tensor_tensor(mod, turned_rows, bias, ALU.add))
            for i, (sec, r) in enumerate(((SC1, R_N1), (SC2, R_N2))):
                gain = m.par[:, 1, r:r + KB].unsqueeze(2).to_broadcast([P, KB, 2])
                ch(eng.tensor_scalar(m.scale[:, i], m.mod[:, sec], 1.0, None, ALU.add))
                ch(eng.tensor_tensor(m.scale[:, i], m.scale[:, i], gain, ALU.mult))
            ch(eng.tensor_scalar(m.row0[:, :], m.row0[:, :], float(EXPERTS), None, ALU.add))
            for t in range(TILES):
                ch(eng.tensor_copy(m.gate2[:, t, :], m.mod[:, GT2, :, int(t >= LAT // P)]))
    st.close()


def stage_norm(m, which):
    nc = m.nc
    st = Stage(nc, "norm")
    squared, summed, rooted, scaled = (st.sem(n) for n in ("squared", "summed", "rooted", "scaled"))
    dve = st.sem("dve")
    m.used = 0
    sq, root = m.take(KB, T), m.take(T)
    with nc.Block() as block:
        @block.scalar
        def _(eng):
            for k in range(KB):
                eng.activation(sq[:, k, :], m.x[:, k, :], ACT.Square).then_inc(squared, 1)
            eng.wait_ge(summed, 1)
            eng.activation(root[:, :], m.ps[0][:, 0:T], ACT.Sqrt, scale=1.0 / D, bias=m.eps[:, 0:1])\
               .then_inc(rooted, 1)
            for k in range(KB):
                eng.wait_ge(scaled, k + 1)
                if which == 2:
                    eng.activation(m.h[:, k, :], sq[:, k, :], ACT.Copy, scale=m.par[:, 1, R_FG + k:R_FG + k + 1])
                    continue
                for i, (c0, n) in enumerate(SEGMENTS):
                    eng.activation(m.h[:, k, c0:c0 + n], sq[:, k, c0:c0 + n], ACT.Identity,
                                   scale=m.scale[:, which, k, i:i + 1],
                                   bias=m.mod[:, (SH1, SH2)[which], k, i:i + 1])

        @block.tensor
        def _(eng):
            for k in range(KB):
                eng.wait_ge(squared, k + 1)
                for c0, n in SEGMENTS:
                    mm = eng.matmul(m.ps[0][:, c0:c0 + n], m.ones[:, :], sq[:, k, c0:c0 + n],
                                    start=(k == 0), stop=(k == KB - 1))
            mm.then_inc(summed, 1)

        @block.vector
        def _(eng):
            ch = Chain(eng, dve)
            eng.wait_ge(rooted, 1)
            ch(eng.reciprocal(root[:, :], root[:, :]))
            for k in range(KB):
                eng.tensor_tensor(sq[:, k, :], m.x[:, k, :], root[:, :], ALU.mult).then_inc(scaled, 1)
    st.close()

def shift_mix(m, ch, pad, tmp, mu, dst):
    eng = ch.eng
    n = T + 2
    ch(eng.tensor_tensor(tmp, pad[:, 0:n], pad[:, 2:n + 2], ALU.add))
    ch(eng.scalar_tensor_tensor(out=tmp, in0=tmp, scalar=0.5, in1=pad[:, 1:n + 1],
                                op0=ALU.mult, op1=ALU.subtract))
    for c0, w, off in ((0, LAT, 0), (LAT, CTX, 2)):
        ch(eng.scalar_tensor_tensor(out=dst[:, c0:c0 + w], in0=tmp[:, c0 + off:c0 + off + w], scalar=mu,
                                    in1=pad[:, c0 + off + 1:c0 + off + 1 + w], op0=ALU.mult, op1=ALU.add))


def pad_edges(eng, pad):
    return [eng.memset(pad[:, 0:1], 0.0), eng.memset(pad[:, LAT + 1:LAT + 3], 0.0),
            eng.memset(pad[:, T + 3:T + 4], 0.0)]


def project(eng, m, psum, slot, src, blocks=range(KB)):
    for k in blocks:
        for c0, n in SEGMENTS:
            mm = eng.matmul(psum[:, c0:c0 + n], m.w[:, slot, k, :], src[:, k, c0:c0 + n],
                            start=(k == 0), stop=(k == KB - 1))
    return mm


def stage_lowrank(m, l):
    nc = m.nc
    st = Stage(nc, "lo")
    landed = [st.sem(f"w{i}") for i in range(3)]
    projected, padded, mixed, dve = (st.sem(n) for n in ("projected", "padded", "mixed", "dve"))
    m.used = 0
    pad, tmp, mix = m.take(3, T + 4), m.take(T + 2), m.take(3, T)
    with nc.Block() as block:
        @block.sync
        def _(eng):
            for i in range(3):
                eng.dma_start(m.w[:, i], m.w_in[l, B_LO + i]).then_inc(landed[i], 16)
            for i in range(3):
                eng.wait_ge(projected, i + 1)
                m.load_rwkv_weights(eng, l, 0, i)

        @block.tensor
        def _(eng):
            for i in range(3):
                eng.wait_ge(landed[i], 16)
                project(eng, m, m.ps[i], i, m.h).then_inc(projected, 1)

        @block.scalar
        def _(eng):
            for i in range(3):
                eng.wait_ge(projected, i + 1)
                for c0, n, off in ((0, LAT, 1), (LAT, CTX, 3)):
                    eng.activation(pad[:, i, c0 + off:c0 + off + n], m.ps[i][:, c0:c0 + n], ACT.Copy)\
                       .then_inc(padded, 1)
            for i, f in enumerate((ACT.Tanh, ACT.Copy, ACT.Sigmoid)):
                eng.wait_ge(mixed, i + 1)
                eng.activation(m.lo[:, i, :], mix[:, i, :], f)

        @block.vector
        def _(eng):
            ch = Chain(eng, dve)
            for i in range(3):
                for ins in pad_edges(eng, pad[:, i]):
                    ch(ins)
                eng.wait_ge(padded, 2 * i + 2)
                mu = m.par[:, 0, R_MU + B_LO + i:R_MU + B_LO + i + 1]
                shift_mix(m, ch, pad[:, i], tmp, mu, mix[:, i])
                eng.sem_inc(mixed, 1)
    st.close()


def stage_rwkv(m, l, hp):
    nc, d = m.nc, m.dram
    st = Stage(nc, "rwkv")
    s = st.sem
    small, projected, padded, nrm, ss_done, rooted, act = (
        s(n) for n in ("small", "projected", "padded", "kk_squared", "kk_summed", "kk_rooted", "act"))
    dve, pool, mixed, zeroed = s("dve"), s("pool"), s("mixed"), s("zeroed")
    g_done, za, sg, qe, exps = s("g_done"), s("za"), s("sigmoids"), s("qe"), s("exps")
    vbd_ready, bd_ready = s("v_ready"), s("operands_ready")
    t_dve, t_act, t_done = s("products_out_dve"), s("products_out_act"), s("products_done")
    d1, lx, lxe, ld_, lde, lte, ldt = (
        s(n) for n in ("inverse_start", "x_done", "x_out", "dt_done", "d_out", "dt_out", "d_turned"))
    p_done, p_act, p_dve = s("post_done"), s("post_out_act"), s("post_out_dve")
    s_in, s_turned, s_set = s("state_in"), s("state_turned"), s("state_set")
    s_done, s_out, y_done, y_out = s("s_done"), s("s_out"), s("y_done"), s("y_out")
    f_turned, f_out, stored = s("final_turned"), s("final_out"), s("final_stored")
    gsum, yc_ready, gsq, groot = s("y_summed"), s("y_centred"), s("y_squared"), s("gn_rooted")
    second = s("second_operands")
    q_ready, spread, widened = s("bonus_ready"), s("spread"), s("widened")

    m.used = 0
    par = m.take(13)
    wc = m.take(2, NCH)
    by_tok = m.take(TILES, 2)
    pad, tmp = m.take(T + 4), m.take(T + 2)
    r, k, v, nkk = (m.take(T) for _ in range(4))
    sig, q, e, a = (m.take(T) for _ in range(4))
    x1, x2, x3 = (m.take(T) for _ in range(3))
    free_w = m.w[:, 3:5].rearrange("p s k c -> p (s k c)")
    kds, ys, gate = (free_w[:, T * i:T * i + T] for i in range(3))
    ws = m.take(3, P)
    ar, b_rb = m.take(NCH, P + CH), m.take(NCH, P + CH)
    a_bd, rt, b_tok, rbt = ar[:, :, 0:P], ar[:, :, P:], b_rb[:, :, 0:P], b_rb[:, :, P:]
    b_bd, k_bd, v_bd = (m.take(NCH, P) for _ in range(3))
    a_tok, k_tok, v_tok = (m.take(NCH, P) for _ in range(3))
    akt, dd, dt, abt = (m.take(NCH, P) for _ in range(4))
    rkt = m.take(NCH, CH)
    s_raw = m.take(3, P)
    xx = v_bd
    yy, cc, gg, states = dd, akt, xx, abt
    chunks = lambda t: t.rearrange("p (c t) -> p c t", t=CH)
    w2 = d["decay_w2"].rearrange("l e r (b c) -> l b (e r) c", c=P)
    a2 = d["iclr_a2"].rearrange("l e r (b c) -> l b (e r) c", c=P)
    g2 = d["gate_g2"].rearrange("l r (b c) -> l b r c", c=P)
    heads = ((0, CH), (CH, P))
    BY_DVE = {"b_ar": 2, "k_ar": 2}
    TURNED = {"dd": (dt, dd), "a_tok": (a_bd, a_tok), "b_tok": (b_bd, b_tok), "k_tok": (k_bd, k_tok), "v_tok": (v_bd, v_tok)}

    def products(e_):
        names = ("b_ar", "k_ar") + (("v_tok",) if e_ == 0 else ()) + ("a_tok", "b_tok", "k_tok", "dd", "akv")
        return [(w, c0, n) for w in names for c0, n in (PAIRS if w in ("b_ar", "k_ar") else GROUPS)]

    def out_count(e_, n, by_dve):
        ps = [x[0] for i in range(e_) for x in products(i)] + [x[0] for x in products(e_)[:n]]
        return sum(BY_DVE[w] if by_dve else 1 for w in ps if (w in BY_DVE) == by_dve)

    def done_count(e_):
        return sum(len(products(i)) for i in range(e_))

    steps = [(i, c) for i in range(NLAT) for c in ((0, 1) if i < NCTX else (0,))]
    updates = [x for x in steps if x != (NLAT - 1, 0)]
    NS = len(updates)

    def chunk_of(e_, i, c):
        n, base = ((NLAT, 0), (NCTX, NLAT))[c]
        return base + (i if e_ == 0 else n - 1 - i)

    def state_after(e_, i, c):
        return s_raw[:, 2, :] if (i, c) == (NCTX - 1, 1) else states[:, chunk_of(e_, i + 1, c), :]

    def cols(bank, w, n=P):
        return bank[:, 0:n * w].rearrange("p (c t) -> p c t", t=n)

    def over(mask, w, n=P):
        return mask.unsqueeze(1).to_broadcast([P, w, n])

    def pre_a(eng, ch, e_):
        eng.wait_ge(sg, 2 * e_ + 1)
        ch(eng.tensor_tensor_scan(q, m.reset[:, :, :].rearrange("p c t -> p (c t)"), sig, 0.0, ALU.mult, ALU.add))
        if e_ == 1:
            ch(eng.tensor_tensor(chunks(e), chunks(q)[:, :, CH - 1:CH].to_broadcast([P, NCH, CH]), chunks(q),
                                 ALU.subtract))
            ch(eng.tensor_tensor(q, e, sig, ALU.add))
        else:
            ch(eng.tensor_tensor(e, q, sig, ALU.subtract))
        eng.sem_inc(qe, 1)

    def this_k(eng, ch, e_):
        kd = (kds, a)[e_]
        ch(eng.tensor_scalar(kd, a, par[:, 8:9], par[:, 9:10], ALU.mult, ALU.add))
        ch(eng.tensor_tensor(kd, kd, k, ALU.mult))
        if e_ == 1:
            ch(eng.tensor_tensor(kds, kds, a, ALU.add))

    def kk_a(ch):
        ch(ch.eng.tensor_tensor(sig, nkk, a, ALU.mult))

    def a_operand(eng, ch):
        for p0, p1 in heads:
            ch(eng.tensor_tensor(a_bd[p0:p1, :, p0:p1], chunks(nkk)[p0:p1], chunks(x2)[p0:p1], ALU.mult))

    def b_operand(eng, ch):
        for p0, p1 in heads:
            ch(eng.scalar_tensor_tensor(out=b_bd[p0:p1, :, p0:p1], in0=chunks(sig)[p0:p1], scalar=-1.0,
                                        in1=chunks(x3)[p0:p1], op0=ALU.mult, op1=ALU.mult))

    def second_operands(eng, ch):
        eng.wait_ge(qe, 2)
        eng.wait_ge(sg, 4)
        kk_a(ch)
        ch(eng.tensor_scalar(sig, sig, -1.0, None, ALU.mult))
        this_k(eng, ch, 1)
        eng.wait_ge(lx, 1)
        k_operand(eng, ch, 1)
        a_operand(eng, ch)
        for p0, p1 in heads:
            ch(eng.tensor_tensor(b_bd[p0:p1, :, p0:p1], chunks(sig)[p0:p1], chunks(x3)[p0:p1], ALU.mult))
        eng.sem_inc(second, 1)

    def k_operand(eng, ch, e_):
        eng.wait_ge(exps, 3 * (e_ + 1))
        end = CH - 1 if e_ == 0 else 0
        ch(eng.tensor_copy(wc[:, e_].unsqueeze(2), chunks(x1)[:, :, end:end + 1]))
        for p0, p1 in heads:
            ch(eng.tensor_tensor(k_bd[p0:p1, :, p0:p1], chunks((kds, a)[e_])[p0:p1], chunks(x3)[p0:p1], ALU.mult))

    def r_operand(eng, ch):
        ch(eng.tensor_tensor(rt, chunks(r), chunks(x1), ALU.mult))

    def head_sums(eng, src, done):
        for t in range(TILES):
            mm = eng.matmul(m.ps[0][:, 2 * t:2 * t + 2], src[:, P * t:P * t + P],
                            m.block[:, 6, :].rearrange("p (h c) -> p h c", c=HD)[:, :, 0], start=True, stop=True)
        mm.then_inc(done, 1)

    def widen(eng, ch):
        ch(eng.reciprocal(by_tok, by_tok))
        ch(eng.tensor_copy(tmp[:, 0:T].rearrange("p (t h c) -> p t h c", h=2, c=HD),
                           by_tok.unsqueeze(3).to_broadcast([P, TILES, 2, HD])))
        eng.sem_inc(spread, 1)

    def turn_wide(eng, n):
        eng.wait_ge(spread, n)
        for t in range(TILES):
            mm = eng.transpose(m.ps[0][:, P * t:P * t + P], tmp[:, P * t:P * t + P], m.ident[:, :])
        mm.then_inc(widened, 1)

    def za_product(eng, e_, i, psum):
        h0 = CH * e_
        for c0, n in SEGMENTS:
            mm = eng.matmul(psum[:, c0:c0 + n], ws[h0:h0 + CH, i, :], m.lo[h0:h0 + CH, i, c0:c0 + n],
                            start=True, stop=True)
        mm.then_inc(za, 1)

    def act_sigmoid(eng, e_, i, psum):
        eng.wait_ge(za, 2 * e_ + i + 1)
        eng.activation((sig, a)[i], psum[:, 0:T], ACT.Sigmoid, bias=par[:, 3 + 2 * i + e_:4 + 2 * i + e_])\
           .then_inc(sg, 1)

    def act_exps(eng, e_):
        eng.wait_ge(qe, e_ + 1)
        eng.activation(x2, e, ACT.Exp, scale=-DECAY).then_inc(exps, 1)
        eng.activation(x3, q, ACT.Exp, scale=DECAY).then_inc(exps, 1)
        eng.activation(x1, q, ACT.Exp, scale=-DECAY).then_inc(exps, 1)

    with nc.Block() as block:
        @block.sync
        def _(eng):
            for i, t in enumerate((w2, a2, g2)):
                eng.dma_start(ws[:, i, :], t[l, hp]).then_inc(small, 16)
            eng.wait_ge(zeroed, 1)
            for e_ in range(2):
                if e_ == 1:
                    eng.wait_ge(s_set, 1)
                for i, (p0, p1) in enumerate(heads):
                    src = d["state_rwkv"][0].rearrange("l e (b i) v k -> l e i b v k", i=2)[l, e_, i, hp]
                    eng.dma_start(s_raw[p0:p1, 0, p0:p1], src).then_inc(s_in, 16)
                if e_ == 0:
                    for i in range(3):
                        eng.wait_ge(projected, i + 1)
                        m.load_rwkv_weights(eng, l, hp + 1, i)
            out = d["new_state"][0].rearrange("l e (b i) v k -> l e i b v k", i=2)
            for e_ in range(2):
                eng.wait_ge(f_out, e_ + 1)
                for i, (p0, p1) in enumerate(heads):
                    eng.dma_start(out[l, e_, i, hp], s_raw[p0:p1, 1, p0:p1]).then_inc(stored, 16)
                eng.wait_ge(stored, 32 * (e_ + 1))

        @block.gpsimd
        def _(eng):
            ch = Chain(eng, pool)
            for t in (a_bd, b_bd, k_bd, v_bd, s_raw):
                ch(eng.memset(t[0:CH, :, CH:P], 0.0))
                ch(eng.memset(t[CH:P, :, 0:CH], 0.0))
            eng.sem_inc(zeroed, 1)
            second_operands(eng, ch)

        @block.tensor
        def _(eng):
            m.wait_rwkv_weights(eng, l, hp, 0)
            project(eng, m, m.ps[0], 0, m.h).then_inc(projected, 1)
            eng.wait_ge(small, 48)
            za_product(eng, 0, 0, m.ps[3])
            za_product(eng, 0, 1, m.ps[1])
            m.wait_rwkv_weights(eng, l, hp, 1)
            project(eng, m, m.ps[2], 1, m.h).then_inc(projected, 1)
            eng.wait_ge(nrm, 1)
            head_sums(eng, v, ss_done)
            m.wait_rwkv_weights(eng, l, hp, 2)
            eng.wait_ge(sg, 2)
            project(eng, m, m.ps[1], 2, m.h, range(0, 4))
            turn_wide(eng, 1)
            project(eng, m, m.ps[1], 2, m.h, range(4, KB)).then_inc(projected, 1)
            for c0, n in SEGMENTS:
                mm = eng.matmul(m.ps[3][:, c0:c0 + n], ws[:, 2, :], m.lo[:, 2, c0:c0 + n], start=True, stop=True)
            mm.then_inc(g_done, 1)
            eng.wait_ge(padded, 6)
            for e_ in range(2):
                eng.wait_ge(bd_ready, e_ + 1)
                if e_ == 0:
                    eng.wait_ge(rooted, 2)
                else:
                    eng.wait_ge(f_out, 1)
                    eng.wait_ge(y_out, 1)
                for n, (what, c0, w) in enumerate(products(e_)):
                    if n >= 8:
                        eng.wait_ge(t_dve, out_count(e_, n - 7, True))
                        eng.wait_ge(t_act, out_count(e_, n - 7, False))
                    if what == "akv":
                        eng.wait_ge(t_dve, out_count(e_ + 1, 0, True))
                    if (what, c0) == ("dd", 0):
                        eng.wait_ge(d1, e_ + 1)
                    if (what, c0) == ("v_tok", 0):
                        eng.wait_ge(vbd_ready, 1)
                    width = P + CH if what in ("b_ar", "k_ar") else P
                    for j in range(w):
                        c = c0 + j
                        o = m.bank(n % 8)[:, width * j:width * j + width]
                        if what == "b_ar":
                            mm = eng.matmul(o, b_bd[:, c, :], ar[:, c, :], start=True, stop=True)
                        elif what == "k_ar":
                            mm = eng.matmul(o, k_bd[:, c, :], ar[:, c, :], start=True, stop=True)
                        elif what == "akv":
                            mm = eng.matmul(o, akt[:, c, :], v_tok[:, c, :], start=True, stop=True)
                        else:
                            mm = eng.transpose(o, TURNED[what][0][:, c, :], m.ident[:, :])
                    mm.then_inc(t_done, 1)
                eng.wait_ge(t_dve, out_count(e_ + 1, 0, True))
                eng.wait_ge(t_act, out_count(e_ + 1, 0, False))
                for lv in range(5):
                    n0 = 15 * e_ + 3 * lv
                    for g, (c0, w) in enumerate(GROUPS):
                        if lv > 0:
                            eng.wait_ge(lde, 12 * e_ + 3 * (lv - 1) + g + 1)
                            eng.wait_ge(lte, n0 - 3 + g + 1)
                        for j in range(w):
                            mm = eng.matmul(m.bank(g)[:, P * j:P * j + P], abt[:, c0 + j, :], dd[:, c0 + j, :],
                                            start=True, stop=True)
                        mm.then_inc(lx, 1)
                    for g, (c0, w) in enumerate(GROUPS):
                        eng.wait_ge(lxe, n0 + g + 1)
                        for j in range(w):
                            mm = eng.matmul(m.bank(g)[:, P * j:P * j + P], xx[:, c0 + j, :], dt[:, c0 + j, :],
                                            start=True, stop=True)
                        mm.then_inc(ld_, 1)
                    for g, (c0, w) in enumerate(GROUPS):
                        if lv < 4:
                            eng.wait_ge(lte, n0 + g + 1)
                            for j in range(w):
                                mm = eng.transpose(m.bank(3 + g)[:, P * j:P * j + P], dt[:, c0 + j, :], m.ident[:, :])
                            mm.then_inc(ldt, 1)
                    if e_ == 0 and lv < 2:
                        if lv == 1:
                            eng.wait_ge(sg, 3)
                        za_product(eng, 1, lv, m.ps[3])
                for n, (what, c0, w) in enumerate([("yy", *g) for g in GROUPS] + [("cc", *g) for g in GROUPS]
                                                  + [("gr", *g) for g in PAIRS]):
                    if what == "yy":
                        eng.wait_ge(lte, 15 * e_ + 12 + n + 1)
                    if what == "gr":
                        eng.wait_ge(p_act, 6 * e_ + n - 5)
                    width = P + CH if what == "gr" else P
                    for j in range(w):
                        c, o = c0 + j, m.bank(n % 6)[:, width * j:width * j + width]
                        if what == "yy":
                            mm = eng.matmul(o, dt[:, c, :], a_tok[:, c, :], start=True, stop=True)
                        elif what == "cc":
                            mm = eng.matmul(o, dt[:, c, :], akt[:, c, :], start=True, stop=True)
                        else:
                            mm = eng.matmul(o, yy[:, c, :], b_rb[:, c, :], start=True, stop=True)
                    mm.then_inc(p_done, 1)
                eng.wait_ge(s_in, 32 * (e_ + 1))
                if e_ == 0:
                    eng.wait_ge(sg, 4)
                eng.transpose(m.ps[3][:, 0:P], s_raw[:, 0, :], m.ident[:, :]).then_inc(s_turned, 1)

                def h_part(n):
                    x = chunk_of(e_, *updates[n])
                    if n < 6:
                        eng.wait_ge(p_dve, 10 * (e_ + 1))
                        eng.wait_ge(p_act, 6 * (e_ + 1))
                    else:
                        eng.wait_ge(s_out, NS * e_ + n - 5)
                    eng.matmul(m.bank(n % 6)[:, 0:P], b_tok[:, x, :], cc[:, x, :], start=True, stop=False)
                    eng.matmul(m.bank(n % 6)[:, 0:P], k_tok[:, x, :], v_tok[:, x, :], start=False, stop=False)

                h_part(0)
                h_part(1)
                eng.wait_ge(s_set, e_ + 1)
                for i, c in steps:
                    x = chunk_of(e_, i, c)
                    if i > 0:
                        eng.wait_ge(s_out, NS * e_ + updates.index((i - 1, c)) + 1)
                    if (i, c) in updates:
                        n = updates.index((i, c))
                        eng.matmul(m.bank(n % 6)[:, 0:P], gg[:, x, :], states[:, x, :], start=False, stop=True)\
                           .then_inc(s_done, 1)
                    by = m.ps[3][:, CH * x:CH * x + CH]
                    eng.matmul(by, states[:, x, :], rt[:, x, :], start=True, stop=False)
                    eng.matmul(by, cc[:, x, :], rbt[:, x, :], start=False, stop=False)
                    mm = eng.matmul(by, v_tok[:, x, :], rkt[:, x, :], start=False, stop=True)
                    if (i, c) in updates and n + 2 < NS:
                        h_part(n + 2)
                mm.then_inc(y_done, 1)
                eng.wait_ge(s_out, NS * (e_ + 1))
                eng.transpose(m.bank(0)[:, 0:P], s_raw[:, 2, :], m.ident[:, :]).then_inc(f_turned, 1)
            eng.wait_ge(q_ready, 1)
            eng.wait_ge(f_out, 2)
            for c0, n in SEGMENTS:
                mm = eng.matmul(m.ps[2][:, c0:c0 + n], m.block[:, 6, :], x1[:, c0:c0 + n], start=True, stop=True)
            mm.then_inc(gsum, 1)
            eng.wait_ge(y_out, 2)
            for c0, n in SEGMENTS:
                mm = eng.matmul(m.ps[0][:, c0:c0 + n], m.block[:, 6, :], ys[:, c0:c0 + n], start=True, stop=True)
            mm.then_inc(gsum, 1)
            eng.wait_ge(gsq, 1)
            head_sums(eng, x2, gsum)
            turn_wide(eng, 2)

        @block.scalar
        def _(eng):
            ch = Chain(eng, act)

            def pad_in(i):
                eng.wait_ge(projected, i + 1)
                eng.wait_ge(mixed, i + 1)
                src = m.ps[(0, 2, 1)[i]]
                for c0, n, off in ((0, LAT, 1), (LAT, CTX, 3)):
                    eng.activation(pad[:, c0 + off:c0 + off + n], src[:, c0:c0 + n], ACT.Copy).then_inc(padded, 1)

            pad_in(0)
            act_sigmoid(eng, 0, 0, m.ps[3])
            act_sigmoid(eng, 0, 1, m.ps[1])
            act_exps(eng, 0)
            pad_in(1)
            eng.wait_ge(ss_done, 1)
            eng.activation(by_tok.rearrange("p t h -> p (t h)"), m.ps[0][:, 0:2 * TILES], ACT.Sqrt).then_inc(rooted, 1)
            pad_in(2)
            eng.wait_ge(g_done, 1)
            eng.activation(gate, m.ps[3][:, 0:T], ACT.Copy).then_inc(rooted, 1)
            for e_ in range(2):
                for n, (what, c0, w) in enumerate(products(e_)):
                    if what in BY_DVE:
                        continue
                    eng.wait_ge(t_done, done_count(e_) + n + 1)
                    dst = akt if what == "akv" else TURNED[what][1]
                    eng.activation(dst[:, c0:c0 + w, :], cols(m.bank(n % 8), w), ACT.Copy).then_inc(t_act, 1)
                for lv in range(4):
                    for g, (c0, w) in enumerate(GROUPS):
                        eng.wait_ge(ldt, 12 * e_ + 3 * lv + g + 1)
                        eng.activation(dd[:, c0:c0 + w, :], cols(m.bank(3 + g), w), ACT.Copy).then_inc(lde, 1)
                    if e_ == 0 and lv < 2:
                        act_sigmoid(eng, 1, lv, m.ps[3])
                    if e_ == 0 and lv == 1:
                        act_exps(eng, 1)
                for n in range(6):
                    c0, w = GROUPS[n % 3]
                    eng.wait_ge(p_done, 11 * e_ + n + 1)
                    eng.activation((yy, cc)[n // 3][:, c0:c0 + w, :], cols(m.bank(n), w), ACT.Copy).then_inc(p_act, 1)
                eng.wait_ge(s_turned, e_ + 1)
                ch(eng.activation(states[:, chunk_of(e_, 0, 0), :], m.ps[3][:, 0:P], ACT.Copy))
                ch(eng.activation(states[:, chunk_of(e_, 0, 1), :], m.ident[:, :], ACT.Copy, scale=0.0))
                eng.sem_inc(s_set, 1)
                if e_ == 0:
                    eng.wait_ge(y_done, 1)
                    eng.activation(ys, m.ps[3][:, 0:T], ACT.Copy).then_inc(y_out, 1)
                eng.wait_ge(f_turned, e_ + 1)
                if e_ == 1:
                    eng.wait_ge(stored, 32)
                ch(eng.activation(s_raw[:, 1, :], m.bank(0)[:, 0:P], ACT.Copy))
                eng.sem_inc(f_out, 1)
            eng.wait_ge(yc_ready, 1)
            eng.activation(x2, ys, ACT.Square).then_inc(gsq, 1)
            eng.wait_ge(gsum, 3)
            eng.activation(by_tok.rearrange("p t h -> p (t h)"), m.ps[0][:, 0:2 * TILES], ACT.Sqrt, scale=1.0 / HD,
                           bias=m.eps[:, 1:2]).then_inc(groot, 1)

        @block.vector
        def _(eng):
            ch = Chain(eng, dve)
            for j, (i, r0) in enumerate(((0, R_MU), (0, R_MU + 8), (0, R_MU + 16), (0, R_W0), (0, R_W0 + 8), (0, R_A0),
                                         (0, R_A0 + 8), (0, R_KK), (0, R_KA), (1, R_RK), (1, R_GNG), (1, R_GNB))):
                j = j if j < 9 else j + 1
                ch(eng.tensor_copy(par[:, j:j + 1], m.par[:, i, bass.ds(hp + r0, 1)]))
            ch(eng.tensor_scalar(par[:, 9:10], par[:, 8:9], -1.0, 1.0, ALU.mult, ALU.add))
            for ins in pad_edges(eng, pad):
                ch(ins)
            eng.sem_inc(mixed, 1)
            eng.wait_ge(padded, 2)
            shift_mix(m, ch, pad, tmp, par[:, 1:2], k)
            eng.sem_inc(mixed, 1)
            ch(eng.tensor_scalar(nkk, k, par[:, 7:8], None, ALU.mult))
            ch(eng.tensor_tensor(v, nkk, nkk, ALU.mult))
            eng.sem_inc(nrm, 1)
            pre_a(eng, ch, 0)
            eng.wait_ge(sg, 2)
            this_k(eng, ch, 0)
            eng.wait_ge(zeroed, 1)
            k_operand(eng, ch, 0)
            eng.wait_ge(padded, 4)
            shift_mix(m, ch, pad, tmp, par[:, 0:1], r)
            eng.sem_inc(mixed, 1)
            eng.wait_ge(rooted, 1)
            ch(eng.tensor_scalar(by_tok, by_tok, 1e-12, None, ALU.max))
            widen(eng, ch)
            r_operand(eng, ch)
            eng.wait_ge(widened, 1)
            ch(eng.scalar_tensor_tensor(out=nkk, in0=nkk, scalar=-1.0, in1=m.ps[0][:, 0:T], op0=ALU.mult, op1=ALU.mult))
            kk_a(ch)
            a_operand(eng, ch)
            b_operand(eng, ch)
            eng.sem_inc(bd_ready, 1)
            eng.wait_ge(padded, 6)
            shift_mix(m, ch, pad, tmp, par[:, 2:3], v)
            for p0, p1 in heads:
                ch(eng.tensor_copy(v_bd[p0:p1, :, p0:p1], chunks(v)[p0:p1]))
            eng.sem_inc(vbd_ready, 1)
            for e_ in range(2):
                for n, (what, c0, w) in enumerate(products(e_)):
                    if what not in BY_DVE:
                        continue
                    eng.wait_ge(t_done, done_count(e_) + n + 1)
                    to_a, to_r = ((abt, rbt), (akt, rkt))[what == "k_ar"]
                    src = cols(m.bank(n % 8), w, P + CH)
                    eng.tensor_tensor(to_a[:, c0:c0 + w, :], src[:, :, 0:P], over(m.tri[:, e_], w), ALU.mult)\
                       .then_inc(t_dve, 1)
                    eng.tensor_tensor(to_r[:, c0:c0 + w, :], src[:, :, P:], over(m.trid[:, e_], w, CH), ALU.mult)\
                       .then_inc(t_dve, 1)
                    if (what, c0) == ("b_ar", PAIRS[-1][0]):
                        eng.wait_ge(t_dve, out_count(e_, n + 1, True))
                        ch(eng.tensor_tensor(dt, abt, over(m.level[:, 0], NCH), ALU.mult))
                        ch(eng.tensor_tensor(dt, dt, over(m.ident[:, :], NCH), ALU.add))
                        eng.sem_inc(d1, 1)
                for lv in range(5):
                    n0 = 15 * e_ + 3 * lv
                    for g, (c0, w) in enumerate(GROUPS):
                        eng.wait_ge(lx, n0 + g + 1)
                        eng.tensor_tensor(xx[:, c0:c0 + w, :], cols(m.bank(g), w), over(m.level[:, lv + 1], w), ALU.mult)\
                           .then_inc(lxe, 1)
                    for g, (c0, w) in enumerate(GROUPS):
                        eng.wait_ge(ld_, n0 + g + 1)
                        eng.tensor_tensor(dt[:, c0:c0 + w, :], dt[:, c0:c0 + w, :], cols(m.bank(g), w), ALU.add)\
                           .then_inc(lte, 1)
                    if e_ == 0 and lv == 0:
                        pre_a(eng, ch, 1)
                for n, (c0, w) in enumerate(PAIRS):
                    eng.wait_ge(p_done, 11 * e_ + n + 7)
                    src = cols(m.bank(n), w, P + CH)
                    eng.tensor_tensor(gg[:, c0:c0 + w, :], src[:, :, 0:P], over(m.ident[:, :], w), ALU.add).then_inc(p_dve, 1)
                    eng.tensor_tensor(rt[:, c0:c0 + w, :], rt[:, c0:c0 + w, :], src[:, :, P:], ALU.add).then_inc(p_dve, 1)
                for n, (i, c) in enumerate(updates):
                    x = chunk_of(e_, i, c)
                    eng.wait_ge(s_done, NS * e_ + n + 1)
                    eng.tensor_scalar(state_after(e_, i, c), m.bank(n % 6)[:, 0:P], wc[:, e_, x:x + 1], None, ALU.mult)\
                       .then_inc(s_out, 1)
                eng.wait_ge(y_done, e_ + 1)
                if e_ == 0:
                    eng.wait_ge(second, 1)
                    r_operand(eng, ch)
                    eng.sem_inc(bd_ready, 1)
                else:
                    eng.tensor_tensor(ys, ys, m.ps[3][:, 0:T], ALU.add).then_inc(y_out, 1)
            ch(eng.scalar_tensor_tensor(out=x1, in0=kds, scalar=par[:, 10:11], in1=r, op0=ALU.mult, op1=ALU.mult))
            eng.sem_inc(q_ready, 1)
            eng.wait_ge(gsum, 2)
            ch(eng.scalar_tensor_tensor(out=ys, in0=m.ps[0][:, 0:T], scalar=-1.0 / HD, in1=ys,
                                        op0=ALU.mult, op1=ALU.add))
            eng.sem_inc(yc_ready, 1)
            ch(eng.tensor_tensor(v, v, m.ps[2][:, 0:T], ALU.mult))
            eng.wait_ge(groot, 1)
            widen(eng, ch)
            eng.wait_ge(widened, 2)
            ch(eng.tensor_tensor(ys, ys, m.ps[0][:, 0:T], ALU.mult))
            ch(eng.tensor_scalar(ys, ys, par[:, 11:12], par[:, 12:13], ALU.mult, ALU.add))
            ch(eng.tensor_tensor(ys, ys, v, ALU.add))
            ch(eng.tensor_tensor(ys, ys, gate, ALU.mult))
            ch(eng.tensor_copy(m.ya[:, hp, :], ys))
    st.close()

def stage_branches(m, l):
    nc, d = m.nc, m.dram
    st = Stage(nc, "br")
    s = st.sem
    landed = [s(f"w{i}") for i in range(WRING)]
    pw_in, used, out_act, zeroed, pooled, mixed = (
        s(n) for n in ("pool_w", "projected", "taken_out", "zeroed", "pooled", "pool_mixed"))
    dve, pool, act, gated, conv, cen, sums, sq_done, rooted, norm, sgm = (
        s(n) for n in ("dve", "pool", "act", "gated", "convolved", "centred", "sums", "squares", "rooted", "normed",
                       "sigmoids"))
    pool_bias, diags, conv_pe = s("pool_bias"), s("diagonals"), s("convolved_by_tensor")
    m.used = 0
    yb, yc = m.take(4, T), m.take(4, T)
    HALO = 8
    NL, NC_ = (ROWS + 2 * HALO) * GRID_W, CTX + 2 * HALO
    za, zb = m.take(4, NL + NC_), m.take(2, NL + NC_)
    cnt = m.take(3, ROWS + 2 * HALO + NC_)
    pw = m.take(4, P)
    HT = TAPS // 2
    RW = GRID_W + 2 * HT
    uc = m.take(4, ROWS * RW + CTX + 2 * HT)
    ga, gv = m.take(2, T), m.take(2, T)
    TT = 11
    dg = [m.take(TT, P) for i in range(2)]
    root = ga[:, 0]
    pbs = m.take(4)
    NPROJ = 12
    cols = [B_POOL + i for i in range(4)]
    for i in range(4):
        cols += [B_CONV + 4 + i, B_CONV + i]

    def lat(t):
        return t[:, 0:NL]

    def ctx(t):
        return t[:, NL:NL + NC_]

    def lat_u(g):
        return uc[:, g, 0:ROWS * RW].rearrange("p (r w) -> p r w", w=RW)

    def ctx_u(g):
        return uc[:, g, ROWS * RW:]

    def grid(t):
        return t.rearrange("p (r w) -> p r w", w=GRID_W)

    def tap(t, g):
        return m.par[:, 2, 4 * t + g:4 * t + g + 1]

    def add_sums(eng, ch, g):
        eng.wait_ge(conv_pe, g + 1)
        ch(eng.tensor_tensor(yc[:, g, :], yc[:, g, :], m.ps[g % 3][:, 0:T], ALU.add))
        eng.sem_inc(conv, 1)

    def pool_maps(eng):
        eng.wait_ge(pw_in, 16)
        for g in range(4):
            eng.wait_ge(pooled, g + 1)
            if g > 0:
                eng.wait_ge(mixed, g)
            for c0, w in SEGMENTS:
                mm = eng.matmul(m.ps[3][:, c0:c0 + w], pw[:, g, :], za[:, g, c0:c0 + w], start=True, stop=True)
            mm.then_inc(sums, 1)

    with nc.Block() as block:
        @block.sync
        def _(eng):
            for i in range(3):
                m.wait_rwkv_weights(eng, l, KB, i)
            for n, b in enumerate(cols):
                if n == 4:
                    eng.dma_start(pw, d["pool_w"].rearrange("l g c e -> l c g e")[l]).then_inc(pw_in, 16)
                if n >= WRING:
                    eng.wait_ge(used, n - WRING + 1)
                eng.dma_start(m.w[:, n % WRING], m.w_in[l, b]).then_inc(landed[n % WRING], 16)

        @block.gpsimd
        def _(eng):
            ch = Chain(eng, pool)
            for t in [za[:, i] for i in range(4)]:
                ch(eng.memset(t[:, 0:HALO * GRID_W], 0.0))
                ch(eng.memset(t[:, (HALO + ROWS) * GRID_W:NL + HALO], 0.0))
                ch(eng.memset(t[:, NL + HALO + CTX:NL + NC_], 0.0))
            ch(eng.memset(uc, 0.0))
            ch(eng.memset(cnt, 0.0))
            ch(eng.memset(cnt[:, 0, HALO:HALO + ROWS], 1.0))
            ch(eng.memset(cnt[:, 0, ROWS + 3 * HALO:ROWS + 3 * HALO + CTX], 1.0))
            eng.sem_inc(zeroed, 1)
            for g in range(4):
                eng.wait_ge(out_act, 6 + 2 * g)
                ch(eng.tensor_tensor(lat_u(g)[:, :, HT:HT + GRID_W], grid(ga[:, g % 2, 0:LAT]),
                                     grid(gv[:, g % 2, 0:LAT]), ALU.mult))
                ch(eng.tensor_tensor(ctx_u(g)[:, HT:HT + CTX], ga[:, g % 2, LAT:T], gv[:, g % 2, LAT:T], ALU.mult))
                eng.sem_inc(gated, 1)

        @block.tensor
        def _(eng):
            for n in range(NPROJ):
                eng.wait_ge(landed[n % WRING], 16 * (n // WRING + 1))
                if n >= 3:
                    eng.wait_ge(out_act, n - 2)
                project(eng, m, m.ps[n % 3], n % WRING, m.h).then_inc(used, 1)
            for g in range(4):
                if g == 2:
                    pool_maps(eng)
                eng.wait_ge(gated, g + 1)
                if g == 3:
                    eng.wait_ge(conv, 1)
                for t in range(TT):
                    eng.wait_ge(diags, TT * g + t + 1)
                    eng.matmul(m.ps[g % 3][:, 0:LAT], dg[g % 2][:, t, :], lat_u(g)[:, :, t:t + GRID_W],
                               start=(t == 0), stop=(t == TT - 1))
                    mm = eng.matmul(m.ps[g % 3][:, LAT:T], dg[g % 2][:, t, :], ctx_u(g)[:, t:t + CTX],
                                    start=(t == 0), stop=(t == TT - 1))
                mm.then_inc(conv_pe, 1)
            eng.wait_ge(out_act, NPROJ)
            eng.wait_ge(conv, 4)
            for g in range(4):
                for c0, n in SEGMENTS:
                    mm = eng.matmul(m.ps[0][:, c0:c0 + n], m.ones[:, :], yc[:, g, c0:c0 + n],
                                    start=(g == 0), stop=(g == 3))
            mm.then_inc(sums, 1)
            for g in range(4):
                eng.wait_ge(sq_done, g + 1)
                for c0, n in SEGMENTS:
                    mm = eng.matmul(m.ps[1][:, c0:c0 + n], m.ones[:, :], za[:, g, c0:c0 + n],
                                    start=(g == 0), stop=(g == 3))
            mm.then_inc(sums, 1)

        @block.scalar
        def _(eng):
            ch = Chain(eng, act)
            eng.wait_ge(zeroed, 1)
            for n in range(NPROJ):
                eng.wait_ge(used, n + 1)
                src = m.ps[n % 3]
                if n < 4:
                    ch(eng.activation(lat(za[:, n])[:, HALO * GRID_W:(HALO + ROWS) * GRID_W], src[:, 0:LAT], ACT.Copy))
                    ch(eng.activation(ctx(za[:, n])[:, HALO:HALO + CTX], src[:, LAT:T], ACT.Copy))
                else:
                    g = (n - 4) // 2
                    if g >= 2:
                        eng.wait_ge(gated, g - 1)
                    ch(eng.activation((ga, gv)[n % 2][:, g % 2], src[:, 0:T], (ACT.Sigmoid, ACT.Copy)[n % 2]))
                eng.sem_inc(out_act, 1)
            for g in range(4):
                if g == 2:
                    eng.wait_ge(pool_bias, 1)
                    for i in range(4):
                        eng.wait_ge(sums, i + 1)
                        eng.activation(yb[:, i, :], m.ps[3][:, 0:T], ACT.Identity, scale=m.par[:, 1, R_PS + i:R_PS + i + 1],
                                       bias=pbs[:, i:i + 1]).then_inc(mixed, 1)
                if g >= 2:
                    eng.wait_ge(conv_pe, g - 1)
                for t in range(TT):
                    eng.activation(dg[g % 2][:, t, :], m.ident[:, :], ACT.Copy, scale=tap(t, g)).then_inc(diags, 1)
            for g in range(4):
                eng.wait_ge(cen, g + 1)
                eng.activation(za[:, g, 0:T], yc[:, g, :], ACT.Square).then_inc(sq_done, 1)
            eng.wait_ge(sums, 6)
            eng.activation(root, m.ps[1][:, 0:T], ACT.Sqrt, scale=1.0 / 512, bias=m.eps[:, 2:3]).then_inc(rooted, 1)
            for g in range(4):
                eng.wait_ge(norm, g + 1)
                eng.activation(za[:, g, 0:T], yc[:, g, :], ACT.Sigmoid).then_inc(sgm, 1)

        @block.vector
        def _(eng):
            ch = Chain(eng, dve)
            ch(eng.tensor_tensor(pbs, m.par[:, 1, R_PB:R_PB + 4], m.par[:, 1, R_PS:R_PS + 4], ALU.mult))
            eng.sem_inc(pool_bias, 1)
            eng.wait_ge(zeroed, 1)
            nr = ROWS + 2 * HALO
            for g in range(4):
                eng.wait_ge(out_act, g + 1)
                srcs, c_src = za[:, g], cnt[:, 0]
                for j in range(g + 1):
                    sh = 1 << j
                    dst, c_dst = zb[:, j % 2], cnt[:, 1 + j % 2]
                    nl, nx = NL - (2 * sh - 1) * GRID_W, NC_ - (2 * sh - 1)
                    ch(eng.tensor_tensor(dst[:, 0:nl], srcs[:, 0:nl], srcs[:, sh * GRID_W:sh * GRID_W + nl], ALU.add))
                    ch(eng.tensor_tensor(ctx(dst)[:, 0:nx], ctx(srcs)[:, 0:nx], ctx(srcs)[:, sh:sh + nx], ALU.add))
                    for a0, w in ((0, nr - (2 * sh - 1)), (nr, nx)):
                        ch(eng.tensor_tensor(c_dst[:, a0:a0 + w], c_src[:, a0:a0 + w], c_src[:, a0 + sh:a0 + sh + w],
                                             ALU.add))
                    srcs, c_src = dst, c_dst
                half = 1 << g
                o, oc = HALO - half, zb[:, (g + 1) % 2]
                cr, cx = c_src[:, o:o + ROWS], c_src[:, nr + o:nr + o + CTX]
                ch(eng.reciprocal(cr, cr))
                ch(eng.reciprocal(cx, cx))
                sl = srcs[:, o * GRID_W:(o + ROWS) * GRID_W].rearrange("p (r w) -> p r w", w=GRID_W)
                ch(eng.tensor_tensor(oc[:, 0:LAT].rearrange("p (r w) -> p r w", w=GRID_W), sl,
                                     cr.unsqueeze(2).to_broadcast([P, ROWS, GRID_W]), ALU.mult))
                ch(eng.tensor_tensor(oc[:, LAT:T], ctx(srcs)[:, o:o + CTX], cx, ALU.mult))
                ch(eng.tensor_tensor(oc[:, 0:LAT], oc[:, 0:LAT], za[:, g, HALO * GRID_W:(HALO + ROWS) * GRID_W],
                                     ALU.subtract))
                ch(eng.tensor_tensor(oc[:, LAT:T], oc[:, LAT:T], ctx(za[:, g])[:, HALO:HALO + CTX], ALU.subtract))
                ch(eng.tensor_copy(za[:, g, 0:T], oc[:, 0:T]))
                eng.sem_inc(pooled, 1)
            for g in range(4):
                eng.wait_ge(gated, g + 1)
                dl, dc = grid(yc[:, g, 0:LAT]), yc[:, g, LAT:T]
                for t in range(TT, TAPS):
                    il, ic = lat_u(g)[:, :, t:t + GRID_W], ctx_u(g)[:, t:t + CTX]
                    if t == TT:
                        cb = m.par[:, 1, R_CB + g:R_CB + g + 1]
                        ch(eng.tensor_scalar(dl, il, tap(t, g), cb, ALU.mult, ALU.add))
                        ch(eng.tensor_scalar(dc, ic, tap(t, g), cb, ALU.mult, ALU.add))
                    else:
                        ch(eng.scalar_tensor_tensor(out=dl, in0=il, scalar=tap(t, g), in1=dl, op0=ALU.mult, op1=ALU.add))
                        ch(eng.scalar_tensor_tensor(out=dc, in0=ic, scalar=tap(t, g), in1=dc, op0=ALU.mult, op1=ALU.add))
                if g > 0:
                    add_sums(eng, ch, g - 1)
            add_sums(eng, ch, 3)
            eng.wait_ge(sums, 5)
            for g in range(4):
                ch(eng.scalar_tensor_tensor(out=yc[:, g, :], in0=m.ps[0][:, 0:T], scalar=-1.0 / 512, in1=yc[:, g, :],
                                            op0=ALU.mult, op1=ALU.add))
                eng.sem_inc(cen, 1)
            eng.wait_ge(rooted, 1)
            ch(eng.reciprocal(root, root))
            for g in range(4):
                ch(eng.tensor_tensor(yc[:, g, :], yc[:, g, :], root, ALU.mult))
                ch(eng.tensor_scalar(yc[:, g, :], yc[:, g, :], m.par[:, 1, R_LG + g:R_LG + g + 1],
                                     m.par[:, 1, R_LB + g:R_LB + g + 1], ALU.mult, ALU.add))
                eng.sem_inc(norm, 1)
            for g in range(4):
                eng.wait_ge(sgm, g + 1)
                ch(eng.tensor_tensor(yc[:, g, :], yc[:, g, :], za[:, g, 0:T], ALU.mult))

    st.close()


def stage_merge(m, l):
    nc, d = m.nc, m.dram
    st = Stage(nc, "mg")
    s = st.sem
    landed = [s(f"w{i}") for i in range(WRING)]
    done, gates, values, dve = s("done"), s("gates"), s("values"), s("dve")
    m.used = 0
    yb, yc, merged = m.take(4, T), m.take(4, T), m.take(KB, T)
    g, acc, part = m.take(6, T), m.take(T), m.take(T)
    outs = [d[n].rearrange("l (k p) (b c) -> l b p k c", p=P, c=P) for n in ("w_a_out", "w_b_out", "w_c_out")]
    SLOT = (0, 1, 2, 4, 3, 4)
    with nc.Block() as block:
        @block.sync
        def _(eng):
            with eng.Fori(0, KB) as db:
                for i in range(6):
                    eng.wait_ge(done, db * 6 + (i + 1))
                    if i % 2 == 0:
                        dst, src = m.w[:, SLOT[i]], m.w_in[l, db + (B_GATE + KB * (i // 2))]
                    elif i == 1:
                        dst, src = m.w[:, SLOT[i]], outs[0][l, db]
                    else:
                        dst, src = m.w[:, SLOT[i], 4 * (i // 4):4 * (i // 4) + 4], outs[i // 2][l, db]
                    eng.dma_start(dst, src).then_inc(landed[SLOT[i]], 16)

        @block.tensor
        def _(eng):
            eng.sem_inc(done, 6)
            with eng.Fori(0, KB // 2) as pair:
                for odd in range(2):
                    db = pair * 2 + odd
                    for i in range(6):
                        j = i // 2
                        ps = m.ps[(6 * odd + i) % 4]
                        if i == 3 or i == 5:
                            eng.wait_ge(landed[4], db * 32 + 32)
                        else:
                            eng.wait_ge(landed[SLOT[i]], db * 16 + 16)
                        if i % 2 == 0:
                            eng.wait_ge(gates, db * 3 + (j + 2))
                        else:
                            eng.wait_ge(values, db * 3 + (j + 5))
                        if i < 3 or i == 4:
                            mm = project(eng, m, ps, SLOT[i], m.ya if i == 1 else m.h)
                        else:
                            for k in range(4):
                                for c0, n in SEGMENTS:
                                    mm = eng.matmul(ps[:, c0:c0 + n], m.w[:, 4, 4 * (j - 1) + k, :],
                                                    (yb, yc)[j - 1][:, k, c0:c0 + n], start=(k == 0), stop=(k == 3))
                        mm.then_inc(done, 1)

        @block.scalar
        def _(eng):
            eng.sem_inc(gates, 3)
            with eng.Fori(0, KB // 2) as pair:
                for odd in range(2):
                    db = pair * 2 + odd
                    for j in range(3):
                        eng.wait_ge(done, db * 6 + (2 * j + 7))
                        eng.wait_ge(values, db * 3 + (j + 1))
                        eng.activation(g[:, 3 * odd + j, :], m.ps[(6 * odd + 2 * j) % 4][:, 0:T], ACT.Sigmoid)\
                           .then_inc(gates, 1)

        @block.vector
        def _(eng):
            eng.sem_inc(values, 6)
            with eng.Fori(0, KB // 2) as pair:
                for odd in range(2):
                    db = pair * 2 + odd
                    for j in range(3):
                        eng.wait_ge(gates, db * 3 + (j + 4))
                        eng.wait_ge(done, db * 6 + (2 * j + 8))
                        eng.tensor_tensor(part if j else acc, g[:, 3 * odd + j, :],
                                          m.ps[(6 * odd + 2 * j + 1) % 4][:, 0:T], ALU.mult).then_inc(values, 1)
                        eng.wait_ge(values, db * 3 + (j + 7))
                        if j > 0:
                            eng.tensor_tensor(acc if j == 1 else merged[:, db, :], acc, part, ALU.add).then_inc(dve, 1)
                            eng.wait_ge(dve, db * 2 + j)
    st.close()


def stage_out(m, l):
    nc, d = m.nc, m.dram
    st = Stage(nc, "out")
    s = st.sem
    landed = [s(f"w{i}") for i in range(4)]
    done, dve, taken, gate_in = s("done"), s("dve"), s("taken"), s("gate_in")
    m.used = 0
    m.take(4, T), m.take(4, T)
    merged = m.take(KB, T)
    gt = m.take(4, 2)
    res = m.take(T)
    w = d["w_out"].rearrange("l (k p) (b c) -> l b p k c", p=P, c=P)
    with nc.Block() as block:
        @block.sync
        def _(eng):
            with eng.Fori(0, 2) as half:
                for i in range(4):
                    eng.wait_ge(done, half * 4 + (i + 1))
                    eng.dma_start(m.w[:, i], w[l, half * 4 + i]).then_inc(landed[i], 16)

        @block.tensor
        def _(eng):
            eng.sem_inc(done, 4)
            with eng.Fori(0, 2) as half:
                for i in range(4):
                    eng.wait_ge(landed[i], half * 16 + 16)
                    eng.wait_ge(taken, half * 4 + (i + 1))
                    project(eng, m, m.ps[i], i, merged).then_inc(done, 1)

        @block.vector
        def _(eng):
            eng.sem_inc(taken, 4)
            with eng.Fori(0, 2) as half:
                eng.tensor_copy(gt, m.mod[:, GT1, bass.ds(half * 4, 4), :]).then_inc(gate_in, 1)
                eng.wait_ge(gate_in, half + 1)
                for i in range(4):
                    eng.wait_ge(done, half * 4 + (i + 5))
                    for j, (c0, n) in enumerate(SEGMENTS):
                        ins = eng.tensor_scalar(res[:, c0:c0 + n], m.ps[i][:, c0:c0 + n], gt[:, i, j:j + 1], None, ALU.mult)
                        if j == 0:
                            ins.then_inc(dve, 1)
                    ins.then_inc(taken, 1)
                    eng.wait_ge(dve, half * 8 + (2 * i + 1))
                    eng.wait_ge(taken, half * 4 + (i + 5))
                    eng.tensor_tensor(m.x[:, half * 4 + i, :], m.x[:, half * 4 + i, :], res, ALU.add).then_inc(dve, 1)
                    eng.wait_ge(dve, half * 8 + (2 * i + 2))
    st.close()

def stage_store(m):
    nc, d = m.nc, m.dram
    st = Stage(nc, "tok")
    turned, copied, stored = st.sem("turned"), st.sem("copied"), st.sem("stored")
    rows = m.ya[:, :, :].rearrange("p a b -> p (a b)").rearrange("p (t c) -> p t c", c=D)
    NT = TILES * KB // 4
    with nc.Block() as block:
        @block.tensor
        def _(eng):
            for n in range(NT):
                t, k0 = n // 2, 4 * (n % 2)
                if n >= 8:
                    eng.wait_ge(copied, n - 7)
                for j in range(4):
                    mm = eng.transpose(m.bank(n % 8)[:, P * j:P * j + P], m.h[:, k0 + j, P * t:P * t + P], m.ident[:, :])
                mm.then_inc(turned, 1)

        @block.vector
        def _(eng):
            for n in range(NT):
                t, k0 = n // 2, 4 * (n % 2)
                eng.wait_ge(turned, n + 1)
                eng.tensor_copy(rows[:, t, P * k0:P * k0 + 4 * P], m.bank(n % 8)).then_inc(copied, 1)

        @block.sync
        def _(eng):
            eng.wait_ge(copied, 8)
            eng.dma_start(d["y_sample"][0].rearrange("(t p) c -> p t c", p=P), rows[:, 0:4, :]).then_inc(stored, 16)
            eng.wait_ge(copied, NT)
            eng.dma_start(d["y_prompt"][0], rows[:, 4, :]).then_inc(stored, 16)
            eng.wait_ge(stored, 32)
    st.close()


def top16(ch, vals, idx, src, spare):
    eng = ch.eng
    ch(eng.max(vals[:, 0:8], src))
    ch(eng.max_index(idx[:, 0:8], vals[:, 0:8], src))
    ch(eng.match_replace(spare, vals[:, 0:8], src, -3.4028235e38))
    ch(eng.max(vals[:, 8:16], spare))
    ch(eng.max_index(idx[:, 8:16], vals[:, 8:16], spare))


def peer_tables(m):
    m.used = 0
    return m.take(TILES + 1, 2 * HEADS_Q, TOPK), m.take(TILES + 1, 2 * HEADS_Q, TOPK)


GROUP = 32
PAIR = GROUP // TOPK
GROUPS_T = SLOTS // GROUP


class Selection:
    pass


def select_tables(m):
    w = Selection()
    w.top_v, w.top_i = peer_tables(m)
    w.idx, w.gate = m.take((TILES + 1) * SLOTS), m.take((TILES + 1) * SLOTS)
    w.iota, w.tv, w.ti = m.take(TOPK), m.take(2 * PAIR, TOPK), m.take(2 * PAIR, TOPK)
    w.cand, w.hot, w.spare = m.take(PAIR, TOPK * TOPK), m.take(PAIR, TOPK, TOPK), m.take(TOPK * TOPK)
    w.best, w.place, w.part = m.take(PAIR, TOPK), m.take(PAIR, TOPK).bitcast(U32), m.take(PAIR, TOPK).bitcast(U32)
    w.e, w.ex, w.rows, w.tot = m.take(PAIR, PAIR * TOPK), m.take(PAIR, TOPK), m.take(GROUP), m.take(PAIR)
    return w


def select_part(ch, w, g, part, shifted, exped, softmaxed):
    eng = ch.eng
    full = [P, PAIR, TOPK, TOPK]
    flat = "p h k -> p (h k)"
    if part == 0:
        for local, table in ((w.tv, w.top_v), (w.ti, w.top_i)):
            ch(eng.tensor_copy(local.rearrange(flat),
                               table.rearrange("p t b k -> p (t b k)")[:, bass.ds(g * (2 * GROUP), 2 * GROUP)]))
        tv = w.tv.rearrange("p (h e) k -> p h e k", e=2)
        ch(eng.tensor_tensor(w.cand.rearrange("p h (i j) -> p h i j", j=TOPK), tv[:, :, 0].unsqueeze(3).to_broadcast(full),
                             tv[:, :, 1].unsqueeze(2).to_broadcast(full), ALU.add))
        top16(ch, w.best[:, 0], w.place[:, 0], w.cand[:, 0], w.spare)
    elif part == 1:
        top16(ch, w.best[:, 1], w.place[:, 1], w.cand[:, 1], w.spare)
        ch(eng.tensor_tensor(w.ex, w.best, w.best[:, :, 0:1].to_broadcast([P, PAIR, TOPK]), ALU.subtract))
        eng.sem_inc(shifted, 1)
    else:
        half = part - 2
        op, by = ((ALU.logical_shift_right, 4), (ALU.bitwise_and, 15))[half]
        e = w.e[:, half].rearrange("p (h k) -> p h k", k=TOPK)
        ch(eng.tensor_scalar(w.part, w.place, by, None, op))
        ch(eng.tensor_copy(e, w.part))
        ch(eng.tensor_tensor(w.hot, e.unsqueeze(3).to_broadcast(full),
                             w.iota.unsqueeze(1).unsqueeze(1).to_broadcast(full), ALU.is_equal))
        keys = w.ti.rearrange("p (h e) k -> p h e k", e=2)[:, :, half].unsqueeze(2).to_broadcast(full)
        ch(eng.tensor_tensor(w.hot, w.hot, keys, ALU.mult))
        ch(eng.tensor_reduce(e, w.hot, AX.X, ALU.add))
    if part == 3:
        ch(eng.tensor_scalar(w.rows, w.e[:, 0], float(KEYS), w.row0, ALU.mult, ALU.add))
        ch(eng.tensor_tensor(w.rows, w.rows, w.e[:, 1], ALU.add))
        ch(eng.tensor_copy(w.idx.bitcast(U32)[:, bass.ds(g * GROUP, GROUP)], w.rows))
        eng.wait_ge(exped, softmaxed)
        ch(eng.tensor_reduce(w.tot, w.ex, AX.X, ALU.add))
        ch(eng.reciprocal(w.tot, w.tot))
        ch(eng.tensor_tensor(w.ex, w.ex, w.tot.unsqueeze(2).to_broadcast([P, PAIR, TOPK]), ALU.mult))
        ch(eng.tensor_copy(w.gate[:, bass.ds(g * GROUP, GROUP)], w.ex.rearrange(flat)))


def stage_scores(m, l):
    nc, d = m.nc, m.dram
    st = Stage(nc, "sc")
    s = st.sem
    landed = [s(f"w{i}") for i in range(4)]
    keys_in, q_done, k_done, q_out, s_done, s_out, dve, top_done = (
        s(n) for n in ("keys", "q_done", "k_turned", "q_out", "scored", "s_out", "dve", "tops"))
    round_, begun, shifted, exped, drawn = (s(n) for n in ("round", "begun", "shifted", "exponentials", "iota"))
    w = select_tables(m)
    w.row0 = m.row0[:, 0:1]
    keys, qt, kt, sc = m.take(4, P), m.take(2, T), m.take(2, P), m.take(2, TILES, P)
    vals, places = m.take(TILES, 4, TOPK), m.take(TILES, 4, TOPK).bitcast(U32)
    spare = m.take(P)
    wq = d["peer_wq"].rearrange("l (k p) (b c) -> l b p k c", p=P, c=P)
    pk = d["peer_keys"].rearrange("l h e n q -> l (h e) n q")
    ints = w.spare[:, 0:TOPK].bitcast(mybir.dt.int32)
    turned, copied = s("turned"), s("copied")
    rows = m.ya[:, :, :].rearrange("p a b -> p (a b)").rearrange("p (t c) -> p t c", c=D)

    def take(eng, quarter, i):
        eng.wait_ge(s_done, quarter * 4 + (i + 3))
        eng.wait_ge(top_done, quarter * 4 + (i + 1))
        eng.activation(sc[:, i % 2].rearrange("p t n -> p (t n)"), m.ps[2 + i % 2][:, 0:T], ACT.Copy).then_inc(s_out, 1)

    def score(eng, quarter, i):
        eng.wait_ge(q_out, quarter * 8 + (2 * i + 6))
        eng.wait_ge(s_out, quarter * 4 + (i + 1))
        for t in range(TILES):
            mm = eng.matmul(m.ps[2 + i % 2][:, P * t:P * t + P], qt[:, i % 2, P * t:P * t + P], kt[:, i % 2, :],
                            start=True, stop=True)
        mm.then_inc(s_done, 1)

    with nc.Block() as block:
        @block.sync
        def _(eng):
            with eng.Fori(0, 4) as quarter:
                eng.wait_ge(k_done, quarter * 4 + 4)
                eng.dma_start(keys, pk[l, bass.ds(quarter * 4, 4)].rearrange("b n q -> n b q")).then_inc(keys_in, 16)
                for i in range(4):
                    eng.wait_ge(q_done, quarter * 4 + (i + 1))
                    eng.dma_start(m.w[:, i], wq[l, quarter * 4 + i]).then_inc(landed[i], 16)

        @block.gpsimd
        def _(eng):
            eng.iota(ints, pattern=[[1, TOPK]], base=0, channel_multiplier=0).then_inc(drawn, 1)

        @block.tensor
        def _(eng):
            eng.sem_inc(q_done, 4)
            eng.sem_inc(k_done, 4)
            eng.sem_inc(s_done, 2)
            with eng.Fori(0, 4) as quarter:
                eng.wait_ge(keys_in, quarter * 16 + 16)
                for i in range(4):
                    eng.wait_ge(landed[i], quarter * 16 + 16)
                    eng.wait_ge(q_out, quarter * 8 + (2 * i + 2))
                    project(eng, m, m.ps[i % 2], i, m.h).then_inc(q_done, 1)
                    eng.transpose(m.ps[i % 2][:, 768:768 + P], keys[:, i, :], m.ident[:, :]).then_inc(k_done, 1)
                    if i >= 1:
                        score(eng, quarter, i - 1)
                score(eng, quarter, 3)
            eng.wait_ge(q_out, 36)
            for n in range(2 * TILES):
                t, k0 = n // 2, 4 * (n % 2)
                if n >= 4:
                    eng.wait_ge(copied, n - 3)
                for j in range(4):
                    mm = eng.transpose(m.bank(n % 4)[:, P * j:P * j + P], m.h[:, k0 + j, P * t:P * t + P], m.ident[:, :])
                mm.then_inc(turned, 1)

        @block.scalar
        def _(eng):
            eng.sem_inc(q_out, 4)
            eng.sem_inc(s_out, 2)
            with eng.Fori(0, 4) as quarter:
                for i in range(4):
                    eng.wait_ge(k_done, quarter * 4 + (i + 5))
                    eng.wait_ge(s_done, quarter * 4 + (i + 1))
                    eng.activation(qt[:, i % 2, :], m.ps[i % 2][:, 0:T], ACT.Copy).then_inc(q_out, 1)
                    eng.activation(kt[:, i % 2, :], m.ps[i % 2][:, 768:768 + P], ACT.Copy).then_inc(q_out, 1)
                    if i >= 1:
                        take(eng, quarter, i - 1)
                take(eng, quarter, 3)
                eng.wait_ge(shifted, quarter + 1)
                eng.activation(w.ex, w.ex, ACT.Exp).then_inc(exped, 1)
            for n in range(2 * TILES):
                t, k0 = n // 2, 4 * (n % 2)
                eng.wait_ge(turned, n + 1)
                eng.activation(rows[:, t, P * k0:P * k0 + 4 * P], m.bank(n % 4), ACT.Copy).then_inc(copied, 1)

        @block.vector
        def _(eng):
            ch = Chain(eng, dve)
            eng.sem_inc(top_done, 2)
            for table in (w.top_v, w.top_i):
                ch(eng.memset(table[:, TILES], 0.0))
            eng.wait_ge(drawn, 1)
            ch(eng.tensor_copy(w.iota, ints))
            with eng.Fori(0, 4) as quarter:
                eng.sem_clear(round_)
                ch = Chain(eng, round_)
                for i in range(4):
                    eng.wait_ge(s_out, quarter * 4 + (i + 3))
                    eng.sem_inc(begun, 1)
                    for t in range(TILES):
                        top16(ch, vals[:, t, i], places[:, t, i], sc[:, i % 2, t], spare)
                    eng.sem_inc(top_done, 1)
                ch(eng.tensor_copy(w.top_v[:, 0:TILES, bass.ds(quarter * 4, 4), :], vals))
                ch(eng.tensor_copy(w.top_i[:, 0:TILES, bass.ds(quarter * 4, 4), :], places))
                for part in range(4):
                    select_part(ch, w, quarter, part, shifted, exped, quarter + 1)
    st.close()


def stage_retrieve(m, l):
    nc, d = m.nc, m.dram
    st = Stage(nc, "ret")
    s = st.sem
    SUB = 4
    QS = GROUP // SUB
    LEAD = 4
    HALF = GROUP // 2
    u_in, v_in = m.u_in, m.v_in
    before = l * (16 * TILES * SLOTS // RING)
    u_free, v_free, hid_done, gel_done, w_done, dg_done, staged, g_in = (
        s(n) for n in ("u_free", "v_free", "hid_done", "gelu_done", "weights_done", "diag_done", "staged", "gates_in"))
    dve, pair, shifted, exped, selected = (s(n) for n in ("dve", "pair", "shifted", "exponentials", "selected"))
    summed, sum_out, turned, asked, h_in, x_out, zeroed, begun = (
        s(n) for n in ("summed", "sum_out", "turned", "asked", "h_in", "x_out", "zeroed", "begun"))
    w = select_tables(m)
    w.row0 = m.row0[:, 0:1]
    hs, sm = m.take(D), m.take(D)
    ub, vb, dg = m.take(RING, D), m.take(RING, D), m.take(RING, P)
    stage, hid, gel, wgt, g16 = (m.take(GROUP) for _ in range(5))
    gt, zero = m.take(KB), m.take(512)
    ut = d["peer_u"].rearrange("l e c -> (l e) c")
    vt = d["peer_v"].rearrange("l e c -> (l e) c")
    rows = m.ya[:, :, :].rearrange("p a b -> p (a b)").rearrange("p (t c) -> p t c", c=D)

    def stage_rows(eng, g, half):
        a = HALF * half
        eng.wait_ge(selected, g + 1)
        eng.tensor_copy(stage.bitcast(U32)[:, a:a + HALF],
                        w.idx.bitcast(U32)[:, bass.ds(g * GROUP + a, HALF)]).then_inc(staged, 1)
        eng.wait_ge(staged, g * 2 + (half + 1))

    def gather(eng, g, i, free, table, buf, landed):
        off = bass.IndirectOffsetOnAxis(ap=stage.bitcast(U32)[:, i % GROUP:i % GROUP + 1], axis=0)
        eng.wait_ge(free, g * GROUP + (i + 1))
        eng.sem_inc(asked, 1)
        eng.indirect_dma_start(buf[:, i % RING, :], None, table, off).then_inc(landed[i % RING], 16)

    def gather_u(eng, g, i):
        gather(eng, g, i, u_free, ut, ub, u_in)

    def gather_v(eng, g, i):
        gather(eng, g, i, v_free, vt, vb, v_in)

    def weights(eng, g, q):
        a = slice(SUB * q, SUB * q + SUB)
        eng.wait_ge(gel_done, g * QS + (q + 1))
        eng.tensor_tensor(wgt[:, a], gel[:, a], g16[:, a], ALU.mult).then_inc(w_done, 1)

    def diag(eng, g, q):
        eng.wait_ge(w_done, g * QS + (q + 1))
        for i in range(SUB * q, SUB * q + SUB):
            eng.wait_ge(v_free, g * GROUP + (i + 1))
            eng.activation(dg[:, i % RING, :], m.ident[:, :], ACT.Copy, scale=wgt[:, i:i + 1]).then_inc(dg_done, 1)

    with nc.Block() as block:
        @block.gpsimd
        def _(eng):
            stage_rows(eng, 0, 0)
            for i in range(LEAD):
                gather_u(eng, 0, i)
            with eng.Fori(0, TILES * GROUPS_T - 1) as g:
                for i in range(GROUP):
                    if i == HALF - LEAD:
                        stage_rows(eng, g, 1)
                    if i == GROUP - LEAD:
                        stage_rows(eng, g + 1, 0)
                    gather_u(eng, g, i + LEAD)
                    gather_v(eng, g, i)
            g = TILES * GROUPS_T - 1
            for i in range(GROUP):
                if i == HALF - LEAD:
                    stage_rows(eng, g, 1)
                if i < GROUP - LEAD:
                    gather_u(eng, g, i + LEAD)
                gather_v(eng, g, i)

        @block.vector
        def _(eng):
            eng.sem_inc(selected, GROUPS_T)
            eng.sem_inc(u_free, RING)
            eng.sem_inc(x_out, 1)
            eng.memset(zero, 0.0).then_inc(zeroed, 1)
            with eng.Fori(0, TILES) as t:
                eng.tensor_copy(hs, rows[:, t, :]).then_inc(h_in, 1)
                eng.tensor_copy(gt, m.gate2[:, t, :]).then_inc(h_in, 1)
                eng.wait_ge(h_in, t * 2 + 2)
                eng.sem_inc(begun, 1)
                with eng.Fori(0, GROUPS_T) as tg:
                    g = t * GROUPS_T + tg
                    eng.tensor_copy(g16, w.gate[:, bass.ds(g * GROUP, GROUP)]).then_inc(g_in, 1)
                    eng.wait_ge(g_in, g + 1)
                    eng.sem_inc(begun, 1)
                    eng.sem_clear(pair)
                    ch = Chain(eng, pair)
                    for i in range(GROUP):
                        r = i % RING
                        eng.wait_ge(u_in[r], before + g * (16 * (GROUP // RING)) + 16 * (i // RING + 1))
                        eng.tensor_tensor_reduce(ub[:, r, :], ub[:, r, :], hs, 1.0, 0.0, ALU.mult, ALU.add,
                                                 hid[:, i:i + 1]).then_inc(u_free, 1)
                        if i % SUB == SUB - 1:
                            q = i // SUB
                            eng.wait_ge(u_free, g * GROUP + (RING + i + 1))
                            eng.sem_inc(hid_done, 1)
                            if q > 0:
                                weights(eng, g, q - 1)
                            if q % 2 == 0:
                                select_part(ch, w, g + GROUPS_T, q // 2, shifted, exped, g + 1)
                    weights(eng, g, QS - 1)
                    eng.wait_ge(w_done, g * QS + QS)
                    eng.sem_inc(selected, 1)
                eng.wait_ge(turned, t + 1)
                turned_sums = m.ps[1][:, :].rearrange("p (k c) -> p k c", c=P)
                sums = sm.rearrange("p (k c) -> p k c", c=P)
                eng.tensor_tensor(sums, turned_sums, gt.unsqueeze(2).to_broadcast([P, KB, P]), ALU.mult).then_inc(dve, 1)
                eng.wait_ge(dve, t * 2 + 1)
                xs = m.x[:, :, bass.ds(t * P, P)]
                eng.tensor_tensor(xs, xs, sums, ALU.add).then_inc(dve, 1)
                eng.wait_ge(dve, t * 2 + 2)
                eng.sem_inc(x_out, 1)

        @block.scalar
        def _(eng):
            with eng.Fori(0, TILES) as t:
                with eng.Fori(0, GROUPS_T) as tg:
                    g = t * GROUPS_T + tg
                    for q in range(QS):
                        a = slice(SUB * q, SUB * q + SUB)
                        eng.wait_ge(hid_done, g * QS + (q + 1))
                        eng.activation(gel[:, a], hid[:, a], ACT.Gelu).then_inc(gel_done, 1)
                        if q > 0:
                            diag(eng, g, q - 1)
                        if q == 4:
                            eng.wait_ge(shifted, g + 1)
                            eng.activation(w.ex, w.ex, ACT.Exp).then_inc(exped, 1)
                    diag(eng, g, QS - 1)
                eng.wait_ge(summed, t + 1)
                eng.wait_ge(x_out, t + 1)
                for i in range(2):
                    eng.activation(sm[:, 512 * i:512 * i + 512], m.bank(i), ACT.Copy).then_inc(sum_out, 1)

        @block.tensor
        def _(eng):
            eng.wait_ge(zeroed, 1)
            eng.sem_inc(v_free, RING)
            with eng.Fori(0, TILES) as t:
                for i in range(2):
                    eng.matmul(m.bank(i), zero[:, 0:P], zero, start=True, stop=False)
                with eng.Fori(0, GROUPS_T) as tg:
                    g = t * GROUPS_T + tg
                    for i in range(GROUP):
                        r = i % RING
                        eng.wait_ge(v_in[r], before + g * (16 * (GROUP // RING)) + 16 * (i // RING + 1))
                        eng.wait_ge(dg_done, g * GROUP + (i + 1))
                        for j in range(2):
                            mm = eng.matmul(m.bank(j), dg[:, r, :], vb[:, r, 512 * j:512 * j + 512], start=False, stop=False)
                        mm.then_inc(v_free, 1)
                for i in range(2):
                    mm = eng.matmul(m.bank(i), zero[:, 0:P], zero, start=False, stop=True)
                mm.then_inc(summed, 1)
                eng.wait_ge(sum_out, t * 2 + 2)
                for k in range(KB):
                    mm = eng.transpose(m.ps[1][:, P * k:P * k + P], sm[:, P * k:P * k + P], m.ident[:, :])
                mm.then_inc(turned, 1)
    st.close()

def program(nc, dram):
    with ExitStack() as ctx:
        m = Model(nc, ctx, dram)
        stage_constants(m)
        stage_load_x(m)
        with nc.Fori(0, LAYERS) as l:
            stage_params(m, l)
            stage_modulation(m, l)
            stage_norm(m, 0)
            stage_lowrank(m, l)
            with nc.Fori(0, KB) as hp:
                stage_rwkv(m, l, hp)
            stage_branches(m, l)
            stage_merge(m, l)
            stage_out(m, l)
            stage_norm(m, 1)
            stage_scores(m, l)
            stage_retrieve(m, l)
        stage_norm(m, 2)
        stage_store(m)


_OUTS = [("y_prompt", (1, CTX, D)), ("y_sample", (1, LAT, D)), ("new_state", (1, LAYERS, 2, 16, HD, HD))]


def kernel(**inputs):
    import numpy as np
    import concourse.bacc as bacc
    from concourse.bass_utils import run_bass_kernel_spmd

    nc = bacc.Bacc("TRN2", target_bir_lowering=False, num_devices=1)
    arrays, dram = {}, {}
    for name, value in inputs.items():
        a = np.ascontiguousarray(value)
        arrays[name] = a
        dram[name] = nc.dram_tensor(name, a.shape, mybir.dt.from_np(a.dtype), kind="ExternalInput").ap()
    for name, shape in _OUTS:
        dram[name] = nc.dram_tensor(name, shape, F32, kind="ExternalOutput").ap()
    program(nc, dram)
    r = run_bass_kernel_spmd(nc, [arrays], core_ids=[0])
    return tuple(r.results[0][name] for name, _ in _OUTS)
```
